# Optimizing a Trainium2 kernel written in Bass

```python
import math
import jax, jax.numpy as jnp
from jax import lax
import numpy as np

D_MODEL = 1024
BATCH = 1
SEQ = 512
DEPTH = 1

MEM_LEN = 256
EPS = 1e-6

SSD_HEADS = 16
SSD_HEAD_DIM = 64
SSD_WIDTH = SSD_HEADS * SSD_HEAD_DIM
SSD_GROUPS = 4
SSD_STATE = 128
CONV_WIDTH = 4
SSD_CHUNK = 128
CONV_CH = SSD_WIDTH + 2 * SSD_GROUPS * SSD_STATE

DA_HEADS = 8
DA_HEAD_DIM = 64
DA_V_DIM = 2 * DA_HEAD_DIM
DA_WIDTH = DA_HEADS * DA_V_DIM
Q_BLOCK = 128

NUM_BUCKETS = 32
MAX_DISTANCE = 128

IN_SIZES = (SSD_WIDTH, CONV_CH, SSD_HEADS, DA_WIDTH, DA_WIDTH, DA_WIDTH)
IN_WIDTH = SSD_WIDTH + CONV_CH + SSD_HEADS + 3 * DA_WIDTH
MIX_WIDTH = SSD_WIDTH + DA_WIDTH

CROSS_HEADS = 4
CROSS_HEAD_DIM = D_MODEL // CROSS_HEADS

D_FF = 2816


def rms_norm(x, w):
    x32 = x.astype(jnp.float32)
    y = x32 * lax.rsqrt(jnp.mean(x32 * x32, axis=-1, keepdims=True) + EPS)
    return y.astype(x.dtype) * w

def swiglu(h, w_in, w_out):
    gate, up = jnp.split(h @ w_in, 2, axis=-1)
    return (jax.nn.silu(gate) * up) @ w_out

def split_sizes(u, sizes):
    idx, acc = [], 0
    for s in sizes[:-1]:
        acc += s
        idx.append(acc)
    return jnp.split(u, idx, axis=-1)

def causal_dwconv(u, w, b):
    y = lax.conv_general_dilated(u, w[:, None, :], window_strides=(1,),
                                 padding=[(CONV_WIDTH - 1, 0)],
                                 dimension_numbers=('NWC', 'WIO', 'NWC'),
                                 feature_group_count=u.shape[-1])
    return y + b

def ssd_scan(xh, dt, a, b_in, c_in):
    bsz, seqlen, nh, hp = xh.shape
    ng, ns = b_in.shape[2], b_in.shape[3]
    r = nh // ng
    nc = seqlen // SSD_CHUNK
    xdt = (xh * dt[..., None]).reshape(bsz, nc, SSD_CHUNK, ng, r, hp)
    la = (dt * a).reshape(bsz, nc, SSD_CHUNK, ng, r)
    bc = b_in.reshape(bsz, nc, SSD_CHUNK, ng, ns)
    cc = c_in.reshape(bsz, nc, SSD_CHUNK, ng, ns)
    la_cum = jnp.cumsum(la, axis=2)
    causal = jnp.tril(jnp.ones((SSD_CHUNK, SSD_CHUNK), dtype=bool))
    seg = la_cum[:, :, :, None] - la_cum[:, :, None, :]
    decay = jnp.exp(jnp.where(causal[None, None, :, :, None, None], seg, -jnp.inf))
    cb = jnp.einsum('bclgn,bcsgn->bclsg', cc, bc)
    y_diag = jnp.einsum('bclsg,bclsgr,bcsgrp->bclgrp', cb, decay, xdt)
    decay_to_end = jnp.exp(la_cum[:, :, -1:] - la_cum)
    chunk_states = jnp.einsum('bclgn,bclgr,bclgrp->bcgrpn', bc, decay_to_end, xdt)
    chunk_decay = jnp.exp(la_cum[:, :, -1])

    def step(state, inp):
        st, dec = inp
        return state * dec[..., None, None] + st, state

    init = jnp.zeros_like(chunk_states[:, 0])
    _, prev = lax.scan(step, init, (jnp.moveaxis(chunk_states, 1, 0),
                                    jnp.moveaxis(chunk_decay, 1, 0)))
    prev = jnp.moveaxis(prev, 0, 1)
    y_off = jnp.einsum('bclgn,bcgrpn,bclgr->bclgrp', cc, prev, jnp.exp(la_cum))
    return (y_diag + y_off).reshape(bsz, seqlen, nh, hp)

def rel_bucket(rel):
    n = jnp.maximum(-rel, 0)
    max_exact = NUM_BUCKETS // 2
    nf = jnp.maximum(n, 1).astype(jnp.float32)
    large = max_exact + (jnp.log(nf / max_exact) / math.log(MAX_DISTANCE / max_exact)
                         * (NUM_BUCKETS - max_exact)).astype(jnp.int32)
    large = jnp.minimum(large, NUM_BUCKETS - 1)
    return jnp.where(n < max_exact, n, large)

def diff_attention(q, k, v, lam, rel_bias):
    bsz, seqlen, nh, _, dh = q.shape
    nb = seqlen // Q_BLOCK
    scale = dh ** -0.5
    qb = jnp.moveaxis(q.reshape(bsz, nb, Q_BLOCK, nh, 2, dh), 1, 0)
    k_pos = jnp.arange(seqlen)

    def block(args):
        q_blk, i = args
        q_pos = i * Q_BLOCK + jnp.arange(Q_BLOCK)
        rel = k_pos[None, :] - q_pos[:, None]
        bias = jnp.transpose(rel_bias[rel_bucket(rel)], (2, 0, 1)).astype(jnp.float32)
        logits = jnp.einsum('bqhcd,bkhcd->bhcqk', q_blk, k,
                            preferred_element_type=jnp.float32) * scale
        logits = logits + bias[None, :, None]
        logits = jnp.where(rel[None, None, None] <= 0, logits, -jnp.inf)
        p = jax.nn.softmax(logits, axis=-1)
        w = p[:, :, 0] - lam * p[:, :, 1]
        return jnp.einsum('bhqk,bkhe->bqhe', w.astype(v.dtype), v,
                          preferred_element_type=jnp.float32)

    out = lax.map(block, (qb, jnp.arange(nb)))
    return jnp.moveaxis(out, 0, 1).reshape(bsz, seqlen, nh, 2 * dh)

def hybrid_mixer(h, w_in, conv_w, conv_b, dt_bias, a_log, d_skip, ssd_norm_w,
                 lq1, lk1, lq2, lk2, subln_w, rel_bias, w_out, lambda_init):
    bsz, seqlen, _ = h.shape
    z, xbc, dt_raw, q, k, v = split_sizes(h @ w_in, IN_SIZES)

    xbc = jax.nn.silu(causal_dwconv(xbc, conv_w, conv_b))
    xs, bs, cs = jnp.split(xbc, [SSD_WIDTH, SSD_WIDTH + SSD_GROUPS * SSD_STATE], axis=-1)
    dt = jax.nn.softplus(dt_raw.astype(jnp.float32) + dt_bias.astype(jnp.float32))
    a = -jnp.exp(a_log.astype(jnp.float32))
    xh = xs.reshape(bsz, seqlen, SSD_HEADS, SSD_HEAD_DIM).astype(jnp.float32)
    y = ssd_scan(xh, dt, a,
                 bs.reshape(bsz, seqlen, SSD_GROUPS, SSD_STATE).astype(jnp.float32),
                 cs.reshape(bsz, seqlen, SSD_GROUPS, SSD_STATE).astype(jnp.float32))
    y = y + d_skip.astype(jnp.float32)[:, None] * xh
    y = y.reshape(bsz, seqlen, SSD_WIDTH) * jax.nn.silu(z.astype(jnp.float32))
    yg = y.reshape(bsz, seqlen, SSD_GROUPS, SSD_WIDTH // SSD_GROUPS)
    yg = yg * lax.rsqrt(jnp.mean(yg * yg, axis=-1, keepdims=True) + EPS)
    y_ssd = yg.reshape(bsz, seqlen, SSD_WIDTH).astype(h.dtype) * ssd_norm_w

    q = q.reshape(bsz, seqlen, DA_HEADS, 2, DA_HEAD_DIM)
    k = k.reshape(bsz, seqlen, DA_HEADS, 2, DA_HEAD_DIM)
    v = v.reshape(bsz, seqlen, DA_HEADS, DA_V_DIM)
    lam = (jnp.exp(jnp.sum(lq1.astype(jnp.float32) * lk1.astype(jnp.float32)))
           - jnp.exp(jnp.sum(lq2.astype(jnp.float32) * lk2.astype(jnp.float32)))
           + lambda_init)
    o = diff_attention(q, k, v, lam, rel_bias)
    o = o * lax.rsqrt(jnp.mean(o * o, axis=-1, keepdims=True) + EPS)
    y_attn = (o.astype(h.dtype) * subln_w * (1.0 - lambda_init)).reshape(bsz, seqlen, DA_WIDTH)

    return jnp.concatenate([y_ssd, y_attn], axis=-1) @ w_out

def memory_cross_attention(h, mem_n, w_cq, w_ck, w_cv, w_co):
    bsz, seqlen, _ = h.shape
    mlen = mem_n.shape[1]
    q = (h @ w_cq).reshape(bsz, seqlen, CROSS_HEADS, CROSS_HEAD_DIM)
    k = (mem_n @ w_ck).reshape(bsz, mlen, CROSS_HEADS, CROSS_HEAD_DIM)
    v = (mem_n @ w_cv).reshape(bsz, mlen, CROSS_HEADS, CROSS_HEAD_DIM)
    logits = jnp.einsum('bqhd,bkhd->bhqk', q, k,
                        preferred_element_type=jnp.float32) * (CROSS_HEAD_DIM ** -0.5)
    p = jax.nn.softmax(logits, axis=-1)
    o = jnp.einsum('bhqk,bkhd->bqhd', p.astype(v.dtype), v).reshape(bsz, seqlen, D_MODEL)
    return o @ w_co

def first_inputs(seed: int = 0) -> dict:
    key = jax.random.key(seed)
    ks = jax.random.split(key, 32)
    f32 = jnp.float32

    def nrm(k, shape, scale):
        return jax.random.normal(k, shape, f32) * scale

    def gain(k, shape):
        return 1.0 + 0.02 * jax.random.normal(k, shape, f32)

    L = DEPTH
    dt0 = jnp.exp(jax.random.uniform(ks[10], (L, SSD_HEADS), f32,
                                     math.log(1e-3), math.log(1e-1)))
    dt_bias = dt0 + jnp.log(-jnp.expm1(-dt0))
    a_log = jnp.log(jax.random.uniform(ks[11], (L, SSD_HEADS), f32, 1.0, 16.0))
    return {
        'x': jax.random.normal(ks[0], (BATCH, SEQ, D_MODEL), f32),
        'mem': jax.random.normal(ks[1], (BATCH, MEM_LEN, D_MODEL), f32),
        'norm_ffn1_w': gain(ks[2], (L, D_MODEL)),
        'ffn1_w_in': nrm(ks[3], (L, D_MODEL, 2 * D_FF), D_MODEL ** -0.5),
        'ffn1_w_out': nrm(ks[4], (L, D_FF, D_MODEL), D_FF ** -0.5),
        'norm_mix_w': gain(ks[5], (L, D_MODEL)),
        'w_in_mix': nrm(ks[6], (L, D_MODEL, IN_WIDTH), D_MODEL ** -0.5),
        'conv_w': nrm(ks[7], (L, CONV_WIDTH, CONV_CH), CONV_WIDTH ** -0.5),
        'conv_b': nrm(ks[8], (L, CONV_CH), 0.01),
        'dt_bias': dt_bias,
        'a_log': a_log,
        'd_skip': gain(ks[9], (L, SSD_HEADS)),
        'ssd_norm_w': gain(ks[12], (L, SSD_WIDTH)),
        'lambda_q1': nrm(ks[13], (L, DA_HEAD_DIM), 0.1),
        'lambda_k1': nrm(ks[14], (L, DA_HEAD_DIM), 0.1),
        'lambda_q2': nrm(ks[15], (L, DA_HEAD_DIM), 0.1),
        'lambda_k2': nrm(ks[16], (L, DA_HEAD_DIM), 0.1),
        'subln_w': gain(ks[17], (L, DA_V_DIM)),
        'rel_bias': nrm(ks[18], (NUM_BUCKETS, DA_HEADS), 0.2),
        'w_out_mix': nrm(ks[19], (L, MIX_WIDTH, D_MODEL), MIX_WIDTH ** -0.5),
        'norm_cross_w': gain(ks[20], (L, D_MODEL)),
        'norm_mem_w': gain(ks[21], (L, D_MODEL)),
        'w_cq': nrm(ks[22], (L, D_MODEL, D_MODEL), D_MODEL ** -0.5),
        'w_ck': nrm(ks[23], (L, D_MODEL, D_MODEL), D_MODEL ** -0.5),
        'w_cv': nrm(ks[24], (L, D_MODEL, D_MODEL), D_MODEL ** -0.5),
        'w_co': nrm(ks[25], (L, D_MODEL, D_MODEL), D_MODEL ** -0.5),
        'norm_ffn2_w': gain(ks[26], (L, D_MODEL)),
        'ffn2_w_in': nrm(ks[27], (L, D_MODEL, 2 * D_FF), D_MODEL ** -0.5),
        'ffn2_w_out': nrm(ks[28], (L, D_FF, D_MODEL), D_FF ** -0.5),
        'norm_final_w': gain(ks[29], (D_MODEL,)),
    }

def first_block(x, mem, norm_ffn1_w, ffn1_w_in, ffn1_w_out, norm_mix_w, w_in_mix,
              conv_w, conv_b, dt_bias, a_log, d_skip, ssd_norm_w,
              lambda_q1, lambda_k1, lambda_q2, lambda_k2, subln_w, rel_bias,
              w_out_mix, norm_cross_w, norm_mem_w, w_cq, w_ck, w_cv, w_co,
              norm_ffn2_w, ffn2_w_in, ffn2_w_out, norm_final_w):
    for l in range(DEPTH):
        lambda_init = 0.8 - 0.6 * math.exp(-0.3 * l)
        x = x + 0.5 * swiglu(rms_norm(x, norm_ffn1_w[l]), ffn1_w_in[l], ffn1_w_out[l])
        x = x + hybrid_mixer(rms_norm(x, norm_mix_w[l]), w_in_mix[l], conv_w[l], conv_b[l],
                             dt_bias[l], a_log[l], d_skip[l], ssd_norm_w[l],
                             lambda_q1[l], lambda_k1[l], lambda_q2[l], lambda_k2[l],
                             subln_w[l], rel_bias, w_out_mix[l], lambda_init)
        x = x + memory_cross_attention(rms_norm(x, norm_cross_w[l]),
                                       rms_norm(mem, norm_mem_w[l]),
                                       w_cq[l], w_ck[l], w_cv[l], w_co[l])
        x = x + 0.5 * swiglu(rms_norm(x, norm_ffn2_w[l]), ffn2_w_in[l], ffn2_w_out[l])
    return rms_norm(x, norm_final_w)


N_ATTN_HEADS = 8
HEAD_DIM = 64
ATTN_WIDTH = N_ATTN_HEADS * HEAD_DIM
CONV_GROUPS = 8
CONV_WIDTH_2 = 512
CONV_K = 3
D_FF_2 = 4 * D_MODEL
PLE_DIM = 256
SPLIT_SIZES = (ATTN_WIDTH, ATTN_WIDTH, ATTN_WIDTH, CONV_WIDTH_2, CONV_WIDTH_2, CONV_WIDTH_2, D_MODEL, D_MODEL)
SPLIT_POINTS = tuple(int(v) for v in np.cumsum(SPLIT_SIZES)[:-1])
D_IN = sum(SPLIT_SIZES)


def rms_norm_2(x, g):
    xf = x.astype(jnp.float32)
    var = jnp.mean(xf * xf, axis=-1, keepdims=True)
    return (xf * lax.rsqrt(var + EPS) * g.astype(jnp.float32)).astype(x.dtype)

def stick_breaking_attention(q, k, v):
    b, h, s, dh = q.shape
    nblk = s // Q_BLOCK
    scale = dh ** -0.5
    kf = k.astype(jnp.float32)
    vf = v.astype(jnp.float32)
    q_blocks = q.reshape(b, h, nblk, Q_BLOCK, dh).transpose(2, 0, 1, 3, 4)
    key_pos = jnp.arange(s, dtype=jnp.int32)
    starts = jnp.arange(nblk, dtype=jnp.int32) * Q_BLOCK

    def block(args):
        qb, start = args
        z = jnp.einsum('bhqd,bhkd->bhqk', qb.astype(jnp.float32), kf) * scale
        q_pos = start + jnp.arange(Q_BLOCK, dtype=jnp.int32)
        causal = key_pos[None, :] < q_pos[:, None]
        log_beta = jax.nn.log_sigmoid(z)
        log_keep = jnp.where(causal, log_beta - z, 0.0)
        between = lax.cumsum(log_keep, axis=3, reverse=True) - log_keep
        w = jnp.where(causal, jnp.exp(log_beta + between), 0.0)
        return jnp.einsum('bhqk,bhkd->bhqd', w, vf)

    out = lax.map(block, (q_blocks, starts))
    return out.transpose(1, 2, 0, 3, 4).reshape(b, h, s, dh).astype(q.dtype)

def causal_depthwise_conv(u, w):
    c = u.shape[-1]
    return lax.conv_general_dilated(
        u, w[:, None, :].astype(u.dtype), window_strides=(1,),
        padding=((CONV_K - 1, 0),), dimension_numbers=('NWC', 'WIO', 'NWC'),
        feature_group_count=c)

def second_inputs(seed: int = 0) -> dict:
    key = jax.random.key(seed)
    ks = jax.random.split(key, 20)
    f32 = jnp.float32

    def nrm(k, shape, fan_in):
        return jax.random.normal(k, shape, f32) * (fan_in ** -0.5)

    def gain(k, shape):
        return jnp.ones(shape, f32) + 0.05 * jax.random.normal(k, shape, f32)

    return {
        'x': jax.random.normal(ks[0], (BATCH, SEQ, D_MODEL), f32),
        'p': jax.random.normal(ks[1], (DEPTH, BATCH, SEQ, PLE_DIM), f32),
        'g_pre_mix': gain(ks[2], (DEPTH, D_MODEL)),
        'w_in': nrm(ks[3], (DEPTH, D_MODEL, D_IN), D_MODEL),
        'b_gate': 0.1 * jax.random.normal(ks[4], (DEPTH, 2 * D_MODEL), f32),
        'w_conv': nrm(ks[5], (DEPTH, CONV_K, CONV_WIDTH_2), CONV_K),
        'w_attn_out': nrm(ks[6], (DEPTH, ATTN_WIDTH, D_MODEL), ATTN_WIDTH),
        'w_conv_out': nrm(ks[7], (DEPTH, CONV_WIDTH_2, D_MODEL), CONV_WIDTH_2),
        'w_o': nrm(ks[8], (DEPTH, D_MODEL, D_MODEL), D_MODEL),
        'g_post_mix': gain(ks[9], (DEPTH, D_MODEL)),
        'g_pre_mlp': gain(ks[10], (DEPTH, D_MODEL)),
        'w_up': nrm(ks[11], (DEPTH, D_MODEL, D_FF_2), D_MODEL),
        'w_down': nrm(ks[12], (DEPTH, D_FF_2, D_MODEL), D_FF_2),
        'g_post_mlp': gain(ks[13], (DEPTH, D_MODEL)),
        'g_ple': gain(ks[14], (DEPTH, D_MODEL)),
        'w_ple_gate': nrm(ks[15], (DEPTH, D_MODEL, D_MODEL), D_MODEL),
        'w_ple_proj': nrm(ks[16], (DEPTH, PLE_DIM, D_MODEL), PLE_DIM),
    }

def second_block(x, p, g_pre_mix, w_in, b_gate, w_conv, w_attn_out, w_conv_out, w_o,
              g_post_mix, g_pre_mlp, w_up, w_down, g_post_mlp, g_ple, w_ple_gate, w_ple_proj):
    bsz, seq, _ = x.shape
    for i in range(DEPTH):
        h = rms_norm_2(x, g_pre_mix[i])
        proj = h @ w_in[i]
        q, k, v, cb, cc, cu, ga, gc = jnp.split(proj, SPLIT_POINTS, axis=-1)

        def heads(t):
            return t.reshape(bsz, seq, N_ATTN_HEADS, HEAD_DIM).transpose(0, 2, 1, 3)

        o = stick_breaking_attention(heads(q), heads(k), heads(v))
        o = o.transpose(0, 2, 1, 3).reshape(bsz, seq, ATTN_WIDTH)
        y_attn = o @ w_attn_out[i]

        y_conv = (cb * causal_depthwise_conv(cc * cu, w_conv[i])) @ w_conv_out[i]

        gates = jax.nn.sigmoid(jnp.concatenate([ga, gc], axis=-1) + b_gate[i])
        gate_attn, gate_conv = jnp.split(gates, 2, axis=-1)
        mixed = (gate_attn * y_attn + gate_conv * y_conv) @ w_o[i]
        x = x + rms_norm_2(mixed, g_post_mix[i])

        h = rms_norm_2(x, g_pre_mlp[i])
        f = jnp.square(jax.nn.relu(h @ w_up[i])) @ w_down[i]
        x = x + rms_norm_2(f, g_post_mlp[i])

        ple_gate = jax.nn.sigmoid(rms_norm_2(x, g_ple[i]) @ w_ple_gate[i])
        x = x + ple_gate * (p[i] @ w_ple_proj[i])
    return x


def setup_inputs(seed=0):
    out = dict(first_inputs(seed))
    for name, value in second_inputs(seed + 1).items():
        if name != "x":
            out[name + "_2"] = value
    return out


def reference(
    x, mem, norm_ffn1_w, ffn1_w_in, ffn1_w_out, norm_mix_w, w_in_mix, conv_w, conv_b, dt_bias,
    a_log, d_skip, ssd_norm_w, lambda_q1, lambda_k1, lambda_q2, lambda_k2, subln_w, rel_bias,
    w_out_mix, norm_cross_w, norm_mem_w, w_cq, w_ck, w_cv, w_co, norm_ffn2_w, ffn2_w_in,
    ffn2_w_out, norm_final_w, p_2, g_pre_mix_2, w_in_2, b_gate_2, w_conv_2, w_attn_out_2,
    w_conv_out_2, w_o_2, g_post_mix_2, g_pre_mlp_2, w_up_2, w_down_2, g_post_mlp_2, g_ple_2,
    w_ple_gate_2, w_ple_proj_2,
):
    x = first_block(
        x, mem, norm_ffn1_w, ffn1_w_in, ffn1_w_out, norm_mix_w, w_in_mix, conv_w, conv_b,
        dt_bias, a_log, d_skip, ssd_norm_w, lambda_q1, lambda_k1, lambda_q2, lambda_k2, subln_w,
        rel_bias, w_out_mix, norm_cross_w, norm_mem_w, w_cq, w_ck, w_cv, w_co, norm_ffn2_w,
        ffn2_w_in, ffn2_w_out, norm_final_w,
    )
    return second_block(
        x, p_2, g_pre_mix_2, w_in_2, b_gate_2, w_conv_2, w_attn_out_2, w_conv_out_2, w_o_2,
        g_post_mix_2, g_pre_mlp_2, w_up_2, w_down_2, g_post_mlp_2, g_ple_2, w_ple_gate_2,
        w_ple_proj_2,
    )


_drawn_inputs = setup_inputs


def setup_inputs(seed=0):
    import zlib

    import numpy as np

    out = dict(_drawn_inputs(seed))
    spreads = {}
    factors = {'norm_ffn1_w': 3.701,
     'conv_b': 5.553,
     'd_skip': 5.176,
     'ssd_norm_w': 3.892,
     'subln_w': 4.89,
     'norm_cross_w': 8.0,
     'norm_mem_w': 8.0,
     'norm_ffn2_w': 6.735,
     'g_ple_2': 23.659}
    for name, (base, spread) in spreads.items():
        noise = np.random.default_rng([zlib.crc32(name.encode()), seed]).standard_normal(out[name].shape)
        drawn = base * np.exp(spread * noise) if base else spread * noise
        out[name] = __import__('jax').numpy.asarray(drawn.astype(out[name].dtype))
    for name, factor in factors.items():
        out[name] = (out[name] * factor).astype(out[name].dtype)
    return out
```

```python
from contextlib import ExitStack

import numpy as np
import concourse.bass as bass
from concourse import mybir

F32 = mybir.dt.float32
F32R = mybir.dt.float32r
ALU = mybir.AluOpType
ACT = mybir.ActivationFunctionType
AX_X = mybir.AxisListType.X
ds = bass.ds

P = 128
S = 512
TT = S // P
D = 1024
DC = D // P
FF = 2816
FC = FF // P
ML = 256
MT = ML // P
UC = 8
UNIT = UC * P
RING = 4
EPS = 1e-6
NEG = -3.0e38
MASK = 1.0e30
SH, SHD, SG, SN = 16, 64, 4, 128
GH = SH // SG
AH, AV = 8, 128
XH = 4
KH = 8
FF2 = 4096
HC = FF2 // P // 2
LAMBDA_INIT = 0.2
BIAS_W = S + P - 1

STAGES = [
    ("ffn1_in", 2 * FC), ("ffn1_out", 24),
    ("xbc", 16), ("z", 8), ("q", 8), ("k", 8), ("v", 8), ("mix_ssd", 8), ("mix_attn", 8),
    ("ck", 8), ("cv", 8), ("cq", 8), ("co", 8),
    ("ffn2_in", 2 * FC), ("ffn2_out", 24),
    ("qk2", 8), ("v2", 4), ("conv2", 12), ("gates2", 16), ("branch2", 8), ("o2", 8),
    ("up_a", HC), ("down_a", 16), ("up_b", HC), ("down_b", 16), ("proj2", 4), ("ple2", 8),
]
TILES = {"ffn1_in": 2 * FC, "ffn1_out": 8, "xbc": 16, "q": 8, "k": 8, "mix_ssd": 8, "mix_attn": 8,
         "ck": 8, "cq": 8, "co": 8, "ffn2_in": 2 * FC, "ffn2_out": 8, "qk2": 8, "conv2": 12,
         "gates2": 16, "branch2": 16, "o2": 8, "up_a": HC, "down_a": 8, "up_b": HC, "down_b": 8,
         "proj2": 8, "ple2": 8}
UNIT0, TILE0 = {}, {}
_u = _t = 0
for _name, _n in STAGES:
    UNIT0[_name], TILE0[_name] = _u, _t
    _u += _n
    _t += TILES.get(_name, 0)
UNITS = _u
assert UNITS % RING == 0 and all(v % 2 == 0 for v in TILE0.values())

OPERANDS = ["load", "ffn1_out", "mix_attn", "co", "ffn2_out", "branch2", "post", "pmlp"]
SUMS = ["load", "ffn1_out", "mix_attn", "co", "ffn2_out", "o2", "post", "down", "pmlp"]
NORMS = ["n_ffn1", "n_mix", "n_cross", "n_ffn2", "n_fin", "n_post", "n_mlp", "n_pmlp", "n_ple"]

COLS = {}
_c = 0
for _name, _n in (("norm_ffn1_w", 8), ("norm_mix_w", 8), ("conv_w", 64), ("conv_b", 16), ("ssd_norm_w", 8),
                  ("subln_w", 1), ("norm_cross_w", 8), ("norm_mem_w", 8), ("norm_ffn2_w", 8),
                  ("norm_final_w", 8), ("g_pre_mix_2", 8), ("b_gate_2", 16), ("w_conv_2", 12),
                  ("g_post_mix_2", 8), ("g_pre_mlp_2", 8), ("g_post_mlp_2", 8), ("g_ple_2", 8)):
    COLS[_name] = _c
    _c += _n
NCOLS = _c
ROWS = {"dt_bias": 0, "a_log": 16, "d_skip": 32, "lambda_q1": 48, "lambda_k1": 112, "lambda_q2": 176,
        "lambda_k2": 240}
NROWS = 304


def build(nc, wstream, xT, memT, pT, cols_d, rows_d, wdt_d, relb_d, consts_d, onehot_d, pen_d, out):
    ctx = ExitStack()
    with ctx:
        sems = {}

        def sem(name):
            if name not in sems:
                sems[name] = ctx.enter_context(nc.semaphore(name))
            return sems[name]

        def norm_sem(step):
            return sem(f"norm_{step}")

        def norm_count(step, name, k):
            n = NORMS.index(name)
            more = {"root": 2, "row": 1}.get(step, 0)
            return n + k + (more if n > NORMS.index("n_fin") else 0)

        def gx_count(stage, k):
            return OPERANDS.index(stage) * DC + k

        def square_count(stage, k):
            return SUMS.index(stage) * DC + k

        def sum_count(stage, k):
            return SUMS.index(stage) * (DC + 1) + k

        def ffn_count(name, k):
            return (FC if name == "ffn2" else 0) + k

        cursor = [(nc.sbuf_base + 63) // 64 * 64]

        def fixed(name, shape, dt=F32):
            t = nc.alloc_sbuf_tensor_at(name, [P] + shape, dt, offset=cursor[0])
            cursor[0] += (int(np.prod(shape)) * 4 + 63) // 64 * 64
            return t

        x = fixed("x", [DC, S])
        GX_HI, GX_LO = cursor[0], cursor[0] + DC * S * 4
        gx_hi = fixed("gx_hi", [DC, S], F32R)
        gx_lo = fixed("gx_lo", [DC, S], F32R)
        w_raw = fixed("w_raw", [RING, UNIT])
        w_hi = fixed("w_hi", [RING, UNIT], F32R)
        w_lo = fixed("w_lo", [RING, UNIT], F32R)
        consts = fixed("consts", [7 * P])
        cols = fixed("cols", [NCOLS])
        rows = fixed("rows", [NROWS])
        rstd_row = fixed("rstd_row", [S])
        sumsq = fixed("sumsq", [S])
        square = fixed("square", [S])
        rstd_col = fixed("rstd_col", [TT])
        root_col = fixed("root_col", [2 * TT])
        rfin_row = fixed("rfin_row", [S])
        eps_col = fixed("eps_col", [1])
        subln = fixed("subln", [1])
        fin = fixed("fin", [32])
        wdt = fixed("wdt", [8, 16])
        wdt_hi = fixed("wdt_hi", [8, 16], F32R)
        wdt_lo = fixed("wdt_lo", [8, 16], F32R)
        m_root = fixed("m_root", [MT])
        m_rstd = fixed("m_rstd", [MT])
        xmin = fixed("xmin", [16])
        xsum = fixed("xsum", [16])
        xrec = fixed("xrec", [16])
        y_sq, y_root, y_rstd = xmin, xsum, xrec
        REGION = cursor[0]
        REGION_END = nc.sbuf_usable_end if not callable(nc.sbuf_usable_end) else nc.sbuf_usable_end()

        def at(name, kb, shape, dt=F32):
            off = REGION + int(kb * 1024)
            size = int(np.prod(shape)) * 4
            assert off + size <= REGION_END, (name, off + size - REGION_END)
            return nc.alloc_sbuf_tensor_at(name, [P] + shape, dt, offset=off)

        ident, tri_le, ones, flip, neg_ge, neg_ones, tri_lt = (consts[:, i * P:(i + 1) * P] for i in range(7))

        def first(i):
            return isinstance(i, int) and i == 0

        def tile_of(buf, c):
            if isinstance(c, int):
                return buf[:, c, :]
            n = buf.shape[2]
            return buf[:, :, :].rearrange("p a b -> p (a b)")[:, ds(c * n, n)]

        def col(name, i):
            return cols[:, COLS[name] + i:COLS[name] + i + 1]

        def col_at(name, i):
            return cols[:, ds(COLS[name] + i, 1)]

        ff_hi = at("ff_hi", 0, [FC, S], F32R)
        ff_lo = at("ff_lo", 44, [FC, S], F32R)
        ff_gate = at("ff_gate", 88, [S])
        ff_silu = at("ff_silu", 90, [S])
        ff_up = at("ff_up", 92, [S])
        ff_act = at("ff_act", 94, [S])
        sumsq2 = at("sumsq2", 88, [S])
        square2 = at("square2", 90, [S])
        z_tok = at("z_tok", 0, [TT, D])
        bc = at("bc", 16, [8, S])
        xs_tok = at("xs_tok", 32, [TT, D])
        xs_T = at("xs_T", 48, [8, S])
        conv_in = at("conv_in", 92.5, [S + 3])
        conv_acc = at("conv_acc", 88.5, [S])
        dt_pre = at("dt_pre", 70.5, [TT, SH])
        dt_T = at("dt_T", 64, [S])
        dt_exp = at("dt_exp", 70.75, [TT, SH])
        dt_ln = at("dt_ln", 71, [TT, SH])
        dt = at("dt", 71.25, [TT, SH])
        a_row = at("a_row", 71.5, [SH])
        la = at("la", 71.75, [TT, SH])
        cum = at("cum", 72, [TT, SH])
        ecum = at("ecum", 72.5, [TT, SH])
        to_end = at("to_end", 72.75, [TT, SH])
        e_end = at("e_end", 73, [TT, SH])
        c_dec = at("c_dec", 73.25, [TT, SH])
        cb_m = at("cb_m", 74.5, [2, P])
        b_tok = at("b_tok", 75.5, [2, P])
        decay = at("decay", 76.5, [2, GH, P])
        mix_m = at("mix_m", 80.5, [2, GH, P])
        seg = at("seg", 64, [2, GH, P])
        state = at("state", 84.5, [SG, GH, SHD])
        xdt = at("xdt", 88.5, [2, GH, SHD])
        xdte = at("xdte", 90.5, [2, GH, SHD])
        y_a = at("y_a", 92.5, [GH, SHD])
        y_b = at("y_b", 93.5, [GH, SHD])
        y_c = at("y_c", 94.5, [GH, SHD])
        ysq_tmp = at("ysq_tmp", 69, [GH * SHD])
        ys_hi = at("ys_hi", 16, [DC, S], F32R)
        ys_lo = at("ys_lo", 32, [DC, S], F32R)
        q_T = at("q_T", 48, [AH, S])
        k_T = at("k_T", 64, [AH, S])
        v_tok = at("v_tok", 80, [TT, D])
        NB = P * (1 + 2 + 3 + 4)

        def in_gx(name, kb, shape):
            assert kb * 1024 + int(np.prod(shape)) * 4 <= 2 * DC * S * 4
            return nc.alloc_sbuf_tensor_at(name, [P] + shape, F32, offset=GX_HI + int(kb * 1024))

        bias_h = in_gx("bias_h", 0, [2, S])
        prob = in_gx("prob", 4, [2, 2, NB])
        w_T = in_gx("w_T", 24, [NB])
        o_sq = in_gx("o_sq", 29, [S])
        lam_tmp = in_gx("lam_tmp", 29, [SHD])
        rsum = in_gx("rsum", 31, [2, 8])
        rrec = in_gx("rrec", 31.125, [2, 8])
        amin = in_gx("amin", 31.25, [2, 8])
        o_root = in_gx("o_root", 31.5, [TT * AH])
        o_rstd = in_gx("o_rstd", 31.625, [TT * AH])
        lam = in_gx("lam", 31.75, [8])
        o_nrm = in_gx("o_nrm", 0, [2, S])
        o_un = at("o_un", 0, [AH, S])
        bflip = [square, rfin_row]
        o_hi = at("o_hi", 48, [AH, S], F32R)
        o_lo = at("o_lo", 64, [AH, S], F32R)
        relb = at("relb", 80, [AH])
        onehot = at("onehot", 81, [BIAS_W + 1])
        pen = at("pen", 84, [BIAS_W + 1])
        brow = at("brow", 87, [BIAS_W + 1])
        m_T = at("m_T", 0, [DC, ML])
        m_hi = at("m_hi", 8, [DC, ML], F32R)
        m_lo = at("m_lo", 16, [DC, ML], F32R)
        kx_T = at("kx_T", 24, [DC, ML])
        vx = at("vx", 32, [MT, D])
        px = at("px", 40, [4, ML])
        pxT = at("pxT", 44, [MT, S])
        qx_T = at("qx_T", 48, [DC, S])
        ox_hi = at("ox_hi", 64, [DC, S], F32R)
        ox_lo = at("ox_lo", 80, [DC, S], F32R)
        m_sum = at("m_sum", 40, [ML])
        m_row = at("m_row", 41, [ML])
        q2_T = at("q2_T", 0, [4, S])
        k2_T = at("k2_T", 8, [4, S])
        v2_tok = at("v2_tok", 16, [TT, S])
        cv_hi = at("cv_hi", 24, [4, S], F32R)
        cv_lo = at("cv_lo", 32, [4, S], F32R)
        gates = at("gates", 40, [16, S])
        o2_hi = at("o2_hi", 72, [4, S], F32R)
        o2_lo = at("o2_lo", 80, [4, S], F32R)
        gate_t = at("gate_t", 88, [S])
        cc_t = at("cc_t", 90, [S])
        cu_t = at("cu_t", 92, [S])
        cprod = at("cprod", 94, [S + 2])
        cacc = square

        def over(name, base, kb, n):
            return nc.alloc_sbuf_tensor_at(name, [P, n], F32, offset=base + kb * 1024)

        sz_buf = [over(f"stick_exp{i}", GX_HI, 5 * i, NB) for i in range(2)]
        sp_buf = [over(f"stick_sum{i}", GX_LO, 5 * i, NB) for i in range(2)]
        w_buf = [over("stick_w0", GX_HI, 10, NB), over("stick_w1", GX_LO, 10, NB)]
        br_a = at("br_a", 88, [S])
        br_b = at("br_b", 90, [S])
        br_m = at("br_m", 92, [S])
        y_o2 = at("y_o2", 0, [DC, S])
        pn_t = at("pn_t", 38, [S])
        up_hi = at("up_hi", 16, [HC, S], F32R)
        up_lo = at("up_lo", 48, [HC, S], F32R)
        f_acc = at("f_acc", 80, [DC, S])
        up_t = at("up_t", 0, [S])
        up_a = at("up_a", 2, [S])
        p_T = at("p_T", 4, [2, S])
        p_hi = at("p_hi", 8, [2, S], F32R)
        p_lo = at("p_lo", 12, [2, S], F32R)
        proj = at("proj", 16, [DC, S])
        ple_t = at("ple_t", 32, [S])
        ple_g = at("ple_g", 34, [S])
        ple_o = at("ple_o", 36, [DC, S])

        bank = [ctx.enter_context(nc.psum_tensor(f"bank{i}", [P, S], F32)) for i in range(8)]
        bias_r = nc.dram_tensor("bias_rows", (AH, BIAS_W + 1), F32, kind="Internal").ap()

        unit_raw = [sem(f"unit_raw{i}") for i in range(RING)]
        unit_hi = sem("unit_hi")
        unit_lo = sem("unit_lo")
        unit_done = sem("unit_done")
        tile_free = sem("tile_free")
        def wait(eng, s, value):
            if not isinstance(value, int) or value > 0:
                eng.wait_ge(s, value)

        def blocks(eng, n, body, peel=0):
            for i in range(peel):
                body(i)
            if n - peel == 1:
                body(n - 1)
            elif n > peel:
                with eng.Fori(peel, n) as i:
                    body(i)

        block = ctx.enter_context(nc.Block())

        @block.sync
        def _(sp):
            for s in range(RING):
                sp.dma_start(w_raw[:, s, :], wstream[s]).then_inc(unit_raw[s], 16)
            with sp.Fori(1, UNITS // RING) as r:
                for s in range(RING):
                    sp.wait_ge(unit_lo, r * RING + (s - RING + 1))
                    sp.dma_start(w_raw[:, s, :], wstream[ds(r * RING + s, 1)].rearrange("a p n -> (a p) n"))\
                      .then_inc(unit_raw[s], 16)
            for m in range(DC):
                sp.wait_ge(sem("out_ready"), m + 1)
                sp.dma_start(out[m * P:(m + 1) * P, :], ple_o[:, m, :]).then_inc(sem("out_stored"), 16)
            sp.wait_ge(sem("out_stored"), 16 * DC)

        @block.gpsimd
        def _(pool):
            with pool.Fori(0, UNITS // RING) as r:
                for s in range(RING):
                    pool.wait_ge(unit_hi, r * RING + (s + 1))
                    nc.gpsimd.tensor_tensor(w_lo[:, s, :], w_raw[:, s, :], w_hi[:, s, :].bitcast(F32),
                                            ALU.subtract).then_inc(unit_lo, 1)

        @block.tensor
        def _(pe):
            def products(slot, blk, dst, rhs, first, last):
                hi = w_hi[:, slot, blk * P:(blk + 1) * P]
                lo = w_lo[:, slot, blk * P:(blk + 1) * P]
                nc.tensor.matmul(dst, hi, rhs[0], start=first, stop=False)
                nc.tensor.matmul(dst, hi, rhs[1], start=False, stop=False)
                return nc.tensor.matmul(dst, lo, rhs[0], start=False, stop=last)

            def tiles(stage, rhs, chunks, body, peel=0, ready=None, n=S, hooks=()):
                per = -(-chunks // UC)
                assert (body * per) % RING == 0

                def block_of(i):
                    for j in range(body):
                        T = TILE0[stage] + i * body + j
                        wait(pe, tile_free, T - 1)
                        dst = bank[j % 2][:, 0:n]
                        for uu in range(per):
                            jj = j * per + uu
                            pe.wait_ge(unit_lo, UNIT0[stage] + i * (body * per) + (jj + 1))
                            kk = range(uu * UC, min(chunks, (uu + 1) * UC))
                            for k in kk:
                                if ready and (first(i) and j == 0):
                                    ready(k)
                                mm = products((UNIT0[stage] + jj) % RING, k - uu * UC, dst, rhs(k),
                                              k == 0, k == chunks - 1)
                                if first(i) and (j, k) in dict(hooks):
                                    dict(hooks)[(j, k)]()
                            mm.then_inc(unit_done, 1)
                blocks(pe, TILES[stage] // body, block_of, peel)

            def token_group(stage, g, lhs, n_tiles, group, order_of=(2, 3, 4, 5), between=None):
                wait(pe, sem("token_free"), group)
                for u in range(4):
                    U = UNIT0[stage] + 4 * g + u
                    pe.wait_ge(unit_lo, U + 1)
                    for t in range(n_tiles):
                        for b in range(2):
                            k = 2 * u + b
                            rh = w_hi[:, U % RING, b * S:(b + 1) * S]
                            rl = w_lo[:, U % RING, b * S:(b + 1) * S]
                            dst = bank[order_of[t]][:, :]
                            a = [m[:, k, t * P:(t + 1) * P] for m in lhs]
                            nc.tensor.matmul(dst, a[0], rh, start=(k == 0), stop=False, skip_group_check=True)
                            nc.tensor.matmul(dst, a[1], rh, start=False, stop=False, skip_group_check=True)
                            mm = nc.tensor.matmul(dst, a[0], rl, start=False, stop=(k == DC - 1),
                                                  skip_group_check=True)
                    mm.then_inc(unit_done, 1)
                    if between:
                        between(4 * g + u)

            def norm_hooks(name, summed, stats=1):
                def stat():
                    pe.wait_ge(sem("summed"), sum_count(summed, DC + 1))
                    if stats == 2:
                        pe.wait_ge(sem("summed2"), DC + 1)
                    for s in range(stats):
                        src = sumsq if s == 0 else sumsq2
                        for t in range(TT):
                            mm = nc.tensor.matmul(bank[7][:, s * TT + t:s * TT + t + 1], src[:, t * P:(t + 1) * P],
                                                  ones[:, 0:1], start=True, stop=True)
                    mm.then_inc(norm_sem("stat"), 1)

                def row():
                    pe.wait_ge(norm_sem("col"), norm_count("col", name, 1))
                    for t in range(TT):
                        mm = nc.tensor.matmul(bank[7][:, t * P:(t + 1) * P],
                                              rstd_col[:, t:t + 1].to_broadcast([P, P]), ident, start=True, stop=True)
                    mm.then_inc(norm_sem("row"), 1)
                    if stats == 2:
                        pe.wait_ge(norm_sem("ready"), norm_count("ready", name, 1))
                        for t in range(TT):
                            mm = nc.tensor.matmul(bank[7][:, t * P:(t + 1) * P],
                                                  root_col[:, TT + t:TT + t + 1].to_broadcast([P, P]), ident,
                                                  start=True, stop=True)
                        mm.then_inc(norm_sem("row"), 1)
                return (((0, UC - 1), stat), ((1, 3), row))

            gx = lambda k: (gx_hi[:, k, :], gx_lo[:, k, :])

            def gx_ready(name):
                return lambda k: pe.wait_ge(sem("gx_lo_done"), gx_count(name, k + 1))

            def ffn(name, norm, before):
                tiles(f"{name}_in", gx, DC, 4, peel=1, ready=gx_ready(before), hooks=norm_hooks(norm, before))

                def act_ready(k):
                    if k % UC == 0:
                        pe.wait_ge(sem("ffn_act_lo"), ffn_count(name, min(FC, k + UC)))
                tiles(f"{name}_out", lambda k: (ff_hi[:, k, :], ff_lo[:, k, :]), FC, 4, peel=1, ready=act_ready)

            pe.wait_ge(sem("setup_in"), 16 * 7)
            mm = nc.tensor.matmul(bank[2][0:AH, :], relb[0:32, :], onehot[0:32, 0:S], start=True, stop=True)
            mm = nc.tensor.matmul(bank[3][0:AH, 0:P], relb[0:32, :], onehot[0:32, S:S + P], start=True, stop=True)
            mm.then_inc(sem("brow_sum"), 1)

            ffn("ffn1", "n_ffn1", "load")

            tiles("xbc", gx, DC, 4, peel=1, ready=gx_ready("ffn1_out"), hooks=norm_hooks("n_mix", "ffn1_out"))
            pe.wait_ge(sem("wdt_lo"), 1)
            for k in range(DC):
                nc.tensor.matmul(bank[6][0:SH, :], wdt_hi[:, k, :], gx_hi[:, k, :], start=(k == 0), stop=False)
                nc.tensor.matmul(bank[6][0:SH, :], wdt_hi[:, k, :], gx_lo[:, k, :], start=False, stop=False)
                mm = nc.tensor.matmul(bank[6][0:SH, :], wdt_lo[:, k, :], gx_hi[:, k, :], start=False,
                                      stop=(k == DC - 1))
            mm.then_inc(sem("dt_mm"), 1)

            def turn_x(j):
                pe.wait_ge(sem("xbc_silu"), j + 1)
                wait(pe, sem("xs_copied"), j - 1)
                for t in range(TT):
                    mm = nc.tensor.transpose(bank[j % 2][:, t * P:(t + 1) * P],
                                             xs_T[:, j, t * P:(t + 1) * P], ident)
                mm.then_inc(sem("xs_turned"), 1)

            def between_z(u):
                if u == 0:
                    pe.wait_ge(tile_free, TILE0["q"])
                    pe.wait_ge(sem("dt_copied"), 1)
                    for t in range(TT):
                        mm = nc.tensor.transpose(bank[6][:, t * SH:(t + 1) * SH], dt_T[0:SH, t * P:(t + 1) * P],
                                                 ident[0:SH, 0:SH])
                    mm.then_inc(sem("dt_turned"), 1)
                turn_x(u)

            for g in range(2):
                token_group("z", g, (gx_hi, gx_lo), TT, 4 * g, between=between_z)
            pe.wait_ge(sem("la_ready"), 1)
            nc.tensor.matmul(bank[7][:, 0:TT * SH], tri_le, la[:, :, :], start=True, stop=True)
            nc.tensor.matmul(bank[7][:, TT * SH:2 * TT * SH], ones, la[:, :, :], start=True, stop=True)\
              .then_inc(sem("cum_mm"), 1)

            def ssd_front(n):
                t, g, b = n // SG, n % SG, n % 2
                tok = slice(t * P, (t + 1) * P)
                wait(pe, sem("cell_a_read"), 2 * n)
                nc.tensor.matmul(bank[1][:, 0:P], bc[:, g, tok], bc[:, SG + g, tok], start=True, stop=True)
                nc.tensor.transpose(bank[1][:, P:2 * P], bc[:, g, tok], ident).then_inc(sem("cell_a"), 1)
                wait(pe, sem("decayed"), n - 1)
                for r in range(GH):
                    h = g * GH + r
                    mm = nc.tensor.matmul(bank[2 + b][:, r * P:(r + 1) * P],
                                          la[:, t, h:h + 1].to_broadcast([P, P]), tri_le, start=True, stop=True)
                mm.then_inc(sem("cell_b"), 1)

            def ssd_back(n):
                t, g, b = n // SG, n % SG, n % 2
                pe.wait_ge(sem("cell_m"), n + 1)
                wait(pe, sem("cell_done"), n - 1)
                for r in range(GH):
                    mm = nc.tensor.matmul(bank[4 + b][:, r * SHD:(r + 1) * SHD], mix_m[:, b, r, :],
                                          xdt[:, b, r, :], start=True, stop=True)
                if t > 0:
                    wait(pe, sem("cell_done"), n - SG + 1)
                    mm = nc.tensor.matmul(bank[4 + b][:, 2 * P:4 * P], bc[:, SG + g, t * P:(t + 1) * P],
                                          state[:, g, :, :], start=True, stop=True)
                mm = nc.tensor.matmul(bank[6 + b][:, 0:2 * P], b_tok[:, b, :], xdte[:, b, :, :],
                                      start=True, stop=True)
                mm.then_inc(sem("cell_y"), 1)

            def q_half(n):
                c, half = n // 2, n % 2
                if half == 0:
                    pe.wait_ge(unit_lo, UNIT0["q"] + c + 1)
                    pe.wait_ge(tile_free, TILE0["q"] + c)
                for k in range(4 * half, 4 * half + 4):
                    mm = products((UNIT0["q"] + c) % RING, k, bank[0][:, :], gx(k), k == 0, k == DC - 1)
                if half == 1:
                    mm.then_inc(unit_done, 1)

            pe.wait_ge(sem("xs_copied"), 8)
            pe.wait_ge(sem("xbc_silu"), 16)
            pe.wait_ge(sem("cum_read"), 1)
            pe.wait_ge(sem("token_free"), 8)
            for n in range(TT * SG + 1):
                if n < TT * SG:
                    ssd_front(n)
                    q_half(n)
                if n > 0:
                    ssd_back(n - 1)

            def turn_y(j):
                if j == 0:
                    pe.wait_ge(sem("y_norm"), TT * SG)
                wait(pe, sem("ys_lo"), j - 1)
                for t in range(TT):
                    mm = nc.tensor.transpose(bank[6 + j % 2][:, t * P:(t + 1) * P],
                                             z_tok[:, t, j * P:(j + 1) * P], ident)
                mm.then_inc(sem("ys_turned"), 1)

            pe.wait_ge(tile_free, TILE0["k"])
            tiles("k", gx, DC, 4)
            for g in range(2):
                token_group("v", g, (gx_hi, gx_lo), TT, 8 + 4 * g, between=turn_y)
            pe.wait_ge(sem("token_free"), 16)
            pe.wait_ge(tile_free, TILE0["mix_ssd"])

            def ssd_half(h, half):
                if half == 0:
                    pe.wait_ge(unit_lo, UNIT0["mix_ssd"] + h + 1)
                    pe.wait_ge(sem("bias_ready"), min(h + 2, AH))
                    pe.wait_ge(tile_free, TILE0["mix_ssd"] + h)
                for k in range(4 * half, 4 * half + 4):
                    mm = products((UNIT0["mix_ssd"] + h) % RING, k, bank[1][:, :], (ys_hi[:, k, :], ys_lo[:, k, :]),
                                  k == 0, k == DC - 1)
                if half == 1:
                    mm.then_inc(unit_done, 1)

            def score(h, i, c):
                n = h * 8 + i * 2 + c
                wait(pe, sem("score_read"), n - 2)
                hp = slice(c * 64, c * 64 + 64)
                nc.tensor.matmul(bank[2 + n % 3][:, 0:(i + 1) * P], q_T[hp, h, i * P:(i + 1) * P],
                                 k_T[hp, h, 0:(i + 1) * P], start=True, stop=True).then_inc(sem("score"), 1)

            def turn(h):
                pe.wait_ge(sem("diffed"), h + 1)
                if h > 0:
                    pe.wait_ge(sem("wT_dve"), 2 * h)
                    pe.wait_ge(sem("wT_act"), h)
                for j in range(TT):
                    for i in range(j, TT):
                        base = 2 * P * (j == 3)
                        mm = nc.tensor.transpose(
                            bank[5 + min(j, 2)][:, base + (i - j) * P:base + (i - j + 1) * P],
                            prob[:, h % 2, 0, P * (i * (i + 1) // 2 + j):P * (i * (i + 1) // 2 + j + 1)], ident)
                mm.then_inc(sem("turned"), 1)

            def values(h):
                pe.wait_ge(sem("wT_dve"), 2 * (h + 1))
                pe.wait_ge(sem("wT_act"), h + 1)
                wait(pe, sem("o_copied"), h)
                off = 0
                for j in range(TT):
                    w = S - j * P
                    mm = nc.tensor.matmul(bank[0][:, j * P:S], v_tok[:, j, h * AV:(h + 1) * AV],
                                          w_T[:, off:off + w], start=(j == 0), stop=(j == TT - 1),
                                          skip_group_check=True)
                    off += w
                mm.then_inc(sem("o_mm"), 1)

            def head_stat(h):
                pe.wait_ge(sem("o_squared"), h + 1)
                for t in range(TT):
                    mm = nc.tensor.matmul(bank[7][:, 384 + h * TT + t:385 + h * TT + t], o_sq[:, t * P:(t + 1) * P],
                                          ones[:, 0:1], start=True, stop=True)
                mm.then_inc(sem("o_stat"), 1)

            def flip_bias(h):
                pe.wait_ge(sem(f"bias_in{h % 2}"), 16 * (h // 2 + 1))
                wait(pe, sem("bias_ready"), h)
                if h > 1:
                    pe.wait_ge(tile_free, TILE0["mix_ssd"] + h - 1)
                nc.tensor.matmul(bank[1][:, :], flip, bflip[h % 2][:, :], start=True, stop=True)\
                  .then_inc(sem("bias_flip"), 1)

            flip_bias(0)
            for h in range(AH + 2):
                if h < AH:
                    for n in range(3):
                        score(h, n // 2, n % 2)
                if h + 1 < AH:
                    flip_bias(h + 1)
                if h < AH:
                    ssd_half(h, 0)
                if 0 < h <= AH:
                    turn(h - 1)
                if h < AH:
                    for n in range(3, 8):
                        score(h, n // 2, n % 2)
                    ssd_half(h, 1)
                if 0 < h <= AH:
                    values(h - 1)
                if h > 1:
                    head_stat(h - 2)
            pe.wait_ge(sem("o_col"), 1)
            for h in range(AH):
                wait(pe, sem("o_nrmd"), h - 1)
                for t in range(TT):
                    mm = nc.tensor.matmul(bank[2 + h % 2][:, t * P:(t + 1) * P],
                                          o_rstd[:, h * TT + t:h * TT + t + 1].to_broadcast([P, P]), ident,
                                          start=True, stop=True)
                mm.then_inc(sem("o_row"), 1)
            tiles("mix_attn", lambda k: (o_hi[:, k, :], o_lo[:, k, :]), DC, 4, peel=1,
                  ready=lambda k: pe.wait_ge(sem("o_lo"), k + 1))
            pe.wait_ge(sem("m_sum"), DC + 1)
            for t in range(MT):
                mm = nc.tensor.matmul(bank[6][:, t:t + 1], m_sum[:, t * P:(t + 1) * P], ones[:, 0:1],
                                      start=True, stop=True)
            mm.then_inc(sem("m_stat"), 1)
            pe.wait_ge(sem("m_col"), 1)
            for t in range(MT):
                mm = nc.tensor.matmul(bank[6][:, t * P:(t + 1) * P], m_rstd[:, t:t + 1].to_broadcast([P, P]),
                                      ident, start=True, stop=True)
            mm.then_inc(sem("m_rowed"), 1)
            pe.wait_ge(sem("m_lo"), DC)
            tiles("ck", lambda k: (m_hi[:, k, :], m_lo[:, k, :]), DC, 4, n=ML)
            for g in range(2):
                token_group("cv", g, (m_hi, m_lo), MT, 16 + 2 * g)
            tiles("cq", gx, DC, 4, peel=1, ready=gx_ready("mix_attn"), hooks=norm_hooks("n_cross", "mix_attn"))
            pe.wait_ge(tile_free, TILE0["co"])
            pe.wait_ge(sem("token_free"), 20)

            def x_score(n):
                hd, i = n // TT, n % TT
                wait(pe, sem("x_exp"), n - 2)
                for e in range(2):
                    mm = nc.tensor.matmul(bank[2 + n % 3][:, 0:ML], qx_T[:, 2 * hd + e, i * P:(i + 1) * P],
                                          kx_T[:, 2 * hd + e, :], start=(e == 0), stop=(e == 1))
                mm.then_inc(sem("x_score"), 1)

            def x_turn(n):
                hd, i = n // TT, n % TT
                pe.wait_ge(sem("x_prob"), n + 1)
                if i == 0:
                    wait(pe, sem("x_pT"), 2 * hd)
                for kk in range(MT):
                    mm = nc.tensor.transpose(bank[5 + kk][:, i * P:(i + 1) * P],
                                             px[:, n % 4, kk * P:(kk + 1) * P], ident)
                mm.then_inc(sem("x_turned"), 1)

            def x_values(hd):
                pe.wait_ge(sem("x_pT"), 2 * (hd + 1))
                for e in range(2):
                    wait(pe, sem("ox_lo"), 2 * hd + e - 1)
                    for kk in range(MT):
                        mm = nc.tensor.matmul(bank[7 - 6 * e][:, :], vx[:, kk, hd * 256 + e * P:hd * 256 + (e + 1) * P],
                                              pxT[:, kk, :], start=(kk == 0), stop=(kk == MT - 1))
                    mm.then_inc(sem("ox_mm"), 1)

            for n in range(XH * TT + 2):
                if n < XH * TT:
                    x_score(n)
                if 0 < n <= XH * TT:
                    x_turn(n - 1)
                if n > 1 and (n - 2) % TT == TT - 1:
                    x_values((n - 2) // TT)
            tiles("co", lambda k: (ox_hi[:, k, :], ox_lo[:, k, :]), DC, 4, peel=1,
                  ready=lambda k: pe.wait_ge(sem("ox_lo"), k + 1))
            ffn("ffn2", "n_ffn2", "co")
            tiles("qk2", gx, DC, 4, peel=1, ready=gx_ready("ffn2_out"), hooks=norm_hooks("n_fin", "ffn2_out", 2))
            token_group("v2", 0, (gx_hi, gx_lo), TT, 20)
            tiles("conv2", gx, DC, 12)
            tiles("gates2", gx, DC, 4)
            pe.wait_ge(sem("token_free"), 24)
            pe.wait_ge(tile_free, TILE0["branch2"])

            place = {0: (0, 0), 1: (1, 0), 3: (1, 3 * P), 2: (2, 0)}

            def st(buf, b, j, lo=0):
                o = S * place[j][0] + place[j][1]
                return buf[b][:, o + lo:o + S - j * P]

            def scores_into(first_bank, h, j, stop):
                hp = slice(h % 2 * 64, h % 2 * 64 + 64)
                bk, o = place[j]
                return nc.tensor.matmul(bank[first_bank + bk][:, o:o + S - j * P], k2_T[hp, h // 2, j * P:(j + 1) * P],
                                        q2_T[hp, h // 2, j * P:S], start=True, stop=stop)

            def stick_z(h):
                wait(pe, sem("sp_ready"), h)
                for j in (0, 1, 3, 2):
                    mm = scores_into(2, h, j, True)
                mm.then_inc(sem("z_mm"), 1)

            def stick_c(h):
                pe.wait_ge(sem("sp_masked"), h + 1)
                wait(pe, sem("w_exp"), h)
                for j in (0, 1, 3, 2):
                    scores_into(5, h, j, False)
                    bk, o = place[j]
                    dst = bank[5 + bk]
                    for jj in range(j + 1, TT):
                        nc.tensor.matmul(dst[:, o + (jj - j) * P:o + S - j * P], neg_ones,
                                         st(sp_buf, h % 2, jj), start=False, stop=False)
                    mm = nc.tensor.matmul(dst[:, o:o + S - j * P], neg_ge, st(sp_buf, h % 2, j),
                                          start=False, stop=True)
                mm.then_inc(sem("c_mm"), 1)

            def stick_values(h):
                pe.wait_ge(sem("w_masked"), h + 1)
                if h >= 4 and h % 2 == 0:
                    pe.wait_ge(sem("o2_lo"), h // 2 - 1)
                rows_ = slice(h % 2 * 64, h % 2 * 64 + 64)
                for j in range(TT):
                    mm = nc.tensor.matmul(bank[h // 2 % 2][rows_, j * P:S], v2_tok[:, j, h * 64:(h + 1) * 64],
                                          st(w_buf, h % 2, j), start=(j == 0), stop=(j == TT - 1),
                                          skip_group_check=True)
                mm.then_inc(sem("o2_mm"), 1)

            for h in range(KH + 2):
                if h < KH:
                    stick_z(h)
                if 0 < h <= KH:
                    stick_c(h - 1)
                if h > 1:
                    stick_values(h - 2)

            pe.wait_ge(sem("o2_lo"), 4)
            pe.wait_ge(sem("cv_lo"), 4)
            with pe.Fori(0, 2) as i:
                for j in range(4):
                    pe.wait_ge(unit_lo, UNIT0["branch2"] + i * 4 + (j + 1))
                    pe.wait_ge(tile_free, TILE0["branch2"] + i * 8 + 2 * j)
                    for half, (h_, l_) in enumerate(((o2_hi, o2_lo), (cv_hi, cv_lo))):
                        for k in range(4):
                            mm = products(j, half * 4 + k, bank[half][:, :], (h_[:, k, :], l_[:, k, :]),
                                          k == 0, k == 3)
                    mm.then_inc(unit_done, 1)
            tiles("o2", gx, DC, 4, peel=1, ready=gx_ready("branch2"))
            def boundary(name, summed):
                for _, h in norm_hooks(name, summed):
                    h()
            boundary("n_post", "o2")
            tiles("up_a", gx, DC, 4, peel=1, ready=gx_ready("post"), hooks=norm_hooks("n_mlp", "post"))
            up = lambda k: (up_hi[:, k, :], up_lo[:, k, :])

            def up_ready(half):
                def f(k):
                    if k % UC == 0:
                        pe.wait_ge(sem("up_lo"), half * HC + k + UC)
                return f
            tiles("down_a", up, HC, 4, peel=1, ready=up_ready(0))
            tiles("up_b", gx, DC, 4)
            tiles("down_b", up, HC, 4, peel=1, ready=up_ready(1))
            pe.wait_ge(sem("p_lo"), 2)
            for j in range(4):
                pe.wait_ge(unit_lo, UNIT0["proj2"] + j + 1)
                pe.wait_ge(tile_free, TILE0["proj2"] + 2 * j)
                for t in range(2):
                    for k in range(2):
                        mm = products(j, t * 2 + k, bank[t][:, :], (p_hi[:, k, :], p_lo[:, k, :]), k == 0, k == 1)
                mm.then_inc(unit_done, 1)
            boundary("n_pmlp", "down")
            tiles("ple2", gx, DC, 4, peel=1, ready=gx_ready("pmlp"), hooks=norm_hooks("n_ple", "pmlp"))

        @block.scalar
        def _(act):
            chain = [0]

            def link(ins):
                chain[0] += 1
                ins.then_inc(sem("act_chain"), 1)
                act.wait_ge(sem("act_chain"), chain[0])

            def round_unit(v, j):
                if isinstance(v, int) and v >= UNITS:
                    return
                if isinstance(v, int):
                    act.wait_ge(unit_raw[j], 16 * (v // RING + 1))
                else:
                    act.wait_ge(unit_raw[j], v[1])
                    v = v[0]
                wait(act, unit_done, v - RING + 1)
                nc.scalar.copy(w_hi[:, j, :], w_raw[:, j, :]).then_inc(unit_hi, 1)

            def ahead(stage, i, per_block, j):
                u = UNIT0[stage] + j + RING - 1
                if isinstance(i, int):
                    round_unit(u + i * per_block, u % RING)
                else:
                    round_unit((i * per_block + u, i * (per_block // RING * 16) + 16 * (u // RING + 1)), u % RING)

            def norm(name, stats=1, width=D):
                act.wait_ge(norm_sem("stat"), norm_count("stat", name, 1))
                if stats == 1:
                    ins = nc.scalar.activation(root_col[:, 0:TT], bank[7][:, 0:TT], ACT.Sqrt, bias=eps_col[:, :],
                                               scale=1.0 / width)
                else:
                    ins = nc.scalar.activation(root_col[:, :], bank[7][:, 0:2 * TT], ACT.Copy, scale=1.0 / width)
                ins.then_inc(norm_sem("root"), 1)

            def next_operand(stage, weight, i, j, m, T, src, src_ready):
                act.wait_ge(src_ready, T)
                act.wait_ge(sem("summed"), sum_count(stage, m + 1))
                nc.scalar.activation(square[:, :], tile_of(src, m), ACT.Square).then_inc(sem("squared"), 1)
                nc.scalar.activation(tile_of(gx_hi, m), tile_of(src, m), ACT.Copy, scale=col_at(weight, m))\
                  .then_inc(sem("gx_hi_done"), 1)

            def residual_stage(stage, weight, per, body=4, peel=0):
                def block_of(i):
                    for j in range(body):
                        for uu in range(per):
                            ahead(stage, i, body * per, j * per + uu)
                        m = i * body + j
                        next_operand(stage, weight, i, j, m, TILE0[stage] + m + 1, x, tile_free)
                blocks(act, 8 // body, block_of, peel)

            def just_round(stage, per_block=4):
                def block_of(i):
                    for j in range(per_block):
                        ahead(stage, i, per_block, j)
                blocks(act, dict(STAGES)[stage] // per_block, block_of)

            def token_evac(stage, g, dst, scale, n_tiles, func, factor, between=None):
                act.wait_ge(*factor)
                for u in range(4):
                    ahead(stage, 0, 4, 4 * g + u)
                    if between:
                        between(4 * g + u)
                act.wait_ge(unit_done, UNIT0[stage] + 4 * g + 4)
                for t in range(n_tiles):
                    nc.scalar.activation(dst[:, t, g * S:(g + 1) * S], bank[2 + t][:, :], func,
                                         scale=scale[:, t:t + 1]).then_inc(sem("token_free"), 1)

            def ffn(name, norm_name, weight, out_peel=0):
                def block_of(i):
                    for j in range(2):
                        c = i * 2 + j
                        ahead(f"{name}_in", i, 4, 2 * j)
                        if first(i) and j == 0:
                            norm(norm_name)
                        act.wait_ge(tile_free, TILE0[f"{name}_in"] + c * 2 + 1)
                        nc.scalar.activation(ff_silu[:, :], ff_gate[:, :], ACT.Silu).then_inc(sem("ffn_silu"), 1)
                        ahead(f"{name}_in", i, 4, 2 * j + 1)
                        act.wait_ge(sem("ffn_act"), ffn_count(name, c + 1))
                        nc.scalar.copy(tile_of(ff_hi, c), ff_act[:, :]).then_inc(sem("ffn_act_hi"), 1)
                blocks(act, FC // 2, block_of, peel=1)
                residual_stage(f"{name}_out", weight, 3) if name == "ffn1" else final_residual()

            def final_residual():
                def block_of(i):
                    for j in range(4):
                        for uu in range(3):
                            ahead("ffn2_out", i, 12, 3 * j + uu)
                        m = i * 4 + j
                        act.wait_ge(tile_free, TILE0["ffn2_out"] + m + 1)
                        act.wait_ge(sem("summed"), sum_count("ffn2_out", m + 1))
                        nc.scalar.activation(square[:, :], tile_of(x, m), ACT.Square)\
                          .then_inc(sem("squared"), 1)
                        act.wait_ge(sem("xw_ready"), m + 1)
                        nc.scalar.activation(tile_of(gx_hi, m), tile_of(x, m), ACT.Copy,
                                             scale=col_at("g_pre_mix_2", m)).then_inc(sem("gx_hi_done"), 1)
                        nc.scalar.activation(square2[:, :], tile_of(x, m), ACT.Square)\
                          .then_inc(sem("squared2"), 1)
                blocks(act, 2, block_of)

            act.dma_start(x[:, :, :], xT.rearrange("(m p) s -> p m s", p=P)).then_inc(sem("x_in"), 16)
            for dst, src in ((consts[:, :], consts_d), (cols[:, :], cols_d), (wdt[:, :, :], wdt_d),
                             (rows[:, :], bass.AP(rows_d.tensor, 0, [[0, P], [1, NROWS]])),
                             (relb[0:32, :], relb_d), (onehot[0:32, :], onehot_d), (pen[0:AH, :], pen_d)):
                act.dma_start(dst, src).then_inc(sem("setup_in"), 16)
            for v in range(RING - 1):
                round_unit(v, v)
            act.wait_ge(sem("setup_in"), 16 * 7)
            act.wait_ge(sem("x_in"), 16)
            for m in range(DC):
                act.wait_ge(sem("summed"), sum_count("load", m + 1))
                nc.scalar.activation(square[:, :], x[:, m, :], ACT.Square).then_inc(sem("squared"), 1)
                nc.scalar.activation(gx_hi[:, m, :], x[:, m, :], ACT.Copy, scale=col("norm_ffn1_w", m))\
                  .then_inc(sem("gx_hi_done"), 1)
            act.wait_ge(sem("brow_ready"), 2)
            act.dma_start(bias_r, brow[0:AH, :]).then_inc(sem("brow_out"), 16)
            act.wait_ge(sem("brow_out"), 16)

            ffn("ffn1", "n_ffn1", "norm_mix_w")

            def xbc(x_part):
                def block_of(i):
                    for j in range(4):
                        c = i * 4 + j
                        ahead("xbc", i, 4, j)
                        if first(i) and j == 0:
                            norm("n_mix")
                        act.wait_ge(sem("xbc_conv"), c * 4 + 4)
                        dst = tile_of(xs_T, c) if x_part else tile_of(bc, c - 8)
                        nc.scalar.activation(dst, conv_acc[:, :], ACT.Silu).then_inc(sem("xbc_silu"), 1)
                return block_of
            for i in range(2):
                xbc(True)(i)
            with act.Fori(2, 4) as i:
                xbc(False)(i)
            nc.scalar.copy(wdt_hi[:, :, :], wdt[:, :, :]).then_inc(sem("wdt_hi"), 1)
            z_factor = (norm_sem("col"), norm_count("col", "n_mix", 1))
            token_evac("z", 0, z_tok, rstd_col, TT, ACT.Silu, z_factor)
            act.wait_ge(sem("dt_clamped"), 1)
            link(nc.scalar.activation(dt_exp[:, :, :], dt_exp[:, :, :], ACT.Exp))
            nc.scalar.activation(dt_ln[:, :, :], dt_exp[:, :, :], ACT.Ln, bias=1.0).then_inc(sem("dt_lned"), 1)
            nc.scalar.activation(a_row[:, :], rows[:, ROWS["a_log"]:ROWS["a_log"] + SH], ACT.Exp)\
              .then_inc(sem("a_exp"), 1)
            token_evac("z", 1, z_tok, rstd_col, TT, ACT.Silu, z_factor)
            act.wait_ge(sem("cum_read"), 1)
            nc.scalar.activation(ecum[:, :, :], cum[:, :, :], ACT.Exp).then_inc(sem("decay_exp"), 1)
            nc.scalar.activation(e_end[:, :, :], to_end[:, :, :], ACT.Exp).then_inc(sem("decay_exp"), 1)
            nc.scalar.activation(c_dec[:, :, :], c_dec[:, :, :], ACT.Exp).then_inc(sem("decay_exp"), 1)
            for n in range(TT * SG + 1):
                if n < TT * SG:
                    t, g, b = n // SG, n % SG, n % 2
                    if n % 2 == 1:
                        ahead("q", 0, 4, n // 2)
                    act.wait_ge(sem("cell_b"), n + 1)
                    wait(act, sem("cell_m"), n - 1)
                    for r in range(GH):
                        h = g * GH + r
                        ins = nc.scalar.activation(seg[:, b, r, :], bank[2 + b][:, r * P:(r + 1) * P], ACT.Relu,
                                                   bias=cum[:, t, h:h + 1], scale=-1.0)
                    link(ins)
                    nc.scalar.activation(decay[:, b, :, :], seg[:, b, :, :], ACT.Exp, scale=-1.0)\
                      .then_inc(sem("decayed"), 1)
                if n > 0:
                    t, g = (n - 1) // SG, (n - 1) % SG
                    act.wait_ge(sem("cell_done"), n)
                    wait(act, sem("y_squared"), n - 1)
                    nc.scalar.activation(ysq_tmp[:, :], z_tok[:, t, g * 256:(g + 1) * 256], ACT.Square,
                                         accum_out=y_sq[:, n - 1:n]).then_inc(sem("y_squared"), 1)
            act.wait_ge(sem("y_squared"), TT * SG)
            nc.scalar.activation(y_root[:, :], y_sq[:, :], ACT.Sqrt, bias=eps_col[:, :], scale=1.0 / 256)\
              .then_inc(sem("y_rooted"), 1)
            just_round("k")
            v_factor = (norm_sem("col"), norm_count("col", "n_mix", 1))

            def round_y(j):
                act.wait_ge(sem("ys_turned"), j + 1)
                nc.scalar.activation(ys_hi[:, j, :], bank[6 + j % 2][:, :], ACT.Copy,
                                     scale=col("ssd_norm_w", j)).then_inc(sem("ys_hi"), 1)
            for g in range(2):
                token_evac("v", g, v_tok, rstd_col, TT, ACT.Copy, v_factor, between=round_y)
            act.wait_ge(sem("lam_dots"), 2)
            nc.scalar.activation(lam[:, 2:4], lam[:, 0:2], ACT.Exp).then_inc(sem("lam_exp"), 1)
            act.wait_ge(unit_done, UNIT0["mix_ssd"])

            def load_bias(h):
                act.dma_start(bflip[h % 2][:, :], bass.AP(bias_r.tensor, h * (BIAS_W + 1), [[1, P], [1, S]]))\
                   .then_inc(sem(f"bias_in{h % 2}"), 16)

            def copy_bias(h):
                act.wait_ge(sem("bias_flip"), h + 1)
                if h >= 2:
                    act.wait_ge(sem("score_read"), 8 * (h - 1))
                nc.scalar.copy(bias_h[:, h % 2, :], bank[1][:, :]).then_inc(sem("bias_ready"), 1)

            load_bias(0)
            load_bias(1)
            copy_bias(0)

            def exps(h, n0, n1):
                for n in range(n0, n1):
                    i, c = n // 2, n % 2
                    act.wait_ge(sem("score_read"), h * 8 + n + 1)
                    seg = prob[:, h % 2, c, P * (i * (i + 1) // 2):P * ((i + 1) * (i + 2) // 2)]
                    nc.scalar.activation(seg, seg, ACT.Exp, bias=amin[:, h % 2, c * 4 + i:c * 4 + i + 1], scale=-1.0,
                                         accum_out=rsum[:, h % 2, c * 4 + i:c * 4 + i + 1])\
                      .then_inc(sem("exped"), 1)

            for h in range(AH + 1):
                if h < AH:
                    exps(h, 0, 3)
                if h + 1 < AH:
                    copy_bias(h + 1)
                if h > 0:
                    act.wait_ge(sem("turned"), h)
                    wait(act, sem("o_mm"), h - 1)
                    nc.scalar.copy(w_T[:, 0:S], bank[5][:, :]).then_inc(sem("wT_act"), 1)
                if h + 2 < AH:
                    load_bias(h + 2)
                if h < AH:
                    ahead("mix_ssd", 0, 4, h)
                    exps(h, 3, 8)
                if h > 0:
                    act.wait_ge(sem("o_copied"), h)
                    wait(act, sem("o_stat"), h - 1)
                    nc.scalar.activation(o_sq[:, :], o_un[:, h - 1, :], ACT.Square).then_inc(sem("o_squared"), 1)
            act.wait_ge(sem("o_stat"), AH)
            nc.scalar.activation(o_root[:, :], bank[7][:, 384:384 + TT * AH], ACT.Sqrt, bias=eps_col[:, :], scale=1.0 / AV)\
              .then_inc(sem("o_rooted"), 1)
            for h in range(AH):
                act.wait_ge(sem("o_nrmd"), h + 1)
                nc.scalar.copy(o_hi[:, h, :], o_nrm[:, h % 2, :]).then_inc(sem("o_hi"), 1)
            residual_stage("mix_attn", "norm_cross_w", 1)
            act.dma_start(m_T[:, :, :], memT.rearrange("(m p) s -> p m s", p=P)).then_inc(sem("m_in"), 16)
            act.wait_ge(sem("m_in"), 16)
            for m in range(DC):
                act.wait_ge(sem("m_sum"), m + 1)
                nc.scalar.activation(square[:, 0:ML], m_T[:, m, :], ACT.Square).then_inc(sem("m_square"), 1)
                nc.scalar.activation(m_hi[:, m, :], m_T[:, m, :], ACT.Copy, scale=col("norm_mem_w", m))\
                  .then_inc(sem("m_hi"), 1)
            act.wait_ge(sem("m_stat"), 1)
            nc.scalar.activation(m_root[:, :], bank[6][:, 0:MT], ACT.Sqrt, bias=eps_col[:, :], scale=1.0 / D)\
              .then_inc(sem("m_root"), 1)
            just_round("ck")
            act.wait_ge(sem("m_col"), 1)
            for g in range(2):
                token_evac("cv", g, vx, m_rstd, MT, ACT.Copy, (sem("m_col"), 1))
            for j in range(8):
                ahead("cq", 0, 4, j)
                if j == 0:
                    norm("n_cross")
            for n in range(XH * TT + 2):
                if n < XH * TT:
                    act.wait_ge(sem("x_min"), n + 1)
                    wait(act, sem("x_turned"), n - 3)
                    nc.scalar.activation(px[:, n % 4, :], bank[2 + n % 3][:, 0:ML], ACT.Exp,
                                         bias=xmin[:, n:n + 1], scale=-1.0, accum_out=xsum[:, n:n + 1])\
                      .then_inc(sem("x_exp"), 1)
                if n > 1 and (n - 2) % TT == TT - 1:
                    for e in range(2):
                        c = 2 * ((n - 2) // TT) + e
                        act.wait_ge(sem("ox_mm"), c + 1)
                        nc.scalar.copy(ox_hi[:, c, :], bank[7 - 6 * e][:, :]).then_inc(sem("ox_hi"), 1)
            residual_stage("co", "norm_ffn2_w", 1)
            ffn("ffn2", "n_ffn2", None)
            ahead("qk2", 0, 4, 0)
            norm("n_fin", 2)
            act.wait_ge(sem("n_fin_var"), 1)
            nc.scalar.activation(fin[:, 16:20], fin[:, 0:4], ACT.Sqrt, bias=eps_col[:, :])\
              .then_inc(norm_sem("root"), 1)
            nc.scalar.activation(fin[:, 20:24], fin[:, 8:12], ACT.Sqrt).then_inc(norm_sem("root"), 1)
            for j in range(1, 8):
                ahead("qk2", 0, 4, j)
            token_evac("v2", 0, v2_tok, rstd_col, TT, ACT.Copy, (norm_sem("col"), norm_count("col", "n_fin", 1)))
            for c in range(4):
                for j in range(3):
                    ahead("conv2", 0, 12, 3 * c + j)
                act.wait_ge(sem("cv_out"), c + 1)
                nc.scalar.copy(cv_hi[:, c, :], cacc[:, :]).then_inc(sem("cv_hi"), 1)

            def gate_block(i):
                for j in range(4):
                    c = i * 4 + j
                    ahead("gates2", i, 4, j)
                    act.wait_ge(tile_free, TILE0["gates2"] + c + 1)
                    nc.scalar.activation(tile_of(gates, c), gate_t[:, :], ACT.Sigmoid,
                                         bias=col_at("b_gate_2", c)).then_inc(sem("gate_sig"), 1)
            blocks(act, 4, gate_block)
            for h in range(KH + 2):
                if h < KH:
                    act.wait_ge(sem("z_clamped"), 3 * (h + 1))
                    link(nc.scalar.activation(sz_buf[h % 2][:, :], sz_buf[h % 2][:, :], ACT.Exp))
                    nc.scalar.activation(sz_buf[h % 2][:, :], sz_buf[h % 2][:, :], ACT.Ln, bias=1.0)\
                      .then_inc(sem("sp_lned"), 1)
                if 0 < h <= KH:
                    act.wait_ge(sem("c_mm"), h)
                    wait(act, sem("o2_mm"), h - 2)
                    for bk in range(3):
                        n = S if bk < 2 else 2 * P
                        ins = nc.scalar.activation(w_buf[(h - 1) % 2][:, bk * S:bk * S + n], bank[5 + bk][:, 0:n],
                                                   ACT.Exp)
                    ins.then_inc(sem("w_exp"), 1)
                if h > 1 and h % 2 == 1:
                    act.wait_ge(sem("o2_mm"), h - 1)
                    c = (h - 2) // 2
                    nc.scalar.copy(o2_hi[:, c, :], bank[c % 2][:, :]).then_inc(sem("o2_hi"), 1)
            act.wait_ge(sem("sp_masked"), KH)
            with act.Fori(0, 2) as i:
                for j in range(4):
                    ahead("branch2", i, 4, j)
                    c = i * 4 + j
                    act.wait_ge(sem("mixed"), c + 1)
                    nc.scalar.copy(tile_of(gx_hi, c), br_m[:, :]).then_inc(sem("gx_hi_done"), 1)

            def o2_block(i):
                for j in range(4):
                    ahead("o2", i, 4, j)
                    m = i * 4 + j
                    act.wait_ge(tile_free, TILE0["o2"] + m + 1)
                    act.wait_ge(sem("summed"), sum_count("o2", m + 1))
                    nc.scalar.activation(square[:, :], tile_of(y_o2, m), ACT.Square)\
                      .then_inc(sem("squared"), 1)
            blocks(act, 2, o2_block)
            def post(name, weight):
                for m in range(DC):
                    act.wait_ge(sem(f"{name}_x"), m + 1)
                    act.wait_ge(sem("summed"), sum_count(name, m + 1))
                    nc.scalar.activation(gx_hi[:, m, :], x[:, m, :], ACT.Copy, scale=col(weight, m))\
                      .then_inc(sem("gx_hi_done"), 1)
                    nc.scalar.activation(square[:, :], x[:, m, :], ACT.Square).then_inc(sem("squared"), 1)
            norm("n_post")
            post("post", "g_pre_mlp_2")

            def up_stage(stage, half):
                def block_of(i):
                    for j in range(4):
                        c = i * 4 + j
                        ahead(stage, i, 4, j)
                        if first(i) and j == 0 and half == 0:
                            norm("n_mlp")
                        act.wait_ge(sem("up_act"), half * HC + c + 1)
                        nc.scalar.copy(tile_of(up_hi, c), up_a[:, :]).then_inc(sem("up_hi"), 1)
                blocks(act, 4, block_of, peel=1 - half)
            up_stage("up_a", 0)
            just_round("down_a", 8)
            up_stage("up_b", 1)

            def down_block(i):
                for j in range(4):
                    m = i * 4 + j
                    ahead("down_b", i, 8, 2 * j)
                    ahead("down_b", i, 8, 2 * j + 1)
                    act.wait_ge(tile_free, TILE0["down_b"] + m + 1)
                    act.wait_ge(sem("summed"), sum_count("down", m + 1))
                    nc.scalar.activation(square[:, :], tile_of(f_acc, m), ACT.Square)\
                      .then_inc(sem("squared"), 1)
            blocks(act, 2, down_block)
            act.dma_start(p_T[:, :, :], pT.rearrange("(m p) s -> p m s", p=P)).then_inc(sem("p_in"), 16)
            act.wait_ge(sem("p_in"), 16)
            for k in range(2):
                nc.scalar.copy(p_hi[:, k, :], p_T[:, k, :]).then_inc(sem("p_hi"), 1)
            for j in range(4):
                ahead("proj2", 0, 4, j)
            norm("n_pmlp")
            post("pmlp", "g_ple_2")
            for m in range(DC):
                ahead("ple2", 0, 4, m)
                if m == 0:
                    norm("n_ple")
                act.wait_ge(tile_free, TILE0["ple2"] + m + 1)
                nc.scalar.activation(ple_g[:, :], ple_t[:, :], ACT.Sigmoid).then_inc(sem("ple_sig"), 1)

        @block.vector
        def _(dve):
            chain = [0]

            def link(ins):
                chain[0] += 1
                ins.then_inc(sem("dve_chain"), 1)
                dve.wait_ge(sem("dve_chain"), chain[0])

            def norm(name):
                dve.wait_ge(norm_sem("root"), norm_count("root", name, 1))
                nc.vector.reciprocal(rstd_col[:, :], root_col[:, 0:TT]).then_inc(norm_sem("col"), 1)
                dve.wait_ge(norm_sem("row"), norm_count("row", name, 1))
                nc.vector.tensor_copy(rstd_row[:, :], bank[7][:, :]).then_inc(norm_sem("ready"), 1)
                dve.wait_ge(norm_sem("ready"), norm_count("ready", name, 1))

            def start_sums():
                nc.vector.memset(sumsq[:, :], 0.0).then_inc(sem("summed"), 1)

            def add_square(stage, m):
                dve.wait_ge(sem("squared"), square_count(stage, m + 1))
                dve.wait_ge(sem("summed"), sum_count(stage, m + 1))
                nc.vector.tensor_tensor(sumsq[:, :], sumsq[:, :], square[:, :], ALU.add).then_inc(sem("summed"), 1)

            def add_square2(m):
                dve.wait_ge(sem("squared2"), m + 1)
                dve.wait_ge(sem("summed2"), m + 1)
                nc.vector.tensor_tensor(sumsq2[:, :], sumsq2[:, :], square2[:, :], ALU.add)\
                  .then_inc(sem("summed2"), 1)

            def split_lo(stage, weight, m, src):
                dve.wait_ge(sem("gx_hi_done"), gx_count(stage, m + 1))
                nc.vector.scalar_tensor_tensor(out=tile_of(gx_lo, m), in0=tile_of(src, m),
                                               scalar=col_at(weight, m), in1=tile_of(gx_hi, m).bitcast(F32),
                                               op0=ALU.mult, op1=ALU.subtract).then_inc(sem("gx_lo_done"), 1)

            def residual_stage(stage, weight, per, alpha, norm_name, body=4):
                start_sums()

                def block_of(i):
                    for j in range(body):
                        m = i * body + j
                        dve.wait_ge(unit_done, UNIT0[stage] + m * per + per)
                        nc.vector.scalar_tensor_tensor(out=tile_of(x, m), in0=bank[j % 2][:, :], scalar=alpha,
                                                       in1=tile_of(x, m), op0=ALU.mult, op1=ALU.add)\
                          .then_inc(tile_free, 1)
                        add_square(stage, m)
                        split_lo(stage, weight, m, x)
                blocks(dve, 8 // body, block_of)

            def scaled_tiles(stage, dst, count, scale=None, body=4, row=None, first=0):
                def block_of(i):
                    for j in range(body):
                        c = i * body + j
                        dve.wait_ge(unit_done, UNIT0[stage] + first + c + 1)
                        src = bank[j % 2][:, 0:(row or rstd_row).shape[1]]
                        r = (row or rstd_row)[:, :]
                        if scale is None:
                            ins = nc.vector.tensor_tensor(tile_of(dst, c), src, r, ALU.mult)
                        else:
                            ins = nc.vector.scalar_tensor_tensor(out=tile_of(dst, c), in0=src, scalar=scale, in1=r,
                                                                 op0=ALU.mult, op1=ALU.mult)
                        ins.then_inc(tile_free, 1)
                blocks(dve, count // body, block_of)

            def ffn(name, norm_name, weight):
                def block_of(i):
                    for j in range(2):
                        c = i * 2 + j
                        T, U = TILE0[f"{name}_in"] + 2 * c, UNIT0[f"{name}_in"] + 2 * c
                        if first(i) and j == 0:
                            norm(norm_name)
                        dve.wait_ge(unit_done, U + 1)
                        nc.vector.tensor_tensor(ff_gate[:, :], bank[0][:, :], rstd_row[:, :], ALU.mult)\
                          .then_inc(tile_free, 1)
                        dve.wait_ge(unit_done, U + 2)
                        nc.vector.tensor_tensor(ff_up[:, :], bank[1][:, :], rstd_row[:, :], ALU.mult)\
                          .then_inc(tile_free, 1)
                        dve.wait_ge(sem("ffn_silu"), ffn_count(name, c + 1))
                        dve.wait_ge(tile_free, T + 2)
                        nc.vector.tensor_tensor(ff_act[:, :], ff_silu[:, :], ff_up[:, :], ALU.mult)\
                          .then_inc(sem("ffn_act"), 1)
                        dve.wait_ge(sem("ffn_act_hi"), ffn_count(name, c + 1))
                        nc.vector.tensor_tensor(tile_of(ff_lo, c), ff_act[:, :],
                                                tile_of(ff_hi, c).bitcast(F32), ALU.subtract)\
                          .then_inc(sem("ffn_act_lo"), 1)
                blocks(dve, FC // 2, block_of, peel=1)
                if name == "ffn1":
                    residual_stage("ffn1_out", weight, 3, 0.5, "n_mix")
                    return
                start_sums()
                nc.vector.memset(sumsq2[:, :], 0.0).then_inc(sem("summed2"), 1)

                def out_block(i):
                    for j in range(4):
                        m = i * 4 + j
                        xm = tile_of(x, m)
                        dve.wait_ge(unit_done, UNIT0["ffn2_out"] + m * 3 + 3)
                        nc.vector.scalar_tensor_tensor(out=xm, in0=bank[j % 2][:, :], scalar=0.5, in1=xm,
                                                       op0=ALU.mult, op1=ALU.add).then_inc(tile_free, 1)
                        add_square("ffn2_out", m)
                        nc.vector.tensor_scalar(xm, xm, col_at("norm_final_w", m), None, ALU.mult)\
                          .then_inc(sem("xw_ready"), 1)
                        add_square2(m)
                        split_lo("ffn2_out", "g_pre_mix_2", m, x)
                blocks(dve, 2, out_block)

            def x_lo(hd):
                for e in range(2):
                    c = 2 * hd + e
                    dve.wait_ge(sem("ox_hi"), c + 1)
                    nc.vector.tensor_tensor(ox_lo[:, c, :], bank[7 - 6 * e][:, :], ox_hi[:, c, :].bitcast(F32), ALU.subtract)\
                      .then_inc(sem("ox_lo"), 1)

            nc.vector.memset(eps_col[:, :], EPS).then_inc(sem("eps_set"), 1)
            dve.wait_ge(sem("eps_set"), 1)
            dve.wait_ge(sem("setup_in"), 16 * 7)
            dve.wait_ge(sem("x_in"), 16)
            start_sums()
            for m in range(DC):
                add_square("load", m)
                split_lo("load", "norm_ffn1_w", m, x)
            dve.wait_ge(sem("brow_sum"), 1)
            nc.vector.tensor_tensor(brow[0:AH, 0:S], pen[0:AH, 0:S], bank[2][0:AH, :], ALU.subtract)\
              .then_inc(sem("brow_ready"), 1)
            nc.vector.tensor_tensor(brow[0:AH, S:S + P], pen[0:AH, S:S + P], bank[3][0:AH, 0:P], ALU.subtract)\
              .then_inc(sem("brow_ready"), 1)

            ffn("ffn1", "n_ffn1", "norm_mix_w")

            nc.vector.memset(conv_in[:, 0:3], 0.0).then_inc(sem("conv_pad"), 1)
            dve.wait_ge(sem("conv_pad"), 1)

            def conv_block(i):
                for j in range(4):
                    c = i * 4 + j
                    if first(i) and j == 0:
                        norm("n_mix")
                    dve.wait_ge(unit_done, UNIT0["xbc"] + c + 1)
                    wait(dve, sem("xbc_conv"), c * 4)
                    nc.vector.tensor_tensor(conv_in[:, 3:3 + S], bank[j % 2][:, :], rstd_row[:, :], ALU.mult)\
                      .then_inc(tile_free, 1)
                    dve.wait_ge(tile_free, TILE0["xbc"] + c + 1)
                    wait(dve, sem("xbc_silu"), c)
                    nc.vector.tensor_scalar(conv_acc[:, :], conv_in[:, 0:S], col_at("conv_w", c),
                                            col_at("conv_b", c), ALU.mult, ALU.add).then_inc(sem("xbc_conv"), 1)
                    for k in range(1, 4):
                        dve.wait_ge(sem("xbc_conv"), c * 4 + k)
                        nc.vector.scalar_tensor_tensor(out=conv_acc[:, :], in0=conv_in[:, k:k + S],
                                                       scalar=col_at("conv_w", c + 16 * k), in1=conv_acc[:, :],
                                                       op0=ALU.mult, op1=ALU.add).then_inc(sem("xbc_conv"), 1)
            blocks(dve, 4, conv_block, peel=1)
            dve.wait_ge(sem("wdt_hi"), 1)
            nc.vector.tensor_tensor(wdt_lo[:, :, :], wdt[:, :, :], wdt_hi[:, :, :].bitcast(F32), ALU.subtract)\
              .then_inc(sem("wdt_lo"), 1)
            dve.wait_ge(sem("dt_mm"), 1)
            nc.vector.tensor_copy(dt_T[0:SH, :], bank[6][0:SH, :]).then_inc(sem("dt_copied"), 1)
            dve.wait_ge(sem("dt_turned"), 1)
            bias = rows[:, ROWS["dt_bias"]:ROWS["dt_bias"] + SH]
            for t in range(TT):
                ins = nc.vector.scalar_tensor_tensor(out=dt_pre[:, t, :], in0=bank[6][:, t * SH:(t + 1) * SH],
                                                     scalar=rstd_col[:, t:t + 1], in1=bias,
                                                     op0=ALU.mult, op1=ALU.add)
            link(ins)
            nc.vector.tensor_scalar(dt_exp[:, :, :], dt_pre[:, :, :], 40.0, None, ALU.min)\
              .then_inc(sem("dt_clamped"), 1)

            def copy_x(j):
                dve.wait_ge(sem("xs_turned"), j + 1)
                nc.vector.tensor_copy(xs_tok[:, :, j * P:(j + 1) * P],
                                      bank[j % 2][:, :].rearrange("p (t c) -> p t c", t=TT))\
                  .then_inc(sem("xs_copied"), 1)
            for j in range(5):
                copy_x(j)
            dve.wait_ge(sem("dt_lned"), 1)
            dve.wait_ge(sem("a_exp"), 1)
            link(nc.vector.tensor_tensor(dt[:, :, :], dt_ln[:, :, :], dt_pre[:, :, :], ALU.max))
            nc.vector.scalar_tensor_tensor(out=la[:, :, :], in0=dt[:, :, :], scalar=-1.0,
                                           in1=a_row[:, :].unsqueeze(1).to_broadcast([P, TT, SH]),
                                           op0=ALU.mult, op1=ALU.mult).then_inc(sem("la_ready"), 1)
            for j in range(5, 8):
                copy_x(j)
            dve.wait_ge(sem("cum_mm"), 1)
            r3 = lambda ap: ap.rearrange("p (t h) -> p t h", t=TT)
            link(nc.vector.tensor_copy(cum[:, :, :], r3(bank[7][:, 0:TT * SH])))
            nc.vector.tensor_copy(c_dec[:, :, :], r3(bank[7][:, TT * SH:2 * TT * SH]))
            nc.vector.tensor_tensor(to_end[:, :, :], r3(bank[7][:, TT * SH:2 * TT * SH]), cum[:, :, :],
                                    ALU.subtract).then_inc(sem("cum_read"), 1)
            dve.wait_ge(sem("decay_exp"), 3)

            def heads(ap):
                return ap.unsqueeze(2).to_broadcast([P, GH, SHD])

            def cell(buf, t, g):
                return buf[:, t, g * 256:(g + 1) * 256].rearrange("p (r c) -> p r c", r=GH)

            def ssd_front(n):
                t, g, b = n // SG, n % SG, n % 2
                hs = slice(g * GH, (g + 1) * GH)
                dve.wait_ge(sem("cell_a"), n + 1)
                wait(dve, sem("cell_y"), n - 1)
                nc.vector.tensor_tensor(cb_m[:, b, :], bank[1][:, 0:P], tri_le, ALU.mult)\
                  .then_inc(sem("cell_a_read"), 1)
                nc.vector.tensor_copy(b_tok[:, b, :], bank[1][:, P:2 * P]).then_inc(sem("cell_a_read"), 1)
                link(nc.vector.tensor_tensor(xdt[:, b, :, :], cell(xs_tok, t, g), heads(dt[:, t, hs]), ALU.mult))
                nc.vector.tensor_tensor(xdte[:, b, :, :], xdt[:, b, :, :], heads(e_end[:, t, hs]), ALU.mult)
                dve.wait_ge(sem("decayed"), n + 1)
                nc.vector.tensor_tensor(mix_m[:, b, :, :], decay[:, b, :, :],
                                        cb_m[:, b, :].unsqueeze(1).to_broadcast([P, GH, P]),
                                        ALU.mult).then_inc(sem("cell_m"), 1)

            def ssd_back(n):
                t, g, b = n // SG, n % SG, n % 2
                hs = slice(g * GH, (g + 1) * GH)
                r4 = lambda ap: ap.rearrange("p (r c) -> p r c", r=GH)
                wait(dve, sem("cell_done"), n)
                skip = rows[:, ROWS["d_skip"] + g * GH:ROWS["d_skip"] + (g + 1) * GH]
                nc.vector.tensor_tensor(y_a[:, :, :], cell(xs_tok, t, g), heads(skip), ALU.mult)\
                  .then_inc(sem("y_step"), 1)
                dve.wait_ge(sem("cell_y"), n + 1)
                dve.wait_ge(sem("y_step"), 4 * n + 1)
                nc.vector.tensor_tensor(y_b[:, :, :], r4(bank[4 + b][:, 0:256]), y_a[:, :, :], ALU.add)\
                  .then_inc(sem("y_step"), 1)
                if t > 0:
                    nc.vector.tensor_tensor(y_c[:, :, :], r4(bank[4 + b][:, 256:512]), heads(ecum[:, t, hs]),
                                            ALU.mult).then_inc(sem("y_step"), 1)
                    dve.wait_ge(sem("y_step"), 4 * n + 3)
                    nc.vector.tensor_tensor(y_b[:, :, :], y_b[:, :, :], y_c[:, :, :], ALU.add)\
                      .then_inc(sem("y_step"), 1)
                    link(nc.vector.tensor_tensor(state[:, g, :, :], state[:, g, :, :], heads(c_dec[:, t, hs]),
                                                 ALU.mult))
                    nc.vector.tensor_tensor(state[:, g, :, :], r4(bank[6 + b][:, 0:256]), state[:, g, :, :],
                                            ALU.add)
                else:
                    nc.vector.tensor_copy(state[:, g, :, :], r4(bank[6 + b][:, 0:256])).then_inc(sem("y_step"), 2)
                dve.wait_ge(sem("y_step"), 4 * n + 4)
                z = cell(z_tok, t, g)
                nc.vector.tensor_tensor(z, z, y_b[:, :, :], ALU.mult).then_inc(sem("cell_done"), 1)

            dve.wait_ge(sem("xs_copied"), 8)
            for n in range(TT * SG + 1):
                if n < TT * SG:
                    ssd_front(n)
                if n > 0:
                    ssd_back(n - 1)
                if n % 2 == 1:
                    c = n // 2
                    dve.wait_ge(unit_done, UNIT0["q"] + c + 1)
                    nc.vector.scalar_tensor_tensor(out=q_T[:, c, :], in0=bank[0][:, :], scalar=-0.125,
                                                   in1=rstd_row[:, :], op0=ALU.mult, op1=ALU.mult)\
                      .then_inc(tile_free, 1)
            dve.wait_ge(sem("y_rooted"), 1)
            link(nc.vector.reciprocal(y_rstd[:, :], y_root[:, :]))
            for n in range(TT * SG):
                t, g = n // SG, n % SG
                z = z_tok[:, t, g * 256:(g + 1) * 256]
                nc.vector.tensor_scalar(z, z, y_rstd[:, n:n + 1], None, ALU.mult).then_inc(sem("y_norm"), 1)
            scaled_tiles("k", k_T, 8)
            for j in range(DC):
                dve.wait_ge(sem("ys_hi"), j + 1)
                nc.vector.scalar_tensor_tensor(out=ys_lo[:, j, :], in0=bank[6 + j % 2][:, :],
                                               scalar=col("ssd_norm_w", j), in1=ys_hi[:, j, :].bitcast(F32),
                                               op0=ALU.mult, op1=ALU.subtract).then_inc(sem("ys_lo"), 1)
            dve.wait_ge(unit_done, UNIT0["mix_ssd"])
            r = lambda n: rows[:, ROWS[n]:ROWS[n] + SHD]
            for n, (a, b) in enumerate((("lambda_q1", "lambda_k1"), ("lambda_q2", "lambda_k2"))):
                nc.vector.tensor_tensor_reduce(lam_tmp[:, :], r(a), r(b), 1.0, 0.0, ALU.mult, ALU.add,
                                               lam[:, n:n + 1]).then_inc(sem("lam_dots"), 1)
                dve.wait_ge(sem("lam_dots"), n + 1)
            link(nc.vector.tensor_scalar(subln[:, :], col("subln_w", 0), 1.0 - LAMBDA_INIT, None, ALU.mult))
            dve.wait_ge(sem("lam_exp"), 1)
            link(nc.vector.tensor_tensor(lam[:, 4:5], lam[:, 3:4], lam[:, 2:3], ALU.subtract))
            link(nc.vector.tensor_scalar(lam[:, 5:6], lam[:, 4:5], -LAMBDA_INIT, None, ALU.add))

            def combine(h):
                b = h % 2
                dve.wait_ge(sem("exped"), 8 * (h + 1))
                link(nc.vector.reciprocal(rrec[:, b, :], rsum[:, b, :]))
                link(nc.vector.tensor_scalar(rrec[:, b, 4:8], rrec[:, b, 4:8], lam[:, 5:6], None, ALU.mult))
                for i in range(TT):
                    a, e = P * (i * (i + 1) // 2), P * ((i + 1) * (i + 2) // 2)
                    p0, p1 = prob[:, b, 0, a:e], prob[:, b, 1, a:e]
                    ins = nc.vector.tensor_scalar(p0, p0, rrec[:, b, i:i + 1], None, ALU.mult)
                link(ins)
                for i in range(TT):
                    a, e = P * (i * (i + 1) // 2), P * ((i + 1) * (i + 2) // 2)
                    p0, p1 = prob[:, b, 0, a:e], prob[:, b, 1, a:e]
                    ins = nc.vector.scalar_tensor_tensor(out=p0, in0=p1, scalar=rrec[:, b, 4 + i:5 + i], in1=p0,
                                                         op0=ALU.mult, op1=ALU.add)
                ins.then_inc(sem("diffed"), 1)

            def biased(h, n):
                i, c = n // 2, n % 2
                w = (i + 1) * P
                dve.wait_ge(sem("score"), 8 * h + n + 1)
                nc.vector.tensor_tensor_reduce(
                    prob[:, h % 2, c, P * (i * (i + 1) // 2):P * ((i + 1) * (i + 2) // 2)],
                    bank[2 + (8 * h + n) % 3][:, 0:w], bias_h[:, h % 2, S - w:S], 1.0, -NEG, ALU.add, ALU.min,
                    amin[:, h % 2, c * 4 + i:c * 4 + i + 1]).then_inc(sem("score_read"), 1)

            for h in range(AH + 1):
                if h < AH:
                    dve.wait_ge(sem("bias_ready"), h + 1)
                    if h >= 2:
                        dve.wait_ge(sem("turned"), h - 1)
                    for n in range(3):
                        biased(h, n)
                if h > 0:
                    combine(h - 1)
                if h < AH:
                    for n in range(3, 8):
                        biased(h, n)
                if h > 0:
                    dve.wait_ge(sem("turned"), h)
                    wait(dve, sem("o_mm"), h - 1)
                    nc.vector.tensor_copy(w_T[:, S:S + 384], bank[6][:, 0:384]).then_inc(sem("wT_dve"), 1)
                    nc.vector.tensor_copy(w_T[:, S + 384:NB], bank[7][:, 0:384]).then_inc(sem("wT_dve"), 1)
                    dve.wait_ge(sem("o_mm"), h)
                    nc.vector.tensor_copy(o_un[:, h - 1, :], bank[0][:, :]).then_inc(sem("o_copied"), 1)
                if h < AH:
                    dve.wait_ge(unit_done, UNIT0["mix_ssd"] + h + 1)
                    nc.vector.tensor_tensor(x[:, h, :], bank[1][:, :], x[:, h, :], ALU.add).then_inc(tile_free, 1)
            dve.wait_ge(sem("o_rooted"), 1)
            nc.vector.reciprocal(o_rstd[:, :], o_root[:, :]).then_inc(sem("o_col"), 1)
            for h in range(AH):
                dve.wait_ge(sem("o_row"), h + 1)
                wait(dve, sem("o_lo"), h - 1)
                nc.vector.scalar_tensor_tensor(out=o_nrm[:, h % 2, :], in0=o_un[:, h, :], scalar=subln[:, :],
                                               in1=bank[2 + h % 2][:, :], op0=ALU.mult, op1=ALU.mult)\
                  .then_inc(sem("o_nrmd"), 1)
                dve.wait_ge(sem("o_hi"), h + 1)
                nc.vector.tensor_tensor(o_lo[:, h, :], o_nrm[:, h % 2, :], o_hi[:, h, :].bitcast(F32),
                                        ALU.subtract).then_inc(sem("o_lo"), 1)
            residual_stage("mix_attn", "norm_cross_w", 1, 1.0, "n_cross")
            dve.wait_ge(sem("m_in"), 16)
            nc.vector.memset(m_sum[:, :], 0.0).then_inc(sem("m_sum"), 1)
            for m in range(DC):
                dve.wait_ge(sem("m_square"), m + 1)
                dve.wait_ge(sem("m_sum"), m + 1)
                nc.vector.tensor_tensor(m_sum[:, :], m_sum[:, :], square[:, 0:ML], ALU.add)\
                  .then_inc(sem("m_sum"), 1)
                dve.wait_ge(sem("m_hi"), m + 1)
                nc.vector.scalar_tensor_tensor(out=m_lo[:, m, :], in0=m_T[:, m, :], scalar=col("norm_mem_w", m),
                                               in1=m_hi[:, m, :].bitcast(F32), op0=ALU.mult, op1=ALU.subtract)\
                  .then_inc(sem("m_lo"), 1)
            dve.wait_ge(sem("m_root"), 1)
            nc.vector.reciprocal(m_rstd[:, :], m_root[:, :]).then_inc(sem("m_col"), 1)
            dve.wait_ge(sem("m_rowed"), 1)
            link(nc.vector.tensor_copy(m_row[:, :], bank[6][:, 0:ML]))
            scaled_tiles("ck", kx_T, 8, row=m_row)
            norm("n_cross")
            scaled_tiles("cq", qx_T, 8, scale=-0.0625)
            for n in range(XH * TT + 1):
                if n < XH * TT:
                    dve.wait_ge(sem("x_score"), n + 1)
                    nc.vector.tensor_reduce(xmin[:, n:n + 1], bank[2 + n % 3][:, 0:ML], AX_X, ALU.min)\
                      .then_inc(sem("x_min"), 1)
                if n > 0:
                    k = n - 1
                    dve.wait_ge(sem("x_exp"), k + 1)
                    link(nc.vector.reciprocal(xrec[:, k:k + 1], xsum[:, k:k + 1]))
                    nc.vector.tensor_scalar(px[:, k % 4, :], px[:, k % 4, :], xrec[:, k:k + 1], None, ALU.mult)\
                      .then_inc(sem("x_prob"), 1)
                    if k % TT == TT - 1:
                        hd = k // TT
                        dve.wait_ge(sem("x_turned"), k + 1)
                        wait(dve, sem("ox_mm"), 2 * hd)
                        for kk in range(MT):
                            nc.vector.tensor_copy(pxT[:, kk, :], bank[5 + kk][:, :]).then_inc(sem("x_pT"), 1)
                        if hd > 0:
                            x_lo(hd - 1)
            x_lo(XH - 1)
            residual_stage("co", "norm_ffn2_w", 1, 1.0, "n_ffn2")
            ffn("ffn2", "n_ffn2", None)
            dve.wait_ge(norm_sem("root"), norm_count("root", "n_fin", 1))
            link(nc.vector.tensor_scalar(fin[:, 8:12], root_col[:, 0:4], EPS, None, ALU.add))
            link(nc.vector.reciprocal(fin[:, 12:16], fin[:, 8:12]))
            nc.vector.tensor_tensor(fin[:, 0:4], fin[:, 12:16], root_col[:, 4:8], ALU.mult)\
              .then_inc(sem("n_fin_var"), 1)
            dve.wait_ge(norm_sem("root"), norm_count("root", "n_fin", 3))
            link(nc.vector.reciprocal(fin[:, 24:32], fin[:, 16:24]))
            nc.vector.tensor_copy(root_col[:, 4:8], fin[:, 28:32])
            nc.vector.tensor_tensor(rstd_col[:, :], fin[:, 24:28], fin[:, 28:32], ALU.mult)\
              .then_inc(norm_sem("col"), 1)
            dve.wait_ge(norm_sem("row"), norm_count("row", "n_fin", 1))
            nc.vector.tensor_copy(rstd_row[:, :], bank[7][:, :]).then_inc(norm_sem("ready"), 1)
            dve.wait_ge(norm_sem("row"), norm_count("row", "n_fin", 2))
            link(nc.vector.tensor_copy(rfin_row[:, :], bank[7][:, :]))
            for c in range(4):
                dve.wait_ge(unit_done, UNIT0["qk2"] + c + 1)
                nc.vector.scalar_tensor_tensor(out=q2_T[:, c, :], in0=bank[c % 2][:, :], scalar=0.125,
                                               in1=rstd_row[:, :], op0=ALU.mult, op1=ALU.mult)\
                  .then_inc(tile_free, 1)
            for c in range(4):
                dve.wait_ge(unit_done, UNIT0["qk2"] + 4 + c + 1)
                nc.vector.tensor_tensor(k2_T[:, c, :], bank[c % 2][:, :], rstd_row[:, :], ALU.mult)\
                  .then_inc(tile_free, 1)
            nc.vector.memset(cprod[:, 0:2], 0.0).then_inc(sem("cprod_pad"), 1)
            for m in range(DC):
                nc.vector.tensor_tensor(x[:, m, :], x[:, m, :], rfin_row[:, :], ALU.mult).then_inc(sem("x1"), 1)
            for c in range(4):
                U = UNIT0["conv2"] + 3 * c
                dve.wait_ge(unit_done, U + 1)
                nc.vector.tensor_tensor(cc_t[:, :], bank[(3 * c) % 2][:, :], rstd_row[:, :], ALU.mult)\
                  .then_inc(tile_free, 1)
                dve.wait_ge(unit_done, U + 2)
                nc.vector.tensor_tensor(cu_t[:, :], bank[(3 * c + 1) % 2][:, :], rstd_row[:, :], ALU.mult)\
                  .then_inc(tile_free, 1)
                dve.wait_ge(tile_free, TILE0["conv2"] + 3 * c + 2)
                wait(dve, sem("cv_lo"), c)
                link(nc.vector.tensor_tensor(cprod[:, 2:2 + S], cc_t[:, :], cu_t[:, :], ALU.mult))
                link(nc.vector.tensor_scalar(cacc[:, :], cprod[:, 0:S], col("w_conv_2", c), None, ALU.mult))
                for k in (1, 2):
                    link(nc.vector.scalar_tensor_tensor(out=cacc[:, :], in0=cprod[:, k:k + S],
                                                        scalar=col("w_conv_2", 4 * k + c), in1=cacc[:, :],
                                                        op0=ALU.mult, op1=ALU.add))
                dve.wait_ge(unit_done, U + 3)
                nc.vector.tensor_tensor(cc_t[:, :], bank[(3 * c + 2) % 2][:, :], rstd_row[:, :], ALU.mult)\
                  .then_inc(tile_free, 1)
                dve.wait_ge(tile_free, TILE0["conv2"] + 3 * c + 3)
                nc.vector.tensor_tensor(cacc[:, :], cacc[:, :], cc_t[:, :], ALU.mult).then_inc(sem("cv_out"), 1)
                dve.wait_ge(sem("cv_hi"), c + 1)
                nc.vector.tensor_tensor(cv_lo[:, c, :], cacc[:, :], cv_hi[:, c, :].bitcast(F32), ALU.subtract)\
                  .then_inc(sem("cv_lo"), 1)

            def gate_block(i):
                for j in range(4):
                    c = i * 4 + j
                    dve.wait_ge(unit_done, UNIT0["gates2"] + c + 1)
                    wait(dve, sem("gate_sig"), c)
                    nc.vector.tensor_tensor(gate_t[:, :], bank[j % 2][:, :], rstd_row[:, :], ALU.mult)\
                      .then_inc(tile_free, 1)
            blocks(dve, 4, gate_block, peel=1)
            dve.wait_ge(sem("gate_sig"), 16)

            diag = {j: S * bk + o for j, (bk, o) in {0: (0, 0), 1: (1, 0), 3: (1, 3 * P), 2: (2, 0)}.items()}
            for h in range(KH + 2):
                if h < KH:
                    b = h % 2
                    dve.wait_ge(sem("z_mm"), h + 1)
                    wait(dve, sem("sp_masked"), h - 1)
                    for bk in range(3):
                        n = S if bk < 2 else 2 * P
                        nc.vector.tensor_scalar(sz_buf[b][:, bk * S:bk * S + n], bank[2 + bk][:, 0:n], 40.0, None,
                                                ALU.min).then_inc(sem("z_clamped"), 1)
                if 0 < h <= KH:
                    k = h - 1
                    dve.wait_ge(sem("w_exp"), k + 1)
                    for j in range(TT):
                        w = w_buf[k % 2][:, diag[j]:diag[j] + P]
                        ins = nc.vector.scalar_tensor_tensor(out=w, in0=w, scalar=-NEG, in1=tri_lt, op0=ALU.min,
                                                             op1=ALU.mult)
                    ins.then_inc(sem("w_masked"), 1)
                if h < KH:
                    dve.wait_ge(sem("sp_lned"), h + 1)
                    wait(dve, sem("c_mm"), h - 1)
                    for bk in range(3):
                        n = S if bk < 2 else 2 * P
                        ins = nc.vector.tensor_tensor(sp_buf[b][:, bk * S:bk * S + n], bank[2 + bk][:, 0:n],
                                                      sz_buf[b][:, bk * S:bk * S + n], ALU.max)
                    ins.then_inc(sem("sp_ready"), 1)
                    dve.wait_ge(sem("sp_ready"), h + 1)
                    for j in range(TT):
                        v = sp_buf[b][:, diag[j]:diag[j] + P]
                        ins = nc.vector.tensor_tensor(v, v, tri_lt, ALU.mult)
                    ins.then_inc(sem("sp_masked"), 1)
                if h > 1 and h % 2 == 1:
                    c = (h - 2) // 2
                    dve.wait_ge(sem("o2_hi"), c + 1)
                    nc.vector.tensor_tensor(o2_lo[:, c, :], bank[c % 2][:, :], o2_hi[:, c, :].bitcast(F32),
                                            ALU.subtract).then_inc(sem("o2_lo"), 1)
            with dve.Fori(0, 2) as i:
                for j in range(4):
                    c = i * 4 + j
                    dve.wait_ge(unit_done, UNIT0["branch2"] + c + 1)
                    nc.vector.tensor_tensor(br_a[:, :], bank[0][:, :], tile_of(gates, c), ALU.mult)\
                      .then_inc(tile_free, 1)
                    nc.vector.tensor_tensor(br_b[:, :], bank[1][:, :], tile_of(gates, c + 8), ALU.mult)\
                      .then_inc(tile_free, 1)
                    dve.wait_ge(tile_free, TILE0["branch2"] + 2 * c + 2)
                    nc.vector.tensor_tensor(br_m[:, :], br_a[:, :], br_b[:, :], ALU.add).then_inc(sem("mixed"), 1)
                    dve.wait_ge(sem("gx_hi_done"), gx_count("branch2", c + 1))
                    nc.vector.tensor_tensor(tile_of(gx_lo, c), br_m[:, :], tile_of(gx_hi, c).bitcast(F32),
                                            ALU.subtract).then_inc(sem("gx_lo_done"), 1)
            start_sums()

            def o2_block(i):
                for j in range(4):
                    m = i * 4 + j
                    dve.wait_ge(unit_done, UNIT0["o2"] + m + 1)
                    nc.vector.tensor_copy(tile_of(y_o2, m), bank[j % 2][:, :]).then_inc(tile_free, 1)
                    add_square("o2", m)
            blocks(dve, 2, o2_block)
            def post(name, norm_name, weight, next_weight, src, next_norm):
                norm(norm_name)
                start_sums()
                for m in range(DC):
                    wait(dve, sem(f"{name}_x"), m)
                    link(nc.vector.scalar_tensor_tensor(out=pn_t[:, :], in0=src[:, m, :], scalar=col(weight, m),
                                                        in1=rstd_row[:, :], op0=ALU.mult, op1=ALU.mult))
                    nc.vector.tensor_tensor(x[:, m, :], x[:, m, :], pn_t[:, :], ALU.add)\
                      .then_inc(sem(f"{name}_x"), 1)
                    if m > 0:
                        split_lo(name, next_weight, m - 1, x)
                        add_square(name, m - 1)
                split_lo(name, next_weight, DC - 1, x)
                add_square(name, DC - 1)
            post("post", "n_post", "g_post_mix_2", "g_pre_mlp_2", y_o2, "n_mlp")

            def up_stage(stage, half):
                def block_of(i):
                    for j in range(4):
                        c = i * 4 + j
                        if first(i) and j == 0 and half == 0:
                            norm("n_mlp")
                        dve.wait_ge(unit_done, UNIT0[stage] + c + 1)
                        nc.vector.tensor_tensor(up_t[:, :], bank[j % 2][:, :], rstd_row[:, :], ALU.mult)\
                          .then_inc(tile_free, 1)
                        dve.wait_ge(tile_free, TILE0[stage] + c + 1)
                        nc.vector.scalar_tensor_tensor(out=up_a[:, :], in0=up_t[:, :], scalar=0.0, in1=up_t[:, :],
                                                       op0=ALU.max, op1=ALU.mult).then_inc(sem("up_act"), 1)
                        dve.wait_ge(sem("up_hi"), half * HC + c + 1)
                        nc.vector.tensor_tensor(tile_of(up_lo, c), up_a[:, :],
                                                tile_of(up_hi, c).bitcast(F32), ALU.subtract)\
                          .then_inc(sem("up_lo"), 1)
                blocks(dve, 4, block_of, peel=1 - half)
            up_stage("up_a", 0)

            def down_block(i):
                for j in range(4):
                    m = i * 4 + j
                    dve.wait_ge(unit_done, UNIT0["down_a"] + m * 2 + 2)
                    nc.vector.tensor_copy(tile_of(f_acc, m), bank[j % 2][:, :]).then_inc(tile_free, 1)
            blocks(dve, 2, down_block)
            up_stage("up_b", 1)
            start_sums()

            def down_block_b(i):
                for j in range(4):
                    m = i * 4 + j
                    fm = tile_of(f_acc, m)
                    dve.wait_ge(unit_done, UNIT0["down_b"] + m * 2 + 2)
                    nc.vector.tensor_tensor(fm, bank[j % 2][:, :], fm, ALU.add).then_inc(tile_free, 1)
                    add_square("down", m)
            blocks(dve, 2, down_block_b)
            for k in range(2):
                dve.wait_ge(sem("p_hi"), k + 1)
                nc.vector.tensor_tensor(p_lo[:, k, :], p_T[:, k, :], p_hi[:, k, :].bitcast(F32), ALU.subtract)\
                  .then_inc(sem("p_lo"), 1)
            for m in range(DC):
                dve.wait_ge(unit_done, UNIT0["proj2"] + m // 2 + 1)
                nc.vector.tensor_copy(proj[:, m, :], bank[m % 2][:, :]).then_inc(tile_free, 1)
            post("pmlp", "n_pmlp", "g_post_mlp_2", "g_ple_2", f_acc, "n_ple")
            norm("n_ple")
            for m in range(DC):
                dve.wait_ge(unit_done, UNIT0["ple2"] + m + 1)
                nc.vector.tensor_tensor(ple_t[:, :], bank[m % 2][:, :], rstd_row[:, :], ALU.mult)\
                  .then_inc(tile_free, 1)
                dve.wait_ge(sem("ple_sig"), m + 1)
                link(nc.vector.tensor_tensor(ple_o[:, m, :], ple_g[:, :], proj[:, m, :], ALU.mult))
                nc.vector.tensor_tensor(ple_o[:, m, :], ple_o[:, m, :], x[:, m, :], ALU.add)\
                  .then_inc(sem("out_ready"), 1)


def _cols(v, n):
    return np.ascontiguousarray(np.asarray(v).reshape(n, P).T)


def _units(w):
    K, N = w.shape
    per = -(-K // UNIT)
    if K < per * UNIT:
        w = np.concatenate([w, np.zeros((per * UNIT - K, N), w.dtype)])
    return w.reshape(per, UC, P, N // P, P).transpose(3, 0, 2, 1, 4).reshape(-1, P, UNIT)


def _token_units(w):
    K, N = w.shape
    return w.reshape(K // (2 * P), 2, P, N // S, S).transpose(3, 0, 2, 1, 4).reshape(-1, P, UNIT)


def _interleave(*parts):
    return np.stack(parts, axis=1).reshape(-1, P, UNIT)


def _shape_constants():
    i = np.arange(P)
    f = np.float32
    m = [np.eye(P, dtype=f), (i[:, None] <= i[None, :]).astype(f), np.ones((P, P), f), np.eye(P, dtype=f)[::-1],
         -(i[:, None] >= i[None, :]).astype(f), -np.ones((P, P), f), (i[:, None] < i[None, :]).astype(f)]
    n = (S - 1) - np.arange(BIAS_W + 1)
    big = 16 + (np.log(np.maximum(n, 1).astype(f) / f(16)) / f(np.log(8.0)) * f(16)).astype(np.int32)
    b = np.where(n < 16, np.maximum(n, 0), np.minimum(big, 31))
    onehot = (np.arange(32)[:, None] == b[None, :]).astype(f)
    pen = np.where(n < 0, f(MASK), f(0)).astype(f)[None, :].repeat(AH, 0)
    return np.concatenate(m, axis=1), onehot, np.ascontiguousarray(pen)


def kernel(**inputs):
    import concourse.bacc as bacc
    from concourse.bass_utils import run_bass_kernel_spmd

    v = {k: np.asarray(a) for k, a in inputs.items()}
    w_mix, w2 = v["w_in_mix"][0], v["w_in_2"][0]
    z0, xb0 = 0, D
    dt0 = xb0 + 2048
    q0 = dt0 + 16
    gate, up = _units(v["ffn1_w_in"][0][:, :FF]), _units(v["ffn1_w_in"][0][:, FF:])
    gate2, up2 = _units(v["ffn2_w_in"][0][:, :FF]), _units(v["ffn2_w_in"][0][:, FF:])
    wo = v["w_out_mix"][0]
    branch = np.concatenate([v["w_attn_out_2"][0], v["w_conv_out_2"][0]])
    down = v["w_down_2"][0]
    proj = v["w_ple_proj_2"][0].reshape(2, P, 4, 2, P).transpose(2, 1, 3, 0, 4).reshape(4, P, UNIT // 2)
    proj = np.concatenate([proj, np.zeros_like(proj)], axis=2)
    upw = _units(v["w_up_2"][0])
    stream = np.concatenate([
        _interleave(gate, up), _units(v["ffn1_w_out"][0]),
        _units(w_mix[:, xb0:dt0]), _token_units(w_mix[:, z0:xb0]),
        _units(w_mix[:, q0:q0 + D]), _units(w_mix[:, q0 + D:q0 + 2 * D]), _token_units(w_mix[:, q0 + 2 * D:]),
        _units(wo[:D]), _units(wo[D:]),
        _units(v["w_ck"][0]), _token_units(v["w_cv"][0]), _units(v["w_cq"][0]), _units(v["w_co"][0]),
        _interleave(gate2, up2), _units(v["ffn2_w_out"][0]),
        _units(w2[:, :2 * S]), _token_units(w2[:, 2 * S:3 * S]),
        _interleave(_units(w2[:, 4 * S:5 * S]), _units(w2[:, 5 * S:6 * S]), _units(w2[:, 3 * S:4 * S])),
        _units(w2[:, 6 * S:]),
        _units(branch), _units(v["w_o_2"][0]),
        upw[:HC], _units(down[:FF2 // 2]), upw[HC:], _units(down[FF2 // 2:]),
        proj, _units(v["w_ple_gate_2"][0]),
    ])
    assert stream.shape[0] == UNITS
    cols = np.concatenate([
        _cols(v["norm_ffn1_w"], 8), _cols(v["norm_mix_w"], 8),
        _cols(v["conv_w"][0], 64), _cols(v["conv_b"], 16), _cols(v["ssd_norm_w"], 8), _cols(v["subln_w"], 1),
        _cols(v["norm_cross_w"], 8), _cols(v["norm_mem_w"], 8), _cols(v["norm_ffn2_w"], 8),
        _cols(v["norm_final_w"], 8), _cols(v["g_pre_mix_2"], 8), _cols(v["b_gate_2"], 16),
        _cols(v["w_conv_2"][0], 12), _cols(v["g_post_mix_2"], 8), _cols(v["g_pre_mlp_2"], 8),
        _cols(v["g_post_mlp_2"], 8), _cols(v["g_ple_2"], 8)], axis=1)
    rows = np.concatenate([v[n].reshape(1, -1) for n in ROWS], axis=1)
    consts, onehot, pen = _shape_constants()
    arrays = {
        "wstream": stream, "xT": v["x"][0].T, "memT": v["mem"][0].T, "pT": v["p_2"][0, 0].T,
        "cols": cols, "rows": rows,
        "wdt": w_mix[:, dt0:q0].reshape(8, P, 16).transpose(1, 0, 2), "relb": v["rel_bias"],
        "consts": consts, "onehot": onehot, "pen": pen,
    }
    nc = bacc.Bacc("TRN2", target_bir_lowering=False, num_devices=1)
    args = []
    for name in list(arrays):
        arrays[name] = np.ascontiguousarray(arrays[name])
        args.append(nc.dram_tensor(name, arrays[name].shape, F32, kind="ExternalInput").ap())
    args.append(nc.dram_tensor("outT", (D, S), F32, kind="ExternalOutput").ap())
    build(nc, *args)
    got = run_bass_kernel_spmd(nc, [arrays], core_ids=[0]).results[0]["outT"]
    return np.ascontiguousarray(got.T)[None]
```

```python
from contextlib import ExitStack

import numpy as np
import concourse.bass as bass
from concourse import mybir

F32 = mybir.dt.float32
F32R = mybir.dt.float32r
ALU = mybir.AluOpType
ACT = mybir.ActivationFunctionType
AX_X = mybir.AxisListType.X
ds = bass.ds

P = 128
S = 512
TT = S // P
D = 1024
DC = D // P
FF = 2816
FC = FF // P
ML = 256
MT = ML // P
UC = 8
UNIT = UC * P
RING = 4
EPS = 1e-6
NEG = -3.0e38
MASK = 1.0e30
SH, SHD, SG, SN = 16, 64, 4, 128
GH = SH // SG
AH, AV = 8, 128
XH = 4
KH = 8
FF2 = 4096
HC = FF2 // P // 2
LAMBDA_INIT = 0.2
BIAS_W = S + P - 1

STAGES = [
    ("ffn1_in", 2 * FC), ("ffn1_out", 24),
    ("xbc", 16), ("z", 8), ("q", 8), ("k", 8), ("v", 8), ("mix_ssd", 8), ("mix_attn", 8),
    ("ck", 8), ("cv", 8), ("cq", 8), ("co", 8),
    ("ffn2_in", 2 * FC), ("ffn2_out", 24),
    ("qk2", 8), ("v2", 4), ("conv2", 12), ("gates2", 16), ("branch2", 8), ("o2", 8),
    ("up_a", HC), ("down_a", 16), ("up_b", HC), ("down_b", 16), ("proj2", 4), ("ple2", 8),
]
TILES = {"ffn1_in": 2 * FC, "ffn1_out": 8, "xbc": 16, "q": 8, "k": 8, "mix_ssd": 8, "mix_attn": 8,
         "ck": 8, "cq": 8, "co": 8, "ffn2_in": 2 * FC, "ffn2_out": 8, "qk2": 8, "conv2": 12,
         "gates2": 16, "branch2": 16, "o2": 8, "up_a": HC, "down_a": 8, "up_b": HC, "down_b": 8,
         "proj2": 8, "ple2": 8}
UNIT0, TILE0 = {}, {}
_u = _t = 0
for _name, _n in STAGES:
    UNIT0[_name], TILE0[_name] = _u, _t
    _u += _n
    _t += TILES.get(_name, 0)
UNITS = _u
assert UNITS % RING == 0 and all(v % 2 == 0 for v in TILE0.values())

OPERANDS = ["load", "ffn1_out", "mix_attn", "co", "ffn2_out", "branch2", "post", "pmlp"]
SUMS = ["load", "ffn1_out", "mix_attn", "co", "ffn2_out", "o2", "post", "down", "pmlp"]
NORMS = ["n_ffn1", "n_mix", "n_cross", "n_ffn2", "n_fin", "n_post", "n_mlp", "n_pmlp", "n_ple"]

COLS = {}
_c = 0
for _name, _n in (("norm_ffn1_w", 8), ("norm_mix_w", 8), ("conv_w", 64), ("conv_b", 16), ("ssd_norm_w", 8),
                  ("subln_w", 1), ("norm_cross_w", 8), ("norm_mem_w", 8), ("norm_ffn2_w", 8),
                  ("norm_final_w", 8), ("g_pre_mix_2", 8), ("b_gate_2", 16), ("w_conv_2", 12),
                  ("g_post_mix_2", 8), ("g_pre_mlp_2", 8), ("g_post_mlp_2", 8), ("g_ple_2", 8)):
    COLS[_name] = _c
    _c += _n
NCOLS = _c
ROWS = {"dt_bias": 0, "a_log": 16, "d_skip": 32, "lambda_q1": 48, "lambda_k1": 112, "lambda_q2": 176,
        "lambda_k2": 240}
NROWS = 304


def build(nc, wstream, xT, memT, pT, cols_d, rows_d, wdt_d, relb_d, consts_d, onehot_d, pen_d, out):
    ctx = ExitStack()
    with ctx:
        sems = {}

        def sem(name):
            if name not in sems:
                sems[name] = ctx.enter_context(nc.semaphore(name))
            return sems[name]

        def norm_sem(step):
            return sem(f"norm_{step}")

        def norm_count(step, name, k):
            n = NORMS.index(name)
            more = {"root": 2, "row": 1}.get(step, 0)
            return n + k + (more if n > NORMS.index("n_fin") else 0)

        def gx_count(stage, k):
            return OPERANDS.index(stage) * DC + k

        def square_count(stage, k):
            return SUMS.index(stage) * DC + k

        def sum_count(stage, k):
            return SUMS.index(stage) * (DC + 1) + k

        def ffn_count(name, k):
            return (FC if name == "ffn2" else 0) + k

        cursor = [(nc.sbuf_base + 63) // 64 * 64]

        def fixed(name, shape, dt=F32):
            t = nc.alloc_sbuf_tensor_at(name, [P] + shape, dt, offset=cursor[0])
            cursor[0] += (int(np.prod(shape)) * 4 + 63) // 64 * 64
            return t

        x = fixed("x", [DC, S])
        GX_HI, GX_LO = cursor[0], cursor[0] + DC * S * 4
        gx_hi = fixed("gx_hi", [DC, S], F32R)
        gx_lo = fixed("gx_lo", [DC, S], F32R)
        w_raw = fixed("w_raw", [RING, UNIT])
        w_hi = fixed("w_hi", [RING, UNIT], F32R)
        w_lo = fixed("w_lo", [RING, UNIT], F32R)
        consts = fixed("consts", [7 * P])
        cols = fixed("cols", [NCOLS])
        rows = fixed("rows", [NROWS])
        rstd_row = fixed("rstd_row", [S])
        sumsq = fixed("sumsq", [S])
        square = fixed("square", [S])
        rstd_col = fixed("rstd_col", [TT])
        root_col = fixed("root_col", [2 * TT])
        rfin_row = fixed("rfin_row", [S])
        eps_col = fixed("eps_col", [1])
        subln = fixed("subln", [1])
        fin = fixed("fin", [32])
        wdt = fixed("wdt", [8, 16])
        wdt_hi = fixed("wdt_hi", [8, 16], F32R)
        wdt_lo = fixed("wdt_lo", [8, 16], F32R)
        m_root = fixed("m_root", [MT])
        m_rstd = fixed("m_rstd", [MT])
        xmin = fixed("xmin", [16])
        xsum = fixed("xsum", [16])
        xrec = fixed("xrec", [16])
        y_sq, y_root, y_rstd = xmin, xsum, xrec
        REGION = cursor[0]
        REGION_END = nc.sbuf_usable_end if not callable(nc.sbuf_usable_end) else nc.sbuf_usable_end()

        def at(name, kb, shape, dt=F32):
            off = REGION + int(kb * 1024)
            size = int(np.prod(shape)) * 4
            assert off + size <= REGION_END, (name, off + size - REGION_END)
            return nc.alloc_sbuf_tensor_at(name, [P] + shape, dt, offset=off)

        ident, tri_le, ones, flip, neg_ge, neg_ones, tri_lt = (consts[:, i * P:(i + 1) * P] for i in range(7))

        def first(i):
            return isinstance(i, int) and i == 0

        def tile_of(buf, c):
            if isinstance(c, int):
                return buf[:, c, :]
            n = buf.shape[2]
            return buf[:, :, :].rearrange("p a b -> p (a b)")[:, ds(c * n, n)]

        def col(name, i):
            return cols[:, COLS[name] + i:COLS[name] + i + 1]

        def col_at(name, i):
            return cols[:, ds(COLS[name] + i, 1)]

        ff_hi = at("ff_hi", 0, [FC, S], F32R)
        ff_lo = at("ff_lo", 44, [FC, S], F32R)
        ff_gate = at("ff_gate", 88, [S])
        ff_silu = at("ff_silu", 90, [S])
        ff_up = at("ff_up", 92, [S])
        ff_act = at("ff_act", 94, [S])
        sumsq2 = at("sumsq2", 88, [S])
        square2 = at("square2", 90, [S])
        z_tok = at("z_tok", 0, [TT, D])
        bc = at("bc", 16, [8, S])
        xs_tok = at("xs_tok", 32, [TT, D])
        xs_T = at("xs_T", 48, [8, S])
        conv_in = at("conv_in", 92.5, [S + 3])
        conv_acc = at("conv_acc", 88.5, [S])
        dt_pre = at("dt_pre", 70.5, [TT, SH])
        dt_T = at("dt_T", 64, [S])
        dt_exp = at("dt_exp", 70.75, [TT, SH])
        dt_ln = at("dt_ln", 71, [TT, SH])
        dt = at("dt", 71.25, [TT, SH])
        a_row = at("a_row", 71.5, [SH])
        la = at("la", 71.75, [TT, SH])
        cum = at("cum", 72, [TT, SH])
        ecum = at("ecum", 72.5, [TT, SH])
        to_end = at("to_end", 72.75, [TT, SH])
        e_end = at("e_end", 73, [TT, SH])
        c_dec = at("c_dec", 73.25, [TT, SH])
        cb_m = at("cb_m", 74.5, [2, P])
        b_tok = at("b_tok", 75.5, [2, P])
        decay = at("decay", 76.5, [2, GH, P])
        mix_m = at("mix_m", 80.5, [2, GH, P])
        seg = at("seg", 64, [2, GH, P])
        state = at("state", 84.5, [SG, GH, SHD])
        xdt = at("xdt", 88.5, [2, GH, SHD])
        xdte = at("xdte", 90.5, [2, GH, SHD])
        y_a = at("y_a", 92.5, [GH, SHD])
        y_b = at("y_b", 93.5, [GH, SHD])
        y_c = at("y_c", 94.5, [GH, SHD])
        ysq_tmp = at("ysq_tmp", 69, [GH * SHD])
        ys_hi = at("ys_hi", 16, [DC, S], F32R)
        ys_lo = at("ys_lo", 32, [DC, S], F32R)
        q_T = at("q_T", 48, [AH, S])
        k_T = at("k_T", 64, [AH, S])
        v_tok = at("v_tok", 80, [TT, D])
        NB = P * (1 + 2 + 3 + 4)

        def in_gx(name, kb, shape):
            assert kb * 1024 + int(np.prod(shape)) * 4 <= 2 * DC * S * 4
            return nc.alloc_sbuf_tensor_at(name, [P] + shape, F32, offset=GX_HI + int(kb * 1024))

        bias_h = in_gx("bias_h", 0, [2, S])
        prob = in_gx("prob", 4, [2, 2, NB])
        w_T = in_gx("w_T", 24, [NB])
        o_sq = in_gx("o_sq", 29, [S])
        lam_tmp = in_gx("lam_tmp", 29, [SHD])
        rsum = in_gx("rsum", 31, [2, 8])
        rrec = in_gx("rrec", 31.125, [2, 8])
        amin = in_gx("amin", 31.25, [2, 8])
        o_root = in_gx("o_root", 31.5, [TT * AH])
        o_rstd = in_gx("o_rstd", 31.625, [TT * AH])
        lam = in_gx("lam", 31.75, [8])
        o_nrm = in_gx("o_nrm", 0, [2, S])
        o_un = at("o_un", 0, [AH, S])
        bflip = [square, rfin_row]
        o_hi = at("o_hi", 48, [AH, S], F32R)
        o_lo = at("o_lo", 64, [AH, S], F32R)
        relb = at("relb", 80, [AH])
        onehot = at("onehot", 81, [BIAS_W + 1])
        pen = at("pen", 84, [BIAS_W + 1])
        brow = at("brow", 87, [BIAS_W + 1])
        m_T = at("m_T", 16, [DC, ML])
        m_hi = at("m_hi", 24, [DC, ML], F32R)
        m_lo = at("m_lo", 32, [DC, ML], F32R)
        kx_T = at("kx_T", 0, [DC, ML])
        vx = at("vx", 8, [MT, D])
        px = at("px", 40, [4, ML])
        pxT = at("pxT", 44, [MT, S])
        qx_T = at("qx_T", 48, [DC, S])
        ox_hi = at("ox_hi", 64, [DC, S], F32R)
        ox_lo = at("ox_lo", 80, [DC, S], F32R)
        m_sum = at("m_sum", 40, [ML])
        m_row = at("m_row", 41, [ML])
        m_sq = at("m_sq", 42, [ML])
        q2_T = at("q2_T", 0, [4, S])
        k2_T = at("k2_T", 8, [4, S])
        v2_tok = at("v2_tok", 16, [TT, S])
        cv_hi = at("cv_hi", 24, [4, S], F32R)
        cv_lo = at("cv_lo", 32, [4, S], F32R)
        gates = at("gates", 40, [16, S])
        o2_hi = at("o2_hi", 72, [4, S], F32R)
        o2_lo = at("o2_lo", 80, [4, S], F32R)
        gate_t = at("gate_t", 88, [S])
        cc_t = at("cc_t", 90, [S])
        cu_t = at("cu_t", 92, [S])
        cprod = at("cprod", 94, [S + 2])
        cacc = square

        def over(name, base, kb, n):
            return nc.alloc_sbuf_tensor_at(name, [P, n], F32, offset=base + kb * 1024)

        sz_buf = [over(f"stick_exp{i}", GX_HI, 5 * i, NB) for i in range(2)]
        sp_buf = [over(f"stick_sum{i}", GX_LO, 5 * i, NB) for i in range(2)]
        w_buf = [over("stick_w0", GX_HI, 10, NB), over("stick_w1", GX_LO, 10, NB)]

        def by_bank(buf):
            return [buf[:, a:e] for a, e in ((0, S), (S, 2 * S), (2 * S, NB))]

        br_a = at("br_a", 88, [S])
        br_b = at("br_b", 90, [S])
        br_m = at("br_m", 92, [S])
        y_o2 = at("y_o2", 0, [DC, S])
        pn_t = at("pn_t", 38, [S])
        post_sq = at("post_sq", 56, [DC, S])
        up_hi = at("up_hi", 16, [HC, S], F32R)
        up_lo = at("up_lo", 48, [HC, S], F32R)
        f_acc = at("f_acc", 80, [DC, S])
        up_t = at("up_t", 0, [S])
        up_a = at("up_a", 2, [S])
        p_T = at("p_T", 4, [2, S])
        p_hi = at("p_hi", 8, [2, S], F32R)
        p_lo = at("p_lo", 12, [2, S], F32R)
        proj = at("proj", 16, [DC, S])
        ple_t = at("ple_t", 32, [S])
        ple_g = at("ple_g", 34, [S])
        ple_o = at("ple_o", 36, [DC, S])

        bank = [ctx.enter_context(nc.psum_tensor(f"bank{i}", [P, S], F32)) for i in range(8)]
        bias_r = nc.dram_tensor("bias_rows", (AH, BIAS_W + 1), F32, kind="Internal").ap()

        unit_raw = [sem(f"unit_raw{i}") for i in range(RING)]
        unit_hi = sem("unit_hi")
        unit_lo = sem("unit_lo")
        unit_done = sem("unit_done")
        tile_free = sem("tile_free")

        def wait(eng, s, value):
            if not isinstance(value, int) or value > 0:
                eng.wait_ge(s, value)

        def blocks(eng, n, body, peel=0):
            for i in range(peel):
                body(i)
            if n - peel == 1:
                body(n - 1)
            elif n > peel:
                with eng.Fori(peel, n) as i:
                    body(i)

        block = ctx.enter_context(nc.Block())

        @block.sync
        def _(sp):
            for s in range(RING):
                sp.dma_start(w_raw[:, s, :], wstream[s]).then_inc(unit_raw[s], 16)
            with sp.Fori(1, UNITS // RING) as r:
                for s in range(RING):
                    sp.wait_ge(unit_lo, r * RING + (s - RING + 1))
                    sp.dma_start(w_raw[:, s, :], wstream[ds(r * RING + s, 1)].rearrange("a p n -> (a p) n"))\
                      .then_inc(unit_raw[s], 16)
            for m in range(DC):
                sp.wait_ge(sem("out_ready"), m + 1)
                sp.dma_start(out[m * P:(m + 1) * P, :], ple_o[:, m, :]).then_inc(sem("out_stored"), 16)
            sp.wait_ge(sem("out_stored"), 16 * DC)

        @block.gpsimd
        def _(pool):
            def split_unit(r, s):
                pool.wait_ge(unit_hi, r * RING + (s + 1))
                nc.gpsimd.tensor_tensor(w_lo[:, s, :], w_raw[:, s, :], w_hi[:, s, :].bitcast(F32),
                                        ALU.subtract).then_inc(unit_lo, 1)

            def rounds(a, b):
                with pool.Fori(a, b) as r:
                    for s in range(RING):
                        split_unit(r, s)

            def post_sums(name):
                for m in range(DC):
                    pool.wait_ge(sem("squared"), square_count(name, m + 1))
                    pool.wait_ge(sem("summed"), sum_count(name, m + 1))
                    nc.gpsimd.tensor_tensor(sumsq[:, :], sumsq[:, :], post_sq[:, m, :], ALU.add)\
                      .then_inc(sem("summed"), 1)

            done = 0
            for stage, name in (("up_a", "post"), ("ple2", "pmlp")):
                r = UNIT0[stage] // RING
                rounds(done, r)
                for s in range(RING - 1):
                    split_unit(r, s)
                post_sums(name)
                split_unit(r, RING - 1)
                done = r + 1
            rounds(done, UNITS // RING)

        @block.tensor
        def _(pe):
            def products(slot, blk, dst, rhs, first, last):
                hi = w_hi[:, slot, blk * P:(blk + 1) * P]
                lo = w_lo[:, slot, blk * P:(blk + 1) * P]
                nc.tensor.matmul(dst, hi, rhs[0], start=first, stop=False)
                nc.tensor.matmul(dst, hi, rhs[1], start=False, stop=False)
                return nc.tensor.matmul(dst, lo, rhs[0], start=False, stop=last)

            def tiles(stage, rhs, chunks, body, peel=0, ready=None, n=S, hooks=(), banks=2, together=1):
                per = -(-chunks // UC)
                assert (body * per) % RING == 0
                at_block = dict(hooks)

                def block_of(i):
                    start = 0
                    if first(i) and together > 1:
                        start = together
                        pe.wait_ge(tile_free, TILE0[stage])
                        for k in range(chunks):
                            ready(k)
                            for j in range(together):
                                if k == 0:
                                    pe.wait_ge(unit_lo, UNIT0[stage] + j + 1)
                                mm = products((UNIT0[stage] + j) % RING, k, bank[j][:, 0:n], rhs(k), k == 0,
                                              k == chunks - 1)
                                if k == chunks - 1:
                                    mm.then_inc(unit_done, 1)
                        if (together - 1, chunks - 1) in at_block:
                            at_block[(together - 1, chunks - 1)]()
                    for j in range(start, body):
                        T = TILE0[stage] + i * body + j
                        wait(pe, tile_free, T - banks + 1)
                        dst = bank[j % banks][:, 0:n]
                        for uu in range(per):
                            jj = j * per + uu
                            pe.wait_ge(unit_lo, UNIT0[stage] + i * (body * per) + (jj + 1))
                            kk = range(uu * UC, min(chunks, (uu + 1) * UC))
                            for k in kk:
                                if ready and (first(i) and j == 0):
                                    ready(k)
                                mm = products((UNIT0[stage] + jj) % RING, k - uu * UC, dst, rhs(k),
                                              k == 0, k == chunks - 1)
                                if first(i) and (j, k) in at_block:
                                    at_block[(j, k)]()
                            mm.then_inc(unit_done, 1)
                blocks(pe, TILES[stage] // body, block_of, peel)

            def token_group(stage, g, lhs, n_tiles, group, between=None):
                for u in range(4):
                    U = UNIT0[stage] + 4 * g + u
                    pe.wait_ge(unit_lo, U + 1)
                    for t in range(n_tiles):
                        if u == 0 and group:
                            pe.wait_ge(sem("token_free"), group - n_tiles + t + 1)
                        for b in range(2):
                            k = 2 * u + b
                            rh = w_hi[:, U % RING, b * S:(b + 1) * S]
                            rl = w_lo[:, U % RING, b * S:(b + 1) * S]
                            dst = bank[2 + t][:, :]
                            a = [m[:, k, t * P:(t + 1) * P] for m in lhs]
                            nc.tensor.matmul(dst, a[0], rh, start=(k == 0), stop=False, skip_group_check=True)
                            nc.tensor.matmul(dst, a[1], rh, start=False, stop=False, skip_group_check=True)
                            mm = nc.tensor.matmul(dst, a[0], rl, start=False, stop=(k == DC - 1),
                                                  skip_group_check=True)
                    mm.then_inc(unit_done, 1)
                    if between:
                        between(4 * g + u)

            def norm_hooks(name, summed, stats=1, together=1):
                def stat():
                    if name == NORMS[0]:
                        pe.wait_ge(sem("setup_in"), 16 * 3)
                    pe.wait_ge(sem("summed"), sum_count(summed, DC + 1))
                    if stats == 2:
                        pe.wait_ge(sem("summed2"), DC + 1)
                    for s in range(stats):
                        src = sumsq if s == 0 else sumsq2
                        for t in range(TT):
                            mm = nc.tensor.matmul(bank[7][:, s * TT + t:s * TT + t + 1], src[:, t * P:(t + 1) * P],
                                                  ones[:, 0:1], start=True, stop=True)
                    mm.then_inc(norm_sem("stat"), 1)

                def row():
                    pe.wait_ge(norm_sem("col"), norm_count("col", name, 1))
                    for t in range(TT):
                        mm = nc.tensor.matmul(bank[7][:, t * P:(t + 1) * P],
                                              rstd_col[:, t:t + 1].to_broadcast([P, P]), ident, start=True, stop=True)
                    mm.then_inc(norm_sem("row"), 1)
                    if stats == 2:
                        pe.wait_ge(norm_sem("ready"), norm_count("ready", name, 1))
                        for t in range(TT):
                            mm = nc.tensor.matmul(bank[7][:, t * P:(t + 1) * P],
                                                  root_col[:, TT + t:TT + t + 1].to_broadcast([P, P]), ident,
                                                  start=True, stop=True)
                        mm.then_inc(norm_sem("row"), 1)
                return (((together - 1, UC - 1), stat), ((together, 3), row))

            gx = lambda k: (gx_hi[:, k, :], gx_lo[:, k, :])

            def gx_ready(name):
                return lambda k: pe.wait_ge(sem("gx_lo_done"), gx_count(name, k + 1))

            def ffn(name, norm, before):
                tiles(f"{name}_in", gx, DC, 4, peel=1, ready=gx_ready(before),
                      hooks=norm_hooks(norm, before, together=3), banks=4, together=3)

                def act_ready(k):
                    if k % UC == 0:
                        pe.wait_ge(sem("ffn_act_lo"), ffn_count(name, min(FC, k + UC)))
                tiles(f"{name}_out", lambda k: (ff_hi[:, k, :], ff_lo[:, k, :]), FC, 4, peel=1,
                      ready=act_ready)

            pe.wait_ge(sem("small_in"), 16 * 4)
            mm = nc.tensor.matmul(bank[4][0:AH, :], relb[0:32, :], onehot[0:32, 0:S], start=True, stop=True)
            mm = nc.tensor.matmul(bank[5][0:AH, 0:P], relb[0:32, :], onehot[0:32, S:S + P], start=True, stop=True)
            mm.then_inc(sem("brow_sum"), 1)

            ffn("ffn1", "n_ffn1", "load")

            tiles("xbc", gx, DC, 4, peel=1, ready=gx_ready("ffn1_out"), hooks=norm_hooks("n_mix", "ffn1_out"))
            pe.wait_ge(sem("wdt_lo"), 1)
            for k in range(DC):
                nc.tensor.matmul(bank[6][0:SH, :], wdt_hi[:, k, :], gx_hi[:, k, :], start=(k == 0), stop=False)
                nc.tensor.matmul(bank[6][0:SH, :], wdt_hi[:, k, :], gx_lo[:, k, :], start=False, stop=False)
                mm = nc.tensor.matmul(bank[6][0:SH, :], wdt_lo[:, k, :], gx_hi[:, k, :], start=False,
                                      stop=(k == DC - 1))
            mm.then_inc(sem("dt_mm"), 1)

            def turn_x(j):
                pe.wait_ge(sem("xbc_silu"), j + 1)
                wait(pe, sem("xs_copied"), j - 1)
                for t in range(TT):
                    mm = nc.tensor.transpose(bank[j % 2][:, t * P:(t + 1) * P],
                                             xs_T[:, j, t * P:(t + 1) * P], ident)
                mm.then_inc(sem("xs_turned"), 1)

            def between_z(u):
                if u == 0:
                    pe.wait_ge(tile_free, TILE0["q"])
                    pe.wait_ge(sem("dt_copied"), 1)
                    for t in range(TT):
                        mm = nc.tensor.transpose(bank[6][:, t * SH:(t + 1) * SH], dt_T[0:SH, t * P:(t + 1) * P],
                                                 ident[0:SH, 0:SH])
                    mm.then_inc(sem("dt_turned"), 1)
                turn_x(u)

            for g in range(2):
                token_group("z", g, (gx_hi, gx_lo), TT, 4 * g, between=between_z)
            pe.wait_ge(sem("la_ready"), 1)
            nc.tensor.matmul(bank[7][:, 0:TT * SH], tri_le, la[:, :, :], start=True, stop=True)
            nc.tensor.matmul(bank[7][:, TT * SH:2 * TT * SH], ones, la[:, :, :], start=True, stop=True)\
              .then_inc(sem("cum_mm"), 1)

            def ssd_front(n):
                t, g, b = n // SG, n % SG, n % 2
                tok = slice(t * P, (t + 1) * P)
                wait(pe, sem("cell_a_read"), 2 * n)
                nc.tensor.matmul(bank[1][:, 0:P], bc[:, g, tok], bc[:, SG + g, tok], start=True, stop=True)
                nc.tensor.transpose(bank[1][:, P:2 * P], bc[:, g, tok], ident).then_inc(sem("cell_a"), 1)
                wait(pe, sem("decayed"), n - 1)
                for r in range(GH):
                    h = g * GH + r
                    mm = nc.tensor.matmul(bank[2 + b][:, r * P:(r + 1) * P],
                                          la[:, t, h:h + 1].to_broadcast([P, P]), tri_le, start=True, stop=True)
                mm.then_inc(sem("cell_b"), 1)

            def ssd_back(n):
                t, g, b = n // SG, n % SG, n % 2
                pe.wait_ge(sem("cell_m"), n + 1)
                wait(pe, sem("cell_done"), n - 1)
                for r in range(GH):
                    mm = nc.tensor.matmul(bank[4 + b][:, r * SHD:(r + 1) * SHD], mix_m[:, b, r, :],
                                          xdt[:, b, r, :], start=True, stop=True)
                if t > 0:
                    wait(pe, sem("cell_done"), n - SG + 1)
                    mm = nc.tensor.matmul(bank[4 + b][:, 2 * P:4 * P], bc[:, SG + g, t * P:(t + 1) * P],
                                          state[:, g, :, :], start=True, stop=True)
                mm = nc.tensor.matmul(bank[6 + b][:, 0:2 * P], b_tok[:, b, :], xdte[:, b, :, :],
                                      start=True, stop=True)
                mm.then_inc(sem("cell_y"), 1)

            def q_half(n):
                c, half = n // 2, n % 2
                if half == 0:
                    pe.wait_ge(unit_lo, UNIT0["q"] + c + 1)
                    pe.wait_ge(tile_free, TILE0["q"] + c)
                for k in range(4 * half, 4 * half + 4):
                    mm = products((UNIT0["q"] + c) % RING, k, bank[0][:, :], gx(k), k == 0, k == DC - 1)
                if half == 1:
                    mm.then_inc(unit_done, 1)

            pe.wait_ge(sem("xs_copied"), 8)
            pe.wait_ge(sem("xbc_silu"), 16)
            pe.wait_ge(sem("cum_read"), 1)
            pe.wait_ge(sem("token_free"), 8)
            for n in range(TT * SG + 1):
                if n < TT * SG:
                    ssd_front(n)
                    q_half(n)
                if n > 0:
                    ssd_back(n - 1)

            def turn_y(j):
                if j == 0:
                    pe.wait_ge(sem("y_norm"), TT * SG)
                wait(pe, sem("ys_lo"), j - 1)
                for t in range(TT):
                    mm = nc.tensor.transpose(bank[6 + j % 2][:, t * P:(t + 1) * P],
                                             z_tok[:, t, j * P:(j + 1) * P], ident)
                mm.then_inc(sem("ys_turned"), 1)

            pe.wait_ge(tile_free, TILE0["k"])
            tiles("k", gx, DC, 4)
            for g in range(2):
                token_group("v", g, (gx_hi, gx_lo), TT, 8 + 4 * g, between=turn_y)
            pe.wait_ge(sem("token_free"), 16)
            pe.wait_ge(tile_free, TILE0["mix_ssd"])

            def ssd_half(h, half):
                if half == 0:
                    pe.wait_ge(unit_lo, UNIT0["mix_ssd"] + h + 1)
                    pe.wait_ge(sem("bias_ready"), min(h + 2, AH))
                    pe.wait_ge(tile_free, TILE0["mix_ssd"] + h)
                for k in range(4 * half, 4 * half + 4):
                    mm = products((UNIT0["mix_ssd"] + h) % RING, k, bank[1][:, :], (ys_hi[:, k, :], ys_lo[:, k, :]),
                                  k == 0, k == DC - 1)
                if half == 1:
                    mm.then_inc(unit_done, 1)

            def score(h, i, c):
                n = h * 8 + i * 2 + c
                wait(pe, sem("score_read"), n - 2)
                hp = slice(c * 64, c * 64 + 64)
                nc.tensor.matmul(bank[2 + n % 3][:, 0:(i + 1) * P], q_T[hp, h, i * P:(i + 1) * P],
                                 k_T[hp, h, 0:(i + 1) * P], start=True, stop=True).then_inc(sem("score"), 1)

            def turn(h):
                pe.wait_ge(sem("diffed"), h + 1)
                if h > 0:
                    pe.wait_ge(sem("wT_dve"), 2 * h)
                    pe.wait_ge(sem("wT_act"), h)
                for j in range(TT):
                    for i in range(j, TT):
                        base = 2 * P * (j == 3)
                        mm = nc.tensor.transpose(
                            bank[5 + min(j, 2)][:, base + (i - j) * P:base + (i - j + 1) * P],
                            prob[:, h % 2, 0, P * (i * (i + 1) // 2 + j):P * (i * (i + 1) // 2 + j + 1)], ident)
                mm.then_inc(sem("turned"), 1)

            def values(h):
                pe.wait_ge(sem("wT_dve"), 2 * (h + 1))
                pe.wait_ge(sem("wT_act"), h + 1)
                wait(pe, sem("o_copied"), h)
                off = 0
                for j in range(TT):
                    w = S - j * P
                    mm = nc.tensor.matmul(bank[0][:, j * P:S], v_tok[:, j, h * AV:(h + 1) * AV],
                                          w_T[:, off:off + w], start=(j == 0), stop=(j == TT - 1),
                                          skip_group_check=True)
                    off += w
                mm.then_inc(sem("o_mm"), 1)

            def head_stat(h):
                pe.wait_ge(sem("o_squared"), h + 1)
                for t in range(TT):
                    mm = nc.tensor.matmul(bank[7][:, 384 + h * TT + t:385 + h * TT + t], o_sq[:, t * P:(t + 1) * P],
                                          ones[:, 0:1], start=True, stop=True)
                mm.then_inc(sem("o_stat"), 1)

            def flip_bias(h):
                pe.wait_ge(sem(f"bias_in{h % 2}"), 16 * (h // 2 + 1))
                wait(pe, sem("bias_ready"), h)
                if h > 1:
                    pe.wait_ge(tile_free, TILE0["mix_ssd"] + h - 1)
                nc.tensor.matmul(bank[1][:, :], flip, bflip[h % 2][:, :], start=True, stop=True)\
                  .then_inc(sem("bias_flip"), 1)

            flip_bias(0)
            for h in range(AH + 2):
                if h < AH:
                    for n in range(3):
                        score(h, n // 2, n % 2)
                if h + 1 < AH:
                    flip_bias(h + 1)
                if h < AH - 1:
                    ssd_half(h, 0)
                elif h == AH:
                    ssd_half(AH - 1, 0)
                    ssd_half(AH - 1, 1)
                if 0 < h <= AH:
                    turn(h - 1)
                if h < AH:
                    for n in range(3, 8):
                        score(h, n // 2, n % 2)
                    if h < AH - 1:
                        ssd_half(h, 1)
                if 0 < h <= AH:
                    values(h - 1)
                if h > 1:
                    head_stat(h - 2)
            pe.wait_ge(sem("o_col"), 1)

            def factor_row(h):
                wait(pe, sem("o_nrmd"), h - 3)
                for t in range(TT):
                    mm = nc.tensor.matmul(bank[4 + h % 4][:, t * P:(t + 1) * P],
                                          o_rstd[:, h * TT + t:h * TT + t + 1].to_broadcast([P, P]), ident,
                                          start=True, stop=True)
                mm.then_inc(sem("o_row"), 1)

            def head_ready(k):
                pe.wait_ge(sem("o_lo"), k + 1)
                if k + 4 < AH:
                    factor_row(k + 4)
            for h in range(4):
                factor_row(h)
            tiles("mix_attn", lambda k: (o_hi[:, k, :], o_lo[:, k, :]), DC, 4, peel=1, banks=4, together=3,
                  ready=head_ready)
            def m_stat():
                pe.wait_ge(sem("m_sum"), DC + 1)
                for t in range(MT):
                    mm = nc.tensor.matmul(bank[6][:, t:t + 1], m_sum[:, t * P:(t + 1) * P], ones[:, 0:1],
                                          start=True, stop=True)
                mm.then_inc(sem("m_stat"), 1)

            def m_rows():
                pe.wait_ge(sem("m_col"), 1)
                for t in range(MT):
                    mm = nc.tensor.matmul(bank[6][:, t * P:(t + 1) * P], m_rstd[:, t:t + 1].to_broadcast([P, P]),
                                          ident, start=True, stop=True)
                mm.then_inc(sem("m_rowed"), 1)
            tiles("ck", lambda k: (m_hi[:, k, :], m_lo[:, k, :]), DC, 4, peel=1, n=ML,
                  ready=lambda k: pe.wait_ge(sem("m_lo"), k + 1),
                  hooks=(((0, 7), m_stat), ((1, 7), m_rows)))
            for g in range(2):
                token_group("cv", g, (m_hi, m_lo), MT, 16 + 2 * g)
            tiles("cq", gx, DC, 4, peel=1, ready=gx_ready("mix_attn"), hooks=norm_hooks("n_cross", "mix_attn"))
            pe.wait_ge(tile_free, TILE0["co"])
            pe.wait_ge(sem("token_free"), 20)

            def x_score(n):
                hd, i = n // TT, n % TT
                wait(pe, sem("x_exp"), n - 2)
                for e in range(2):
                    mm = nc.tensor.matmul(bank[2 + n % 3][:, 0:ML], qx_T[:, 2 * hd + e, i * P:(i + 1) * P],
                                          kx_T[:, 2 * hd + e, :], start=(e == 0), stop=(e == 1))
                mm.then_inc(sem("x_score"), 1)

            def x_turn(n):
                hd, i = n // TT, n % TT
                pe.wait_ge(sem("x_prob"), n + 1)
                if i == 0:
                    wait(pe, sem("x_pT"), 2 * hd)
                for kk in range(MT):
                    mm = nc.tensor.transpose(bank[5 + kk][:, i * P:(i + 1) * P],
                                             px[:, n % 4, kk * P:(kk + 1) * P], ident)
                mm.then_inc(sem("x_turned"), 1)

            def x_values(hd):
                pe.wait_ge(sem("x_pT"), 2 * (hd + 1))
                for e in range(2):
                    wait(pe, sem("ox_lo"), 2 * hd + e - 1)
                    for kk in range(MT):
                        mm = nc.tensor.matmul(bank[7 - 6 * e][:, :], vx[:, kk, hd * 256 + e * P:hd * 256 + (e + 1) * P],
                                              pxT[:, kk, :], start=(kk == 0), stop=(kk == MT - 1))
                    mm.then_inc(sem("ox_mm"), 1)

            for n in range(XH * TT + 4):
                if n < XH * TT:
                    x_score(n)
                if 2 <= n < XH * TT + 2:
                    x_turn(n - 2)
                if n > 3 and (n - 4) % TT == TT - 1:
                    x_values((n - 4) // TT)
            tiles("co", lambda k: (ox_hi[:, k, :], ox_lo[:, k, :]), DC, 4, peel=1,
                  ready=lambda k: pe.wait_ge(sem("ox_lo"), k + 1))
            ffn("ffn2", "n_ffn2", "co")
            tiles("qk2", gx, DC, 4, peel=1, ready=gx_ready("ffn2_out"), hooks=norm_hooks("n_fin", "ffn2_out", 2))
            token_group("v2", 0, (gx_hi, gx_lo), TT, 20)
            tiles("conv2", gx, DC, 12)
            tiles("gates2", gx, DC, 4)
            pe.wait_ge(sem("token_free"), 24)
            pe.wait_ge(tile_free, TILE0["branch2"])

            place = {0: (0, 0), 1: (1, 0), 3: (1, 3 * P), 2: (2, 0)}

            def st(buf, b, j):
                o = S * place[j][0] + place[j][1]
                return buf[b][:, o:o + S - j * P]

            def scores_into(first_bank, h, j, stop):
                hp = slice(h % 2 * 64, h % 2 * 64 + 64)
                bk, o = place[j]
                return nc.tensor.matmul(bank[first_bank + bk][:, o:o + S - j * P], k2_T[hp, h // 2, j * P:(j + 1) * P],
                                        q2_T[hp, h // 2, j * P:S], start=True, stop=stop)

            def stick_z(h):
                for bk, js in enumerate(((0,), (1, 3), (2,))):
                    wait(pe, sem("sp_ready"), 3 * (h - 1) + bk + 1)
                    for j in js:
                        mm = scores_into(2, h, j, True)
                    mm.then_inc(sem("z_mm"), 1)

            def stick_c(h):
                pe.wait_ge(sem("sp_masked"), h + 1)
                wait(pe, sem("w_exp"), h)
                for j in (0, 1, 3, 2):
                    scores_into(5, h, j, False)
                    bk, o = place[j]
                    dst = bank[5 + bk]
                    for jj in range(j + 1, TT):
                        nc.tensor.matmul(dst[:, o + (jj - j) * P:o + S - j * P], neg_ones,
                                         st(sp_buf, h % 2, jj), start=False, stop=False)
                    mm = nc.tensor.matmul(dst[:, o:o + S - j * P], neg_ge, st(sp_buf, h % 2, j),
                                          start=False, stop=True)
                mm.then_inc(sem("c_mm"), 1)

            def stick_values(h):
                pe.wait_ge(sem("w_masked"), h + 1)
                if h >= 4 and h % 2 == 0:
                    pe.wait_ge(sem("o2_lo"), h // 2 - 1)
                rows_ = slice(h % 2 * 64, h % 2 * 64 + 64)
                for j in range(TT):
                    mm = nc.tensor.matmul(bank[h // 2 % 2][rows_, j * P:S], v2_tok[:, j, h * 64:(h + 1) * 64],
                                          st(w_buf, h % 2, j), start=(j == 0), stop=(j == TT - 1),
                                          skip_group_check=True)
                mm.then_inc(sem("o2_mm"), 1)

            for h in range(KH + 2):
                if h < KH:
                    stick_z(h)
                if 0 < h <= KH:
                    stick_c(h - 1)
                if h > 1:
                    stick_values(h - 2)

            pe.wait_ge(sem("o2_lo"), 4)
            pe.wait_ge(sem("cv_lo"), 4)
            with pe.Fori(0, 2) as i:
                for j in range(4):
                    pe.wait_ge(unit_lo, UNIT0["branch2"] + i * 4 + (j + 1))
                    pe.wait_ge(tile_free, i * 8 + (TILE0["branch2"] + 2 * j - 2))
                    for half, (h_, l_) in enumerate(((o2_hi, o2_lo), (cv_hi, cv_lo))):
                        for k in range(4):
                            mm = products(j, half * 4 + k, bank[2 * (j % 2) + half][:, :], (h_[:, k, :], l_[:, k, :]),
                                          k == 0, k == 3)
                    mm.then_inc(unit_done, 1)
            tiles("o2", gx, DC, 4, peel=1, ready=gx_ready("branch2"))
            def boundary(name, summed):
                for _, h in norm_hooks(name, summed):
                    h()
            boundary("n_post", "o2")
            tiles("up_a", gx, DC, 4, peel=1, ready=gx_ready("post"),
                  hooks=norm_hooks("n_mlp", "post", together=3), banks=4, together=3)
            up = lambda k: (up_hi[:, k, :], up_lo[:, k, :])

            def up_ready(half):
                def f(k):
                    if k % UC == 0:
                        pe.wait_ge(sem("up_lo"), half * HC + k + UC)
                return f
            tiles("down_a", up, HC, 4, peel=1, ready=up_ready(0))
            pe.wait_ge(tile_free, TILE0["up_b"])
            tiles("up_b", gx, DC, 4, banks=4)
            tiles("down_b", up, HC, 4, peel=1, ready=up_ready(1))
            pe.wait_ge(sem("p_lo"), 2)
            pe.wait_ge(tile_free, TILE0["proj2"])

            def project(j):
                pe.wait_ge(unit_lo, UNIT0["proj2"] + j + 1)
                pe.wait_ge(tile_free, TILE0["proj2"] + max(0, 2 * j - 2))
                for t in range(2):
                    for k in range(2):
                        mm = products(j, t * 2 + k, bank[2 * (j % 2) + t][:, :], (p_hi[:, k, :], p_lo[:, k, :]),
                                      k == 0, k == 1)
                mm.then_inc(unit_done, 1)
            (_, stat), (_, row) = norm_hooks("n_pmlp", "down")
            project(0)
            project(1)
            stat()
            project(2)
            project(3)
            row()
            tiles("ple2", gx, DC, 4, peel=1, ready=gx_ready("pmlp"),
                  hooks=norm_hooks("n_ple", "pmlp", together=3), banks=4, together=3)

        @block.scalar
        def _(act):
            chain = [0]

            def link(ins):
                chain[0] += 1
                ins.then_inc(sem("act_chain"), 1)
                act.wait_ge(sem("act_chain"), chain[0])

            def round_unit(v, j):
                if isinstance(v, int) and v >= UNITS:
                    return
                if isinstance(v, int):
                    act.wait_ge(unit_raw[j], 16 * (v // RING + 1))
                else:
                    act.wait_ge(unit_raw[j], v[1])
                    v = v[0]
                wait(act, unit_done, v - RING + 1)
                nc.scalar.copy(w_hi[:, j, :], w_raw[:, j, :]).then_inc(unit_hi, 1)

            def ahead(stage, i, per_block, j):
                u = UNIT0[stage] + j + RING - 1
                if isinstance(i, int):
                    round_unit(u + i * per_block, u % RING)
                else:
                    round_unit((i * per_block + u, i * (per_block // RING * 16) + 16 * (u // RING + 1)), u % RING)

            def norm(name, stats=1, width=D):
                act.wait_ge(norm_sem("stat"), norm_count("stat", name, 1))
                if stats == 1:
                    ins = nc.scalar.activation(root_col[:, 0:TT], bank[7][:, 0:TT], ACT.Sqrt, bias=eps_col[:, :],
                                               scale=1.0 / width)
                else:
                    ins = nc.scalar.activation(root_col[:, :], bank[7][:, 0:2 * TT], ACT.Copy, scale=1.0 / width)
                ins.then_inc(norm_sem("root"), 1)

            def next_operand(stage, weight, m):
                act.wait_ge(tile_free, TILE0[stage] + m + 1)
                act.wait_ge(sem("summed"), sum_count(stage, m + 1))
                nc.scalar.activation(square[:, :], tile_of(x, m), ACT.Square).then_inc(sem("squared"), 1)
                nc.scalar.activation(tile_of(gx_hi, m), tile_of(x, m), ACT.Copy, scale=col_at(weight, m))\
                  .then_inc(sem("gx_hi_done"), 1)

            def residual_stage(stage, weight, per, body=4, peel=0, beside=None):
                def block_of(i):
                    for j in range(body):
                        for uu in range(per):
                            ahead(stage, i, body * per, j * per + uu)
                        m = i * body + j
                        next_operand(stage, weight, m)
                        if beside:
                            beside(m)
                blocks(act, 8 // body, block_of, peel)

            def just_round(stage, per_block=4):
                def block_of(i):
                    for j in range(per_block):
                        ahead(stage, i, per_block, j)
                blocks(act, dict(STAGES)[stage] // per_block, block_of)

            def token_evac(stage, g, dst, scale, n_tiles, func, factor, between=None):
                act.wait_ge(*factor)
                for u in range(4):
                    ahead(stage, 0, 4, 4 * g + u)
                    if between:
                        between(4 * g + u)
                act.wait_ge(unit_done, UNIT0[stage] + 4 * g + 4)
                for t in range(n_tiles):
                    nc.scalar.activation(dst[:, t, g * S:(g + 1) * S], bank[2 + t][:, :], func,
                                         scale=scale[:, t:t + 1]).then_inc(sem("token_free"), 1)

            def ffn(name, norm_name, weight):
                def block_of(i):
                    for j in range(2):
                        c = i * 2 + j
                        if not (first(i) and j == 1):
                            ahead(f"{name}_in", i, 4, 2 * j)
                        if first(i) and j == 0:
                            norm(norm_name)
                            for uu in (1, 2):
                                ahead(f"{name}_in", i, 4, uu)
                        act.wait_ge(tile_free, TILE0[f"{name}_in"] + c * 2 + 1)
                        nc.scalar.activation(ff_silu[:, :], ff_gate[:, :], ACT.Silu).then_inc(sem("ffn_silu"), 1)
                        if not (first(i) and j == 0):
                            ahead(f"{name}_in", i, 4, 2 * j + 1)
                        act.wait_ge(sem("ffn_act"), ffn_count(name, c + 1))
                        nc.scalar.copy(tile_of(ff_hi, c), ff_act[:, :]).then_inc(sem("ffn_act_hi"), 1)
                blocks(act, FC // 2, block_of, peel=1)
                residual_stage(f"{name}_out", weight, 3) if name == "ffn1" else final_residual()

            def final_residual():
                def block_of(i):
                    for j in range(4):
                        for uu in range(3):
                            ahead("ffn2_out", i, 12, 3 * j + uu)
                        m = i * 4 + j
                        act.wait_ge(tile_free, TILE0["ffn2_out"] + m + 1)
                        act.wait_ge(sem("summed"), sum_count("ffn2_out", m + 1))
                        nc.scalar.activation(square[:, :], tile_of(x, m), ACT.Square)\
                          .then_inc(sem("squared"), 1)
                        act.wait_ge(sem("xw_ready"), m + 1)
                        nc.scalar.activation(tile_of(gx_hi, m), tile_of(x, m), ACT.Copy,
                                             scale=col_at("g_pre_mix_2", m)).then_inc(sem("gx_hi_done"), 1)
                        nc.scalar.activation(square2[:, :], tile_of(x, m), ACT.Square)\
                          .then_inc(sem("squared2"), 1)
                blocks(act, 2, block_of)

            for dst, src in ((relb[0:32, :], relb_d), (onehot[0:32, :], onehot_d), (pen[0:AH, :], pen_d),
                             (cols[:, :], cols_d)):
                act.dma_start(dst, src).then_inc(sem("small_in"), 16)
            for half in range(2):
                ms = slice(4 * half, 4 * half + 4)
                act.dma_start(x[:, ms, :], xT.rearrange("(m p) s -> p m s", p=P)[:, ms, :])\
                   .then_inc(sem(f"x_in{half}"), 16)
            for dst, src in ((consts[:, :], consts_d), (wdt[:, :, :], wdt_d),
                             (rows[:, :], bass.AP(rows_d.tensor, 0, [[0, P], [1, NROWS]]))):
                act.dma_start(dst, src).then_inc(sem("setup_in"), 16)
            for v in range(RING - 2):
                round_unit(v, v)
            act.wait_ge(sem("brow_ready"), 2)
            act.dma_start(bias_r, brow[0:AH, :]).then_inc(sem("brow_out"), 16)
            for m in range(DC):
                if m % 4 == 0:
                    act.wait_ge(sem(f"x_in{m // 4}"), 16)
                if m == 1:
                    round_unit(RING - 2, RING - 2)
                act.wait_ge(sem("summed"), sum_count("load", m + 1))
                nc.scalar.activation(square[:, :], x[:, m, :], ACT.Square).then_inc(sem("squared"), 1)
                nc.scalar.activation(gx_hi[:, m, :], x[:, m, :], ACT.Copy, scale=col("norm_ffn1_w", m))\
                  .then_inc(sem("gx_hi_done"), 1)
            act.wait_ge(sem("setup_in"), 16 * 3)
            nc.scalar.copy(wdt_hi[:, :, :], wdt[:, :, :]).then_inc(sem("wdt_hi"), 1)
            act.wait_ge(sem("brow_out"), 16)

            ffn("ffn1", "n_ffn1", "norm_mix_w")

            def xbc(x_part):
                def block_of(i):
                    for j in range(4):
                        c = i * 4 + j
                        ahead("xbc", i, 4, j)
                        if first(i) and j == 0:
                            norm("n_mix")
                        act.wait_ge(sem("xbc_conv"), c * 4 + 4)
                        dst = tile_of(xs_T, c) if x_part else tile_of(bc, c - 8)
                        nc.scalar.activation(dst, conv_acc[:, :], ACT.Silu).then_inc(sem("xbc_silu"), 1)
                return block_of
            for i in range(2):
                xbc(True)(i)
            with act.Fori(2, 4) as i:
                xbc(False)(i)
            z_factor = (norm_sem("col"), norm_count("col", "n_mix", 1))
            token_evac("z", 0, z_tok, rstd_col, TT, ACT.Silu, z_factor)
            act.wait_ge(sem("dt_clamped"), 1)
            nc.scalar.activation(dt_exp[:, :, :], dt_exp[:, :, :], ACT.Exp).then_inc(sem("dt_exped"), 1)
            act.wait_ge(sem("dt_exped"), 1)
            nc.scalar.activation(dt_ln[:, :, :], dt_exp[:, :, :], ACT.Ln, bias=1.0).then_inc(sem("dt_lned"), 1)
            nc.scalar.activation(a_row[:, :], rows[:, ROWS["a_log"]:ROWS["a_log"] + SH], ACT.Exp)\
              .then_inc(sem("a_exp"), 1)
            token_evac("z", 1, z_tok, rstd_col, TT, ACT.Silu, z_factor)
            act.wait_ge(sem("cum_read"), 1)
            nc.scalar.activation(ecum[:, :, :], cum[:, :, :], ACT.Exp).then_inc(sem("decay_exp"), 1)
            nc.scalar.activation(e_end[:, :, :], to_end[:, :, :], ACT.Exp).then_inc(sem("decay_exp"), 1)
            nc.scalar.activation(c_dec[:, :, :], c_dec[:, :, :], ACT.Exp).then_inc(sem("decay_exp"), 1)
            for n in range(TT * SG + 2):
                if n < TT * SG:
                    t, g, b = n // SG, n % SG, n % 2
                    if n % 2 == 1:
                        ahead("q", 0, 4, n // 2)
                    act.wait_ge(sem("cell_b"), n + 1)
                    wait(act, sem("cell_m"), n - 1)
                    for r in range(GH):
                        h = g * GH + r
                        ins = nc.scalar.activation(seg[:, b, r, :], bank[2 + b][:, r * P:(r + 1) * P], ACT.Relu,
                                                   bias=cum[:, t, h:h + 1], scale=-1.0)
                    link(ins)
                    nc.scalar.activation(decay[:, b, :, :], seg[:, b, :, :], ACT.Exp, scale=-1.0)\
                      .then_inc(sem("decayed"), 1)
                if n > 1:
                    t, g = (n - 2) // SG, (n - 2) % SG
                    act.wait_ge(sem("cell_done"), n - 1)
                    wait(act, sem("y_squared"), n - 2)
                    nc.scalar.activation(ysq_tmp[:, :], z_tok[:, t, g * 256:(g + 1) * 256], ACT.Square,
                                         accum_out=y_sq[:, n - 2:n - 1]).then_inc(sem("y_squared"), 1)
            act.wait_ge(sem("y_squared"), TT * SG)
            nc.scalar.activation(y_root[:, :], y_sq[:, :], ACT.Sqrt, bias=eps_col[:, :], scale=1.0 / 256)\
              .then_inc(sem("y_rooted"), 1)
            def load_bias(h):
                act.dma_start(bflip[h % 2][:, :], bass.AP(bias_r.tensor, h * (BIAS_W + 1), [[1, P], [1, S]]))\
                   .then_inc(sem(f"bias_in{h % 2}"), 16)
            act.wait_ge(sem("summed"), sum_count("ffn1_out", DC + 1))
            load_bias(0)
            load_bias(1)
            just_round("k")
            v_factor = (norm_sem("col"), norm_count("col", "n_mix", 1))

            def round_y(j):
                act.wait_ge(sem("ys_turned"), j + 1)
                nc.scalar.activation(ys_hi[:, j, :], bank[6 + j % 2][:, :], ACT.Copy,
                                     scale=col("ssd_norm_w", j)).then_inc(sem("ys_hi"), 1)
            for g in range(2):
                token_evac("v", g, v_tok, rstd_col, TT, ACT.Copy, v_factor, between=round_y)
            act.wait_ge(sem("lam_dots"), 2)
            nc.scalar.activation(lam[:, 2:4], lam[:, 0:2], ACT.Exp).then_inc(sem("lam_exp"), 1)
            act.wait_ge(unit_done, UNIT0["mix_ssd"])

            def copy_bias(h):
                act.wait_ge(sem("bias_flip"), h + 1)
                if h >= 2:
                    act.wait_ge(sem("score_read"), 8 * (h - 1))
                nc.scalar.copy(bias_h[:, h % 2, :], bank[1][:, :]).then_inc(sem("bias_ready"), 1)

            copy_bias(0)

            def exps(h, n0, n1):
                for n in range(n0, n1):
                    i, c = n // 2, n % 2
                    act.wait_ge(sem("score_read"), h * 8 + n + 1)
                    seg = prob[:, h % 2, c, P * (i * (i + 1) // 2):P * ((i + 1) * (i + 2) // 2)]
                    nc.scalar.activation(seg, seg, ACT.Exp, bias=amin[:, h % 2, c * 4 + i:c * 4 + i + 1], scale=-1.0,
                                         accum_out=rsum[:, h % 2, c * 4 + i:c * 4 + i + 1])\
                      .then_inc(sem("exped"), 1)

            for h in range(AH + 1):
                if h < AH:
                    exps(h, 0, 3)
                if h + 1 < AH:
                    copy_bias(h + 1)
                if h > 0:
                    act.wait_ge(sem("turned"), h)
                    wait(act, sem("o_mm"), h - 1)
                    nc.scalar.copy(w_T[:, 0:S], bank[5][:, :]).then_inc(sem("wT_act"), 1)
                if h + 2 < AH:
                    load_bias(h + 2)
                if h < AH:
                    ahead("mix_ssd", 0, 4, h)
                    exps(h, 3, 8)
                if h > 0:
                    act.wait_ge(sem("o_copied"), h)
                    wait(act, sem("o_stat"), h - 1)
                    nc.scalar.activation(o_sq[:, :], o_un[:, h - 1, :], ACT.Square).then_inc(sem("o_squared"), 1)
            act.wait_ge(unit_done, UNIT0["mix_attn"])
            act.dma_start(m_T[:, :, :], memT.rearrange("(m p) s -> p m s", p=P)).then_inc(sem("m_in"), 16)
            act.wait_ge(sem("o_stat"), AH)
            nc.scalar.activation(o_root[:, :], bank[7][:, 384:384 + TT * AH], ACT.Sqrt, bias=eps_col[:, :],
                                 scale=1.0 / AV)\
              .then_inc(sem("o_rooted"), 1)
            for h in range(AH):
                act.wait_ge(sem("o_nrmd"), h + 1)
                nc.scalar.copy(o_hi[:, h, :], o_nrm[:, h % 2, :]).then_inc(sem("o_hi"), 1)

            def memory_tile(m):
                if m == 0:
                    act.wait_ge(sem("m_in"), 16)
                act.wait_ge(sem("m_sum"), m + 1)
                nc.scalar.activation(m_sq[:, :], m_T[:, m, :], ACT.Square).then_inc(sem("m_square"), 1)
                nc.scalar.activation(m_hi[:, m, :], m_T[:, m, :], ACT.Copy, scale=col("norm_mem_w", m))\
                  .then_inc(sem("m_hi"), 1)
            residual_stage("mix_attn", "norm_cross_w", 1, body=8, peel=1, beside=memory_tile)
            act.wait_ge(sem("m_stat"), 1)
            nc.scalar.activation(m_root[:, :], bank[6][:, 0:MT], ACT.Sqrt, bias=eps_col[:, :], scale=1.0 / D)\
              .then_inc(sem("m_root"), 1)
            just_round("ck")
            act.wait_ge(sem("m_col"), 1)
            for g in range(2):
                token_evac("cv", g, vx, m_rstd, MT, ACT.Copy, (sem("m_col"), 1))
            for j in range(8):
                ahead("cq", 0, 4, j)
                if j == 0:
                    norm("n_cross")
            for n in range(XH * TT + 4):
                if n < XH * TT:
                    act.wait_ge(sem("x_min"), n + 1)
                    wait(act, sem("x_turned"), n - 3)
                    nc.scalar.activation(px[:, n % 4, :], bank[2 + n % 3][:, 0:ML], ACT.Exp,
                                         bias=xmin[:, n:n + 1], scale=-1.0, accum_out=xsum[:, n:n + 1])\
                      .then_inc(sem("x_exp"), 1)
                if n > 3 and (n - 4) % TT == TT - 1:
                    for e in range(2):
                        c = 2 * ((n - 4) // TT) + e
                        act.wait_ge(sem("ox_mm"), c + 1)
                        nc.scalar.copy(ox_hi[:, c, :], bank[7 - 6 * e][:, :]).then_inc(sem("ox_hi"), 1)
            residual_stage("co", "norm_ffn2_w", 1)
            ffn("ffn2", "n_ffn2", None)
            ahead("qk2", 0, 4, 0)
            norm("n_fin", 2)
            act.wait_ge(sem("n_fin_var"), 1)
            nc.scalar.activation(fin[:, 16:20], fin[:, 0:4], ACT.Sqrt, bias=eps_col[:, :])\
              .then_inc(norm_sem("root"), 1)
            nc.scalar.activation(fin[:, 20:24], fin[:, 8:12], ACT.Sqrt).then_inc(norm_sem("root"), 1)
            for j in range(1, 8):
                ahead("qk2", 0, 4, j)
            token_evac("v2", 0, v2_tok, rstd_col, TT, ACT.Copy, (norm_sem("col"), norm_count("col", "n_fin", 1)))
            for c in range(4):
                for j in range(3):
                    ahead("conv2", 0, 12, 3 * c + j)
                act.wait_ge(sem("cv_out"), c + 1)
                nc.scalar.copy(cv_hi[:, c, :], cacc[:, :]).then_inc(sem("cv_hi"), 1)

            def gate_block(i):
                for j in range(4):
                    c = i * 4 + j
                    ahead("gates2", i, 4, j)
                    act.wait_ge(tile_free, TILE0["gates2"] + c + 1)
                    nc.scalar.activation(tile_of(gates, c), gate_t[:, :], ACT.Sigmoid,
                                         bias=col_at("b_gate_2", c)).then_inc(sem("gate_sig"), 1)
            blocks(act, 4, gate_block)
            for h in range(KH + 2):
                if h < KH:
                    for bk, z in enumerate(by_bank(sz_buf[h % 2])):
                        act.wait_ge(sem("z_clamped"), 3 * h + bk + 1)
                        nc.scalar.activation(z, z, ACT.Exp).then_inc(sem("z_exped"), 1)
                    for bk, z in enumerate(by_bank(sz_buf[h % 2])):
                        act.wait_ge(sem("z_exped"), 3 * h + bk + 1)
                        nc.scalar.activation(z, z, ACT.Ln, bias=1.0).then_inc(sem("sp_lned"), 1)
                if 0 < h <= KH:
                    act.wait_ge(sem("c_mm"), h)
                    wait(act, sem("o2_mm"), h - 2)
                    for bk in range(3):
                        n = S if bk < 2 else 2 * P
                        ins = nc.scalar.activation(w_buf[(h - 1) % 2][:, bk * S:bk * S + n], bank[5 + bk][:, 0:n],
                                                   ACT.Exp)
                    ins.then_inc(sem("w_exp"), 1)
                if h > 1 and h % 2 == 1:
                    act.wait_ge(sem("o2_mm"), h - 1)
                    c = (h - 2) // 2
                    nc.scalar.copy(o2_hi[:, c, :], bank[c % 2][:, :]).then_inc(sem("o2_hi"), 1)
            act.wait_ge(sem("sp_masked"), KH)
            with act.Fori(0, 2) as i:
                for j in range(4):
                    ahead("branch2", i, 4, j)
                    c = i * 4 + j
                    act.wait_ge(sem("mixed"), c + 1)
                    nc.scalar.copy(tile_of(gx_hi, c), br_m[:, :]).then_inc(sem("gx_hi_done"), 1)

            def o2_block(i):
                for j in range(4):
                    ahead("o2", i, 4, j)
                    m = i * 4 + j
                    act.wait_ge(tile_free, TILE0["o2"] + m + 1)
                    act.wait_ge(sem("summed"), sum_count("o2", m + 1))
                    nc.scalar.activation(square[:, :], tile_of(y_o2, m), ACT.Square)\
                      .then_inc(sem("squared"), 1)
            blocks(act, 2, o2_block)
            def post(name, weight):
                for m in range(DC):
                    act.wait_ge(sem(f"{name}_x"), m + 1)
                    nc.scalar.activation(gx_hi[:, m, :], x[:, m, :], ACT.Copy, scale=col(weight, m))\
                      .then_inc(sem("gx_hi_done"), 1)
                    nc.scalar.activation(post_sq[:, m, :], x[:, m, :], ACT.Square).then_inc(sem("squared"), 1)
            norm("n_post")
            post("post", "g_pre_mlp_2")

            def up_stage(stage, half):
                def block_of(i):
                    for j in range(4):
                        c = i * 4 + j
                        if not (first(i) and half == 0 and j in (1, 2)):
                            ahead(stage, i, 4, j)
                        if first(i) and j == 0 and half == 0:
                            norm("n_mlp")
                            for uu in (1, 2):
                                ahead(stage, i, 4, uu)
                        act.wait_ge(sem("up_act"), half * HC + c + 1)
                        nc.scalar.copy(tile_of(up_hi, c), up_a[:, :]).then_inc(sem("up_hi"), 1)
                blocks(act, 4, block_of, peel=1 - half)
            up_stage("up_a", 0)
            just_round("down_a", 8)
            act.dma_start(p_T[:, :, :], pT.rearrange("(m p) s -> p m s", p=P)).then_inc(sem("p_in"), 16)
            up_stage("up_b", 1)
            act.wait_ge(sem("p_in"), 16)
            for k in range(2):
                nc.scalar.copy(p_hi[:, k, :], p_T[:, k, :]).then_inc(sem("p_hi"), 1)

            def down_block(i):
                for j in range(4):
                    m = i * 4 + j
                    ahead("down_b", i, 8, 2 * j)
                    ahead("down_b", i, 8, 2 * j + 1)
                    act.wait_ge(tile_free, TILE0["down_b"] + m + 1)
                    act.wait_ge(sem("summed"), sum_count("down", m + 1))
                    nc.scalar.activation(square[:, :], tile_of(f_acc, m), ACT.Square)\
                      .then_inc(sem("squared"), 1)
            blocks(act, 2, down_block)
            for j in range(3):
                ahead("proj2", 0, 4, j)
            norm("n_pmlp")
            ahead("proj2", 0, 4, 3)
            post("pmlp", "g_ple_2")
            for m in range(DC):
                if m not in (1, 2):
                    ahead("ple2", 0, 4, m)
                if m == 0:
                    norm("n_ple")
                    ahead("ple2", 0, 4, 1)
                    ahead("ple2", 0, 4, 2)
                act.wait_ge(tile_free, TILE0["ple2"] + m + 1)
                nc.scalar.activation(ple_g[:, :], ple_t[:, :], ACT.Sigmoid).then_inc(sem("ple_sig"), 1)

        @block.vector
        def _(dve):
            chain = [0]

            def link(ins):
                chain[0] += 1
                ins.then_inc(sem("dve_chain"), 1)
                dve.wait_ge(sem("dve_chain"), chain[0])

            def norm(name):
                norm_column(name)
                norm_row(name)

            def norm_column(name):
                dve.wait_ge(norm_sem("root"), norm_count("root", name, 1))
                nc.vector.reciprocal(rstd_col[:, :], root_col[:, 0:TT]).then_inc(norm_sem("col"), 1)

            def norm_row(name):
                dve.wait_ge(norm_sem("row"), norm_count("row", name, 1))
                nc.vector.tensor_copy(rstd_row[:, :], bank[7][:, :]).then_inc(norm_sem("ready"), 1)
                dve.wait_ge(norm_sem("ready"), norm_count("ready", name, 1))

            def start_sums():
                nc.vector.memset(sumsq[:, :], 0.0).then_inc(sem("summed"), 1)

            def add_square(stage, m):
                dve.wait_ge(sem("squared"), square_count(stage, m + 1))
                dve.wait_ge(sem("summed"), sum_count(stage, m + 1))
                nc.vector.tensor_tensor(sumsq[:, :], sumsq[:, :], square[:, :], ALU.add).then_inc(sem("summed"), 1)

            def add_square2(m):
                dve.wait_ge(sem("squared2"), m + 1)
                dve.wait_ge(sem("summed2"), m + 1)
                nc.vector.tensor_tensor(sumsq2[:, :], sumsq2[:, :], square2[:, :], ALU.add)\
                  .then_inc(sem("summed2"), 1)

            def split_lo(stage, weight, m, src):
                dve.wait_ge(sem("gx_hi_done"), gx_count(stage, m + 1))
                nc.vector.scalar_tensor_tensor(out=tile_of(gx_lo, m), in0=tile_of(src, m),
                                               scalar=col_at(weight, m), in1=tile_of(gx_hi, m).bitcast(F32),
                                               op0=ALU.mult, op1=ALU.subtract).then_inc(sem("gx_lo_done"), 1)

            def residual_stage(stage, weight, per, alpha, body=4, peel=0, beside=None, banks=2):
                start_sums()

                def block_of(i):
                    for j in range(body):
                        m = i * body + j
                        dve.wait_ge(unit_done, UNIT0[stage] + m * per + per)
                        nc.vector.scalar_tensor_tensor(out=tile_of(x, m), in0=bank[j % banks][:, :], scalar=alpha,
                                                       in1=tile_of(x, m), op0=ALU.mult, op1=ALU.add)\
                          .then_inc(tile_free, 1)
                        add_square(stage, m)
                        split_lo(stage, weight, m, x)
                        if beside:
                            beside(m)
                blocks(dve, 8 // body, block_of, peel)

            def scaled_tiles(stage, dst, count, scale=None, body=4, row=None, first=0):
                def block_of(i):
                    for j in range(body):
                        c = i * body + j
                        dve.wait_ge(unit_done, UNIT0[stage] + first + c + 1)
                        src = bank[j % 2][:, 0:(row or rstd_row).shape[1]]
                        r = (row or rstd_row)[:, :]
                        if scale is None:
                            ins = nc.vector.tensor_tensor(tile_of(dst, c), src, r, ALU.mult)
                        else:
                            ins = nc.vector.scalar_tensor_tensor(out=tile_of(dst, c), in0=src, scalar=scale, in1=r,
                                                                 op0=ALU.mult, op1=ALU.mult)
                        ins.then_inc(tile_free, 1)
                blocks(dve, count // body, block_of)

            def ffn(name, norm_name, weight):
                def block_of(i):
                    for j in range(2):
                        c = i * 2 + j
                        T, U = TILE0[f"{name}_in"] + 2 * c, UNIT0[f"{name}_in"] + 2 * c
                        if first(i) and j == 0:
                            norm(norm_name)
                        dve.wait_ge(unit_done, U + 1)
                        nc.vector.tensor_tensor(ff_gate[:, :], bank[2 * j][:, :], rstd_row[:, :], ALU.mult)\
                          .then_inc(tile_free, 1)
                        dve.wait_ge(unit_done, U + 2)
                        nc.vector.tensor_tensor(ff_up[:, :], bank[2 * j + 1][:, :], rstd_row[:, :], ALU.mult)\
                          .then_inc(tile_free, 1)
                        dve.wait_ge(sem("ffn_silu"), ffn_count(name, c + 1))
                        dve.wait_ge(tile_free, T + 2)
                        nc.vector.tensor_tensor(ff_act[:, :], ff_silu[:, :], ff_up[:, :], ALU.mult)\
                          .then_inc(sem("ffn_act"), 1)
                        dve.wait_ge(sem("ffn_act_hi"), ffn_count(name, c + 1))
                        nc.vector.tensor_tensor(tile_of(ff_lo, c), ff_act[:, :],
                                                tile_of(ff_hi, c).bitcast(F32), ALU.subtract)\
                          .then_inc(sem("ffn_act_lo"), 1)
                blocks(dve, FC // 2, block_of, peel=1)
                if name == "ffn1":
                    residual_stage("ffn1_out", weight, 3, 0.5)
                    return
                start_sums()
                nc.vector.memset(sumsq2[:, :], 0.0).then_inc(sem("summed2"), 1)

                def out_block(i):
                    for j in range(4):
                        m = i * 4 + j
                        xm = tile_of(x, m)
                        dve.wait_ge(unit_done, UNIT0["ffn2_out"] + m * 3 + 3)
                        nc.vector.scalar_tensor_tensor(out=xm, in0=bank[j % 2][:, :], scalar=0.5, in1=xm,
                                                       op0=ALU.mult, op1=ALU.add).then_inc(tile_free, 1)
                        add_square("ffn2_out", m)
                        nc.vector.tensor_scalar(xm, xm, col_at("norm_final_w", m), None, ALU.mult)\
                          .then_inc(sem("xw_ready"), 1)
                        add_square2(m)
                        split_lo("ffn2_out", "g_pre_mix_2", m, x)
                blocks(dve, 2, out_block)

            def x_lo(hd):
                for e in range(2):
                    c = 2 * hd + e
                    dve.wait_ge(sem("ox_hi"), c + 1)
                    nc.vector.tensor_tensor(ox_lo[:, c, :], bank[7 - 6 * e][:, :], ox_hi[:, c, :].bitcast(F32),
                                            ALU.subtract)\
                      .then_inc(sem("ox_lo"), 1)

            nc.vector.memset(eps_col[:, :], EPS).then_inc(sem("eps_set"), 1)
            dve.wait_ge(sem("eps_set"), 1)
            dve.wait_ge(sem("small_in"), 16 * 4)
            dve.wait_ge(sem("brow_sum"), 1)
            nc.vector.tensor_tensor(brow[0:AH, 0:S], pen[0:AH, 0:S], bank[4][0:AH, :], ALU.subtract)\
              .then_inc(sem("brow_ready"), 1)
            nc.vector.tensor_tensor(brow[0:AH, S:S + P], pen[0:AH, S:S + P], bank[5][0:AH, 0:P], ALU.subtract)\
              .then_inc(sem("brow_ready"), 1)
            start_sums()
            for m in range(DC):
                if m % 4 == 0:
                    dve.wait_ge(sem(f"x_in{m // 4}"), 16)
                add_square("load", m)
                split_lo("load", "norm_ffn1_w", m, x)
            dve.wait_ge(sem("wdt_hi"), 1)
            nc.vector.tensor_tensor(wdt_lo[:, :, :], wdt[:, :, :], wdt_hi[:, :, :].bitcast(F32), ALU.subtract)\
              .then_inc(sem("wdt_lo"), 1)

            ffn("ffn1", "n_ffn1", "norm_mix_w")

            nc.vector.memset(conv_in[:, 0:3], 0.0).then_inc(sem("conv_pad"), 1)
            dve.wait_ge(sem("conv_pad"), 1)

            def conv_block(i):
                for j in range(4):
                    c = i * 4 + j
                    if first(i) and j == 0:
                        norm("n_mix")
                    dve.wait_ge(unit_done, UNIT0["xbc"] + c + 1)
                    wait(dve, sem("xbc_conv"), c * 4)
                    nc.vector.tensor_tensor(conv_in[:, 3:3 + S], bank[j % 2][:, :], rstd_row[:, :], ALU.mult)\
                      .then_inc(tile_free, 1)
                    dve.wait_ge(tile_free, TILE0["xbc"] + c + 1)
                    wait(dve, sem("xbc_silu"), c)
                    nc.vector.tensor_scalar(conv_acc[:, :], conv_in[:, 0:S], col_at("conv_w", c),
                                            col_at("conv_b", c), ALU.mult, ALU.add).then_inc(sem("xbc_conv"), 1)
                    for k in range(1, 4):
                        dve.wait_ge(sem("xbc_conv"), c * 4 + k)
                        nc.vector.scalar_tensor_tensor(out=conv_acc[:, :], in0=conv_in[:, k:k + S],
                                                       scalar=col_at("conv_w", c + 16 * k), in1=conv_acc[:, :],
                                                       op0=ALU.mult, op1=ALU.add).then_inc(sem("xbc_conv"), 1)
            blocks(dve, 4, conv_block, peel=1)
            dve.wait_ge(sem("setup_in"), 16 * 3)
            dve.wait_ge(sem("dt_mm"), 1)
            nc.vector.tensor_copy(dt_T[0:SH, :], bank[6][0:SH, :]).then_inc(sem("dt_copied"), 1)
            dve.wait_ge(sem("dt_turned"), 1)
            bias = rows[:, ROWS["dt_bias"]:ROWS["dt_bias"] + SH]
            for t in range(TT):
                ins = nc.vector.scalar_tensor_tensor(out=dt_pre[:, t, :], in0=bank[6][:, t * SH:(t + 1) * SH],
                                                     scalar=rstd_col[:, t:t + 1], in1=bias,
                                                     op0=ALU.mult, op1=ALU.add)
            link(ins)
            nc.vector.tensor_scalar(dt_exp[:, :, :], dt_pre[:, :, :], 40.0, None, ALU.min)\
              .then_inc(sem("dt_clamped"), 1)

            def copy_x(j):
                dve.wait_ge(sem("xs_turned"), j + 1)
                nc.vector.tensor_copy(xs_tok[:, :, j * P:(j + 1) * P],
                                      bank[j % 2][:, :].rearrange("p (t c) -> p t c", t=TT))\
                  .then_inc(sem("xs_copied"), 1)
            for j in range(5):
                copy_x(j)
            dve.wait_ge(sem("dt_exped"), 1)
            link(nc.vector.tensor_scalar(dt[:, :, :], dt_exp[:, :, :], 1.0, None, ALU.add))
            link(nc.vector.tensor_scalar(la[:, :, :], dt[:, :, :], -1.0, None, ALU.add))
            link(nc.vector.tensor_tensor(la[:, :, :], dt_exp[:, :, :], la[:, :, :], ALU.subtract))
            link(nc.vector.reciprocal(dt[:, :, :], dt[:, :, :]))
            link(nc.vector.tensor_tensor(la[:, :, :], la[:, :, :], dt[:, :, :], ALU.mult))
            dve.wait_ge(sem("dt_lned"), 1)
            link(nc.vector.tensor_tensor(dt_ln[:, :, :], dt_ln[:, :, :], la[:, :, :], ALU.add))
            dve.wait_ge(sem("a_exp"), 1)
            link(nc.vector.tensor_tensor(dt[:, :, :], dt_ln[:, :, :], dt_pre[:, :, :], ALU.max))
            nc.vector.scalar_tensor_tensor(out=la[:, :, :], in0=dt[:, :, :], scalar=-1.0,
                                           in1=a_row[:, :].unsqueeze(1).to_broadcast([P, TT, SH]),
                                           op0=ALU.mult, op1=ALU.mult).then_inc(sem("la_ready"), 1)
            for j in range(5, 8):
                copy_x(j)
            dve.wait_ge(sem("cum_mm"), 1)
            r3 = lambda ap: ap.rearrange("p (t h) -> p t h", t=TT)
            link(nc.vector.tensor_copy(cum[:, :, :], r3(bank[7][:, 0:TT * SH])))
            nc.vector.tensor_copy(c_dec[:, :, :], r3(bank[7][:, TT * SH:2 * TT * SH]))
            nc.vector.tensor_tensor(to_end[:, :, :], r3(bank[7][:, TT * SH:2 * TT * SH]), cum[:, :, :],
                                    ALU.subtract).then_inc(sem("cum_read"), 1)
            dve.wait_ge(sem("decay_exp"), 3)

            def heads(ap):
                return ap.unsqueeze(2).to_broadcast([P, GH, SHD])

            def cell(buf, t, g):
                return buf[:, t, g * 256:(g + 1) * 256].rearrange("p (r c) -> p r c", r=GH)

            def ssd_front(n):
                t, g, b = n // SG, n % SG, n % 2
                hs = slice(g * GH, (g + 1) * GH)
                dve.wait_ge(sem("cell_a"), n + 1)
                wait(dve, sem("cell_y"), n - 1)
                nc.vector.tensor_tensor(cb_m[:, b, :], bank[1][:, 0:P], tri_le, ALU.mult)\
                  .then_inc(sem("cell_a_read"), 1)
                nc.vector.tensor_copy(b_tok[:, b, :], bank[1][:, P:2 * P]).then_inc(sem("cell_a_read"), 1)
                link(nc.vector.tensor_tensor(xdt[:, b, :, :], cell(xs_tok, t, g), heads(dt[:, t, hs]), ALU.mult))
                nc.vector.tensor_tensor(xdte[:, b, :, :], xdt[:, b, :, :], heads(e_end[:, t, hs]), ALU.mult)
                dve.wait_ge(sem("decayed"), n + 1)
                nc.vector.tensor_tensor(mix_m[:, b, :, :], decay[:, b, :, :],
                                        cb_m[:, b, :].unsqueeze(1).to_broadcast([P, GH, P]),
                                        ALU.mult).then_inc(sem("cell_m"), 1)

            def ssd_back(n):
                t, g, b = n // SG, n % SG, n % 2
                hs = slice(g * GH, (g + 1) * GH)
                r4 = lambda ap: ap.rearrange("p (r c) -> p r c", r=GH)
                wait(dve, sem("cell_done"), n)
                skip = rows[:, ROWS["d_skip"] + g * GH:ROWS["d_skip"] + (g + 1) * GH]
                nc.vector.tensor_tensor(y_a[:, :, :], cell(xs_tok, t, g), heads(skip), ALU.mult)\
                  .then_inc(sem("y_step"), 1)
                dve.wait_ge(sem("cell_y"), n + 1)
                dve.wait_ge(sem("y_step"), 4 * n + 1)
                nc.vector.tensor_tensor(y_b[:, :, :], r4(bank[4 + b][:, 0:256]), y_a[:, :, :], ALU.add)\
                  .then_inc(sem("y_step"), 1)
                if t > 0:
                    nc.vector.tensor_tensor(y_c[:, :, :], r4(bank[4 + b][:, 256:512]), heads(ecum[:, t, hs]),
                                            ALU.mult).then_inc(sem("y_step"), 1)
                    dve.wait_ge(sem("y_step"), 4 * n + 3)
                    nc.vector.tensor_tensor(y_b[:, :, :], y_b[:, :, :], y_c[:, :, :], ALU.add)\
                      .then_inc(sem("y_step"), 1)
                    link(nc.vector.tensor_tensor(state[:, g, :, :], state[:, g, :, :], heads(c_dec[:, t, hs]),
                                                 ALU.mult))
                    nc.vector.tensor_tensor(state[:, g, :, :], r4(bank[6 + b][:, 0:256]), state[:, g, :, :],
                                            ALU.add)
                else:
                    nc.vector.tensor_copy(state[:, g, :, :], r4(bank[6 + b][:, 0:256])).then_inc(sem("y_step"), 2)
                dve.wait_ge(sem("y_step"), 4 * n + 4)
                z = cell(z_tok, t, g)
                nc.vector.tensor_tensor(z, z, y_b[:, :, :], ALU.mult).then_inc(sem("cell_done"), 1)

            dve.wait_ge(sem("xs_copied"), 8)
            for n in range(TT * SG + 1):
                if n < TT * SG:
                    ssd_front(n)
                if n % 2 == 1:
                    c = n // 2
                    dve.wait_ge(unit_done, UNIT0["q"] + c + 1)
                    nc.vector.scalar_tensor_tensor(out=q_T[:, c, :], in0=bank[0][:, :], scalar=-0.125,
                                                   in1=rstd_row[:, :], op0=ALU.mult, op1=ALU.mult)\
                      .then_inc(tile_free, 1)
                if n > 0:
                    ssd_back(n - 1)
            dve.wait_ge(sem("y_rooted"), 1)
            link(nc.vector.reciprocal(y_rstd[:, :], y_root[:, :]))
            for n in range(TT * SG):
                t, g = n // SG, n % SG
                z = z_tok[:, t, g * 256:(g + 1) * 256]
                nc.vector.tensor_scalar(z, z, y_rstd[:, n:n + 1], None, ALU.mult).then_inc(sem("y_norm"), 1)
            scaled_tiles("k", k_T, 8)
            for j in range(DC):
                dve.wait_ge(sem("ys_hi"), j + 1)
                nc.vector.scalar_tensor_tensor(out=ys_lo[:, j, :], in0=bank[6 + j % 2][:, :],
                                               scalar=col("ssd_norm_w", j), in1=ys_hi[:, j, :].bitcast(F32),
                                               op0=ALU.mult, op1=ALU.subtract).then_inc(sem("ys_lo"), 1)
            dve.wait_ge(unit_done, UNIT0["mix_ssd"])
            r = lambda n: rows[:, ROWS[n]:ROWS[n] + SHD]
            for n, (a, b) in enumerate((("lambda_q1", "lambda_k1"), ("lambda_q2", "lambda_k2"))):
                nc.vector.tensor_tensor_reduce(lam_tmp[:, :], r(a), r(b), 1.0, 0.0, ALU.mult, ALU.add,
                                               lam[:, n:n + 1]).then_inc(sem("lam_dots"), 1)
                dve.wait_ge(sem("lam_dots"), n + 1)
            link(nc.vector.tensor_scalar(subln[:, :], col("subln_w", 0), 1.0 - LAMBDA_INIT, None, ALU.mult))
            dve.wait_ge(sem("lam_exp"), 1)
            link(nc.vector.tensor_tensor(lam[:, 4:5], lam[:, 3:4], lam[:, 2:3], ALU.subtract))
            link(nc.vector.tensor_scalar(lam[:, 5:6], lam[:, 4:5], -LAMBDA_INIT, None, ALU.add))

            def combine(h):
                b = h % 2
                dve.wait_ge(sem("exped"), 8 * (h + 1))
                link(nc.vector.reciprocal(rrec[:, b, :], rsum[:, b, :]))
                link(nc.vector.tensor_scalar(rrec[:, b, 4:8], rrec[:, b, 4:8], lam[:, 5:6], None, ALU.mult))
                for i in range(TT):
                    a, e = P * (i * (i + 1) // 2), P * ((i + 1) * (i + 2) // 2)
                    p0, p1 = prob[:, b, 0, a:e], prob[:, b, 1, a:e]
                    ins = nc.vector.tensor_scalar(p0, p0, rrec[:, b, i:i + 1], None, ALU.mult)
                link(ins)
                for i in range(TT):
                    a, e = P * (i * (i + 1) // 2), P * ((i + 1) * (i + 2) // 2)
                    p0, p1 = prob[:, b, 0, a:e], prob[:, b, 1, a:e]
                    ins = nc.vector.scalar_tensor_tensor(out=p0, in0=p1, scalar=rrec[:, b, 4 + i:5 + i], in1=p0,
                                                         op0=ALU.mult, op1=ALU.add)
                ins.then_inc(sem("diffed"), 1)

            def biased(h, n):
                i, c = n // 2, n % 2
                w = (i + 1) * P
                dve.wait_ge(sem("score"), 8 * h + n + 1)
                nc.vector.tensor_tensor_reduce(
                    prob[:, h % 2, c, P * (i * (i + 1) // 2):P * ((i + 1) * (i + 2) // 2)],
                    bank[2 + (8 * h + n) % 3][:, 0:w], bias_h[:, h % 2, S - w:S], 1.0, -NEG, ALU.add, ALU.min,
                    amin[:, h % 2, c * 4 + i:c * 4 + i + 1]).then_inc(sem("score_read"), 1)

            for h in range(AH + 1):
                if h < AH:
                    dve.wait_ge(sem("bias_ready"), h + 1)
                    if h >= 2:
                        dve.wait_ge(sem("turned"), h - 1)
                    for n in range(3):
                        biased(h, n)
                if h > 0:
                    combine(h - 1)
                if h < AH:
                    for n in range(3, 8):
                        biased(h, n)
                if h > 0:
                    dve.wait_ge(sem("turned"), h)
                    wait(dve, sem("o_mm"), h - 1)
                    nc.vector.tensor_copy(w_T[:, S:S + 384], bank[6][:, 0:384]).then_inc(sem("wT_dve"), 1)
                    nc.vector.tensor_copy(w_T[:, S + 384:NB], bank[7][:, 0:384]).then_inc(sem("wT_dve"), 1)
                    dve.wait_ge(sem("o_mm"), h)
                    nc.vector.tensor_copy(o_un[:, h - 1, :], bank[0][:, :]).then_inc(sem("o_copied"), 1)
                if h != AH - 1:
                    m = min(h, AH - 1)
                    dve.wait_ge(unit_done, UNIT0["mix_ssd"] + m + 1)
                    nc.vector.tensor_tensor(x[:, m, :], bank[1][:, :], x[:, m, :], ALU.add).then_inc(tile_free, 1)
            dve.wait_ge(sem("o_rooted"), 1)
            nc.vector.reciprocal(o_rstd[:, :], o_root[:, :]).then_inc(sem("o_col"), 1)
            for h in range(AH + 1):
                if h < AH:
                    dve.wait_ge(sem("o_row"), h + 1)
                    wait(dve, sem("o_lo"), h - 1)
                    nc.vector.scalar_tensor_tensor(out=o_nrm[:, h % 2, :], in0=o_un[:, h, :], scalar=subln[:, :],
                                                   in1=bank[4 + h % 4][:, :], op0=ALU.mult, op1=ALU.mult)\
                      .then_inc(sem("o_nrmd"), 1)
                if h > 0:
                    dve.wait_ge(sem("o_hi"), h)
                    nc.vector.tensor_tensor(o_lo[:, h - 1, :], o_nrm[:, (h - 1) % 2, :],
                                            o_hi[:, h - 1, :].bitcast(F32), ALU.subtract).then_inc(sem("o_lo"), 1)
            nc.vector.memset(m_sum[:, :], 0.0).then_inc(sem("m_sum"), 1)

            def memory_tile(m):
                dve.wait_ge(sem("m_square"), m + 1)
                dve.wait_ge(sem("m_sum"), m + 1)
                nc.vector.tensor_tensor(m_sum[:, :], m_sum[:, :], m_sq[:, :], ALU.add).then_inc(sem("m_sum"), 1)
                dve.wait_ge(sem("m_hi"), m + 1)
                nc.vector.scalar_tensor_tensor(out=m_lo[:, m, :], in0=m_T[:, m, :], scalar=col("norm_mem_w", m),
                                               in1=m_hi[:, m, :].bitcast(F32), op0=ALU.mult, op1=ALU.subtract)\
                  .then_inc(sem("m_lo"), 1)
            residual_stage("mix_attn", "norm_cross_w", 1, 1.0, body=8, peel=1, beside=memory_tile,
                           banks=4)
            dve.wait_ge(sem("m_root"), 1)
            nc.vector.reciprocal(m_rstd[:, :], m_root[:, :]).then_inc(sem("m_col"), 1)
            dve.wait_ge(sem("m_rowed"), 1)
            link(nc.vector.tensor_copy(m_row[:, :], bank[6][:, 0:ML]))
            scaled_tiles("ck", kx_T, 8, row=m_row)
            norm("n_cross")
            scaled_tiles("cq", qx_T, 8, scale=-0.0625)
            for n in range(XH * TT + 5):
                if n > 2 and (n - 3) % TT == TT - 1 and n - 3 < XH * TT:
                    hd = (n - 3) // TT
                    dve.wait_ge(sem("x_turned"), n - 2)
                    wait(dve, sem("ox_mm"), 2 * hd)
                    for kk in range(MT):
                        nc.vector.tensor_copy(pxT[:, kk, :], bank[5 + kk][:, :]).then_inc(sem("x_pT"), 1)
                if n < XH * TT:
                    dve.wait_ge(sem("x_score"), n + 1)
                    nc.vector.tensor_reduce(xmin[:, n:n + 1], bank[2 + n % 3][:, 0:ML], AX_X, ALU.min)\
                      .then_inc(sem("x_min"), 1)
                if 0 < n <= XH * TT:
                    k = n - 1
                    dve.wait_ge(sem("x_exp"), k + 1)
                    link(nc.vector.reciprocal(xrec[:, k:k + 1], xsum[:, k:k + 1]))
                    nc.vector.tensor_scalar(px[:, k % 4, :], px[:, k % 4, :], xrec[:, k:k + 1], None, ALU.mult)\
                      .then_inc(sem("x_prob"), 1)
                if n > 4 and (n - 5) % TT == TT - 1:
                    x_lo((n - 5) // TT)
            residual_stage("co", "norm_ffn2_w", 1, 1.0)
            ffn("ffn2", "n_ffn2", None)
            dve.wait_ge(norm_sem("root"), norm_count("root", "n_fin", 1))
            link(nc.vector.tensor_scalar(fin[:, 8:12], root_col[:, 0:4], EPS, None, ALU.add))
            link(nc.vector.reciprocal(fin[:, 12:16], fin[:, 8:12]))
            nc.vector.tensor_tensor(fin[:, 0:4], fin[:, 12:16], root_col[:, 4:8], ALU.mult)\
              .then_inc(sem("n_fin_var"), 1)
            dve.wait_ge(norm_sem("root"), norm_count("root", "n_fin", 3))
            link(nc.vector.reciprocal(fin[:, 24:32], fin[:, 16:24]))
            nc.vector.tensor_copy(root_col[:, 4:8], fin[:, 28:32])
            nc.vector.tensor_tensor(rstd_col[:, :], fin[:, 24:28], fin[:, 28:32], ALU.mult)\
              .then_inc(norm_sem("col"), 1)
            dve.wait_ge(norm_sem("row"), norm_count("row", "n_fin", 1))
            nc.vector.tensor_copy(rstd_row[:, :], bank[7][:, :]).then_inc(norm_sem("ready"), 1)
            dve.wait_ge(norm_sem("row"), norm_count("row", "n_fin", 2))
            link(nc.vector.tensor_copy(rfin_row[:, :], bank[7][:, :]))
            for c in range(4):
                dve.wait_ge(unit_done, UNIT0["qk2"] + c + 1)
                nc.vector.scalar_tensor_tensor(out=q2_T[:, c, :], in0=bank[c % 2][:, :], scalar=0.125,
                                               in1=rstd_row[:, :], op0=ALU.mult, op1=ALU.mult)\
                  .then_inc(tile_free, 1)
            for c in range(4):
                dve.wait_ge(unit_done, UNIT0["qk2"] + 4 + c + 1)
                nc.vector.tensor_tensor(k2_T[:, c, :], bank[c % 2][:, :], rstd_row[:, :], ALU.mult)\
                  .then_inc(tile_free, 1)
            nc.vector.memset(cprod[:, 0:2], 0.0).then_inc(sem("cprod_pad"), 1)
            for m in range(DC):
                nc.vector.tensor_tensor(x[:, m, :], x[:, m, :], rfin_row[:, :], ALU.mult).then_inc(sem("x1"), 1)
            for c in range(4):
                U = UNIT0["conv2"] + 3 * c
                dve.wait_ge(unit_done, U + 1)
                nc.vector.tensor_tensor(cc_t[:, :], bank[(3 * c) % 2][:, :], rstd_row[:, :], ALU.mult)\
                  .then_inc(tile_free, 1)
                dve.wait_ge(unit_done, U + 2)
                nc.vector.tensor_tensor(cu_t[:, :], bank[(3 * c + 1) % 2][:, :], rstd_row[:, :], ALU.mult)\
                  .then_inc(tile_free, 1)
                dve.wait_ge(tile_free, TILE0["conv2"] + 3 * c + 2)
                wait(dve, sem("cv_lo"), c)
                link(nc.vector.tensor_tensor(cprod[:, 2:2 + S], cc_t[:, :], cu_t[:, :], ALU.mult))
                link(nc.vector.tensor_scalar(cacc[:, :], cprod[:, 0:S], col("w_conv_2", c), None, ALU.mult))
                for k in (1, 2):
                    link(nc.vector.scalar_tensor_tensor(out=cacc[:, :], in0=cprod[:, k:k + S],
                                                        scalar=col("w_conv_2", 4 * k + c), in1=cacc[:, :],
                                                        op0=ALU.mult, op1=ALU.add))
                dve.wait_ge(unit_done, U + 3)
                nc.vector.tensor_tensor(cc_t[:, :], bank[(3 * c + 2) % 2][:, :], rstd_row[:, :], ALU.mult)\
                  .then_inc(tile_free, 1)
                dve.wait_ge(tile_free, TILE0["conv2"] + 3 * c + 3)
                nc.vector.tensor_tensor(cacc[:, :], cacc[:, :], cc_t[:, :], ALU.mult).then_inc(sem("cv_out"), 1)
                dve.wait_ge(sem("cv_hi"), c + 1)
                nc.vector.tensor_tensor(cv_lo[:, c, :], cacc[:, :], cv_hi[:, c, :].bitcast(F32), ALU.subtract)\
                  .then_inc(sem("cv_lo"), 1)

            def gate_block(i):
                for j in range(4):
                    c = i * 4 + j
                    dve.wait_ge(unit_done, UNIT0["gates2"] + c + 1)
                    wait(dve, sem("gate_sig"), c)
                    nc.vector.tensor_tensor(gate_t[:, :], bank[j % 2][:, :], rstd_row[:, :], ALU.mult)\
                      .then_inc(tile_free, 1)
            blocks(dve, 4, gate_block, peel=1)
            dve.wait_ge(sem("gate_sig"), 16)

            diag = {j: S * bk + o for j, (bk, o) in {0: (0, 0), 1: (1, 0), 3: (1, 3 * P), 2: (2, 0)}.items()}
            for h in range(KH + 2):
                if h < KH:
                    b = h % 2
                    wait(dve, sem("sp_masked"), h - 1)
                    for bk, z in enumerate(by_bank(sz_buf[b])):
                        dve.wait_ge(sem("z_mm"), 3 * h + bk + 1)
                        nc.vector.tensor_scalar(z, bank[2 + bk][:, 0:z.shape[1]], 40.0, None, ALU.min)\
                          .then_inc(sem("z_clamped"), 1)
                    wait(dve, sem("c_mm"), h - 1)
                    for bk, (z, sp_) in enumerate(zip(by_bank(sz_buf[b]), by_bank(sp_buf[b]))):
                        dve.wait_ge(sem("sp_lned"), 3 * h + bk + 1)
                        nc.vector.tensor_tensor(sp_, bank[2 + bk][:, 0:z.shape[1]], z, ALU.max)\
                          .then_inc(sem("sp_ready"), 1)
                    dve.wait_ge(sem("sp_ready"), 3 * (h + 1))
                    for j in range(TT):
                        v = sp_buf[b][:, diag[j]:diag[j] + P]
                        ins = nc.vector.tensor_tensor(v, v, tri_lt, ALU.mult)
                    ins.then_inc(sem("sp_masked"), 1)
                if 0 < h <= KH:
                    k = h - 1
                    dve.wait_ge(sem("w_exp"), k + 1)
                    for j in range(TT):
                        w = w_buf[k % 2][:, diag[j]:diag[j] + P]
                        ins = nc.vector.scalar_tensor_tensor(out=w, in0=w, scalar=-NEG, in1=tri_lt, op0=ALU.min,
                                                             op1=ALU.mult)
                    ins.then_inc(sem("w_masked"), 1)
                if h > 1 and h % 2 == 1:
                    c = (h - 2) // 2
                    dve.wait_ge(sem("o2_hi"), c + 1)
                    nc.vector.tensor_tensor(o2_lo[:, c, :], bank[c % 2][:, :], o2_hi[:, c, :].bitcast(F32),
                                            ALU.subtract).then_inc(sem("o2_lo"), 1)
            with dve.Fori(0, 2) as i:
                for j in range(4):
                    c = i * 4 + j
                    dve.wait_ge(unit_done, UNIT0["branch2"] + c + 1)
                    nc.vector.tensor_tensor(br_a[:, :], bank[2 * (j % 2)][:, :], tile_of(gates, c), ALU.mult)\
                      .then_inc(tile_free, 1)
                    nc.vector.tensor_tensor(br_b[:, :], bank[2 * (j % 2) + 1][:, :], tile_of(gates, c + 8), ALU.mult)\
                      .then_inc(tile_free, 1)
                    dve.wait_ge(tile_free, TILE0["branch2"] + 2 * c + 2)
                    nc.vector.tensor_tensor(br_m[:, :], br_a[:, :], br_b[:, :], ALU.add).then_inc(sem("mixed"), 1)
                    dve.wait_ge(sem("gx_hi_done"), gx_count("branch2", c + 1))
                    nc.vector.tensor_tensor(tile_of(gx_lo, c), br_m[:, :], tile_of(gx_hi, c).bitcast(F32),
                                            ALU.subtract).then_inc(sem("gx_lo_done"), 1)
            start_sums()

            def o2_block(i):
                for j in range(4):
                    m = i * 4 + j
                    dve.wait_ge(unit_done, UNIT0["o2"] + m + 1)
                    nc.vector.tensor_copy(tile_of(y_o2, m), bank[j % 2][:, :]).then_inc(tile_free, 1)
                    add_square("o2", m)
            blocks(dve, 2, o2_block)
            def post(name, weight, next_weight, src):
                for m in range(DC):
                    wait(dve, sem(f"{name}_x"), m)
                    link(nc.vector.scalar_tensor_tensor(out=pn_t[:, :], in0=src[:, m, :], scalar=col(weight, m),
                                                        in1=rstd_row[:, :], op0=ALU.mult, op1=ALU.mult))
                    nc.vector.tensor_tensor(x[:, m, :], x[:, m, :], pn_t[:, :], ALU.add)\
                      .then_inc(sem(f"{name}_x"), 1)
                    if m > 0:
                        split_lo(name, next_weight, m - 1, x)
                    if m == 1:
                        start_sums()
                split_lo(name, next_weight, DC - 1, x)
            norm("n_post")
            post("post", "g_post_mix_2", "g_pre_mlp_2", y_o2)

            def up_stage(stage, half):
                def block_of(i):
                    for j in range(4):
                        c = i * 4 + j
                        if first(i) and j == 0 and half == 0:
                            norm("n_mlp")
                        dve.wait_ge(unit_done, UNIT0[stage] + c + 1)
                        nc.vector.tensor_tensor(up_t[:, :], bank[j][:, :], rstd_row[:, :], ALU.mult)\
                          .then_inc(tile_free, 1)
                        dve.wait_ge(tile_free, TILE0[stage] + c + 1)
                        nc.vector.scalar_tensor_tensor(out=up_a[:, :], in0=up_t[:, :], scalar=0.0, in1=up_t[:, :],
                                                       op0=ALU.max, op1=ALU.mult).then_inc(sem("up_act"), 1)
                        dve.wait_ge(sem("up_hi"), half * HC + c + 1)
                        nc.vector.tensor_tensor(tile_of(up_lo, c), up_a[:, :],
                                                tile_of(up_hi, c).bitcast(F32), ALU.subtract)\
                          .then_inc(sem("up_lo"), 1)
                blocks(dve, 4, block_of, peel=1 - half)
            up_stage("up_a", 0)

            def down_block(i):
                for j in range(4):
                    m = i * 4 + j
                    dve.wait_ge(unit_done, UNIT0["down_a"] + m * 2 + 2)
                    nc.vector.tensor_copy(tile_of(f_acc, m), bank[j % 2][:, :]).then_inc(tile_free, 1)
            blocks(dve, 2, down_block)
            up_stage("up_b", 1)
            start_sums()

            for k in range(2):
                dve.wait_ge(sem("p_hi"), k + 1)
                nc.vector.tensor_tensor(p_lo[:, k, :], p_T[:, k, :], p_hi[:, k, :].bitcast(F32), ALU.subtract)\
                  .then_inc(sem("p_lo"), 1)

            def down_block_b(i):
                for j in range(4):
                    m = i * 4 + j
                    fm = tile_of(f_acc, m)
                    dve.wait_ge(unit_done, UNIT0["down_b"] + m * 2 + 2)
                    nc.vector.tensor_tensor(fm, bank[j % 2][:, :], fm, ALU.add).then_inc(tile_free, 1)
                    add_square("down", m)
            blocks(dve, 2, down_block_b)

            def copy_projection(m):
                dve.wait_ge(unit_done, UNIT0["proj2"] + m // 2 + 1)
                nc.vector.tensor_copy(proj[:, m, :], bank[m % 4][:, :]).then_inc(tile_free, 1)
            for m in range(4):
                copy_projection(m)
            norm_column("n_pmlp")
            for m in range(4, DC):
                copy_projection(m)
            norm_row("n_pmlp")
            post("pmlp", "g_post_mlp_2", "g_ple_2", f_acc)
            norm("n_ple")
            for m in range(DC):
                dve.wait_ge(unit_done, UNIT0["ple2"] + m + 1)
                nc.vector.tensor_tensor(ple_t[:, :], bank[m % 4][:, :], rstd_row[:, :], ALU.mult)\
                  .then_inc(tile_free, 1)
                dve.wait_ge(sem("ple_sig"), m + 1)
                link(nc.vector.tensor_tensor(ple_o[:, m, :], ple_g[:, :], proj[:, m, :], ALU.mult))
                nc.vector.tensor_tensor(ple_o[:, m, :], ple_o[:, m, :], x[:, m, :], ALU.add)\
                  .then_inc(sem("out_ready"), 1)


def _cols(v, n):
    return np.ascontiguousarray(np.asarray(v).reshape(n, P).T)


def _units(w):
    K, N = w.shape
    per = -(-K // UNIT)
    if K < per * UNIT:
        w = np.concatenate([w, np.zeros((per * UNIT - K, N), w.dtype)])
    return w.reshape(per, UC, P, N // P, P).transpose(3, 0, 2, 1, 4).reshape(-1, P, UNIT)


def _token_units(w):
    K, N = w.shape
    return w.reshape(K // (2 * P), 2, P, N // S, S).transpose(3, 0, 2, 1, 4).reshape(-1, P, UNIT)


def _interleave(*parts):
    return np.stack(parts, axis=1).reshape(-1, P, UNIT)


def _shape_constants():
    i = np.arange(P)
    f = np.float32
    m = [np.eye(P, dtype=f), (i[:, None] <= i[None, :]).astype(f), np.ones((P, P), f), np.eye(P, dtype=f)[::-1],
         -(i[:, None] >= i[None, :]).astype(f), -np.ones((P, P), f), (i[:, None] < i[None, :]).astype(f)]
    n = (S - 1) - np.arange(BIAS_W + 1)
    big = 16 + (np.log(np.maximum(n, 1).astype(f) / f(16)) / f(np.log(8.0)) * f(16)).astype(np.int32)
    b = np.where(n < 16, np.maximum(n, 0), np.minimum(big, 31))
    onehot = (np.arange(32)[:, None] == b[None, :]).astype(f)
    pen = np.where(n < 0, f(MASK), f(0)).astype(f)[None, :].repeat(AH, 0)
    return np.concatenate(m, axis=1), onehot, np.ascontiguousarray(pen)


def kernel(**inputs):
    import concourse.bacc as bacc
    from concourse.bass_utils import run_bass_kernel_spmd

    v = {k: np.asarray(a) for k, a in inputs.items()}
    w_mix, w2 = v["w_in_mix"][0], v["w_in_2"][0]
    z0, xb0 = 0, D
    dt0 = xb0 + 2048
    q0 = dt0 + 16
    gate, up = _units(v["ffn1_w_in"][0][:, :FF]), _units(v["ffn1_w_in"][0][:, FF:])
    gate2, up2 = _units(v["ffn2_w_in"][0][:, :FF]), _units(v["ffn2_w_in"][0][:, FF:])
    wo = v["w_out_mix"][0]
    branch = np.concatenate([v["w_attn_out_2"][0], v["w_conv_out_2"][0]])
    down = v["w_down_2"][0]
    proj = v["w_ple_proj_2"][0].reshape(2, P, 4, 2, P).transpose(2, 1, 3, 0, 4).reshape(4, P, UNIT // 2)
    proj = np.concatenate([proj, np.zeros_like(proj)], axis=2)
    upw = _units(v["w_up_2"][0])
    stream = np.concatenate([
        _interleave(gate, up), _units(v["ffn1_w_out"][0]),
        _units(w_mix[:, xb0:dt0]), _token_units(w_mix[:, z0:xb0]),
        _units(w_mix[:, q0:q0 + D]), _units(w_mix[:, q0 + D:q0 + 2 * D]), _token_units(w_mix[:, q0 + 2 * D:]),
        _units(wo[:D]), _units(wo[D:]),
        _units(v["w_ck"][0]), _token_units(v["w_cv"][0]), _units(v["w_cq"][0]), _units(v["w_co"][0]),
        _interleave(gate2, up2), _units(v["ffn2_w_out"][0]),
        _units(w2[:, :2 * S]), _token_units(w2[:, 2 * S:3 * S]),
        _interleave(_units(w2[:, 4 * S:5 * S]), _units(w2[:, 5 * S:6 * S]), _units(w2[:, 3 * S:4 * S])),
        _units(w2[:, 6 * S:]),
        _units(branch), _units(v["w_o_2"][0]),
        upw[:HC], _units(down[:FF2 // 2]), upw[HC:], _units(down[FF2 // 2:]),
        proj, _units(v["w_ple_gate_2"][0]),
    ])
    assert stream.shape[0] == UNITS
    cols = np.concatenate([
        _cols(v["norm_ffn1_w"], 8), _cols(v["norm_mix_w"], 8),
        _cols(v["conv_w"][0], 64), _cols(v["conv_b"], 16), _cols(v["ssd_norm_w"], 8), _cols(v["subln_w"], 1),
        _cols(v["norm_cross_w"], 8), _cols(v["norm_mem_w"], 8), _cols(v["norm_ffn2_w"], 8),
        _cols(v["norm_final_w"], 8), _cols(v["g_pre_mix_2"], 8), _cols(v["b_gate_2"], 16),
        _cols(v["w_conv_2"][0], 12), _cols(v["g_post_mix_2"], 8), _cols(v["g_pre_mlp_2"], 8),
        _cols(v["g_post_mlp_2"], 8), _cols(v["g_ple_2"], 8)], axis=1)
    rows = np.concatenate([v[n].reshape(1, -1) for n in ROWS], axis=1)
    consts, onehot, pen = _shape_constants()
    arrays = {
        "wstream": stream, "xT": v["x"][0].T, "memT": v["mem"][0].T, "pT": v["p_2"][0, 0].T,
        "cols": cols, "rows": rows,
        "wdt": w_mix[:, dt0:q0].reshape(8, P, 16).transpose(1, 0, 2), "relb": v["rel_bias"],
        "consts": consts, "onehot": onehot, "pen": pen,
    }
    nc = bacc.Bacc("TRN2", target_bir_lowering=False, num_devices=1)
    args = []
    for name in list(arrays):
        arrays[name] = np.ascontiguousarray(arrays[name])
        args.append(nc.dram_tensor(name, arrays[name].shape, F32, kind="ExternalInput").ap())
    args.append(nc.dram_tensor("outT", (D, S), F32, kind="ExternalOutput").ap())
    build(nc, *args)
    got = run_bass_kernel_spmd(nc, [arrays], core_ids=[0]).results[0]["outT"]
    return np.ascontiguousarray(got.T)[None]
```
